# Optimizing a Trainium2 kernel written in Bass

```python
import math
import jax
import jax.numpy as jnp
from jax import lax
import numpy as np
import jax, jax.numpy as jnp

D_MODEL = 1024
BATCH = 1
SEQ = 512
DEPTH = 2

A_HEADS = 4
A_DK = 64
A_DV = 64
B_HEADS = 8
B_GROUPS = 2
B_HPG = B_HEADS // B_GROUPS
B_DH = 64
C_HEADS = 4
C_DH = 64
MIX_WIDTH = A_HEADS * A_DV + B_HEADS * B_DH + C_HEADS * C_DH
D_FF = 4 * D_MODEL
ROPE_THETA = 500000.0
ROT_DIM = B_DH // 4
EPS = 1e-6
NEG_BIG = -1e30
POS_BIG = 1e30
TINY = 1e-30
HGRN_CHUNK = 64
CMP_BLOCK = 32
CMP_STRIDE = 16
CMP_HIDDEN = 128
SEL_BLOCK = 64
SEL_TOPK = 16
WINDOW = 512
NSA_QBLOCK = 64
FOX_QBLOCK = 128

IN_SPLIT = (
    A_HEADS * A_DK, A_HEADS * A_DK, A_HEADS * A_DV, A_HEADS * A_DV,
    B_HEADS * B_DH,
    B_GROUPS * B_DH, B_GROUPS * B_DH,
    B_GROUPS * B_DH, B_GROUPS * B_DH,
    B_GROUPS * B_DH, B_GROUPS * B_DH,
    3 * B_HEADS,
    C_HEADS * C_DH, C_HEADS * C_DH, C_HEADS * C_DH, C_HEADS,
)
IN_WIDTH = sum(IN_SPLIT)


def _rmsnorm(x, g):
    xf = x.astype(jnp.float32)
    var = jnp.mean(xf * xf, axis=-1, keepdims=True)
    return xf * lax.rsqrt(var + EPS) * g.astype(jnp.float32)

def _rope_partial(x, pos):
    half = ROT_DIM // 2
    inv_freq = jnp.power(jnp.float32(ROPE_THETA), -jnp.arange(0, ROT_DIM, 2, dtype=jnp.float32) / ROT_DIM)
    ang = pos.astype(jnp.float32)[:, None] * inv_freq[None, :]
    ang = ang.reshape((1, pos.shape[0]) + (1,) * (x.ndim - 3) + (half,))
    cos, sin = jnp.cos(ang), jnp.sin(ang)
    x1 = x[..., :half]
    x2 = x[..., half:ROT_DIM]
    return jnp.concatenate([x1 * cos - x2 * sin, x2 * cos + x1 * sin, x[..., ROT_DIM:]], axis=-1)

def _masked_softmax(logits, mask):
    logits = jnp.where(mask, logits.astype(jnp.float32), NEG_BIG)
    m = jnp.max(logits, axis=-1, keepdims=True)
    p = jnp.where(mask, jnp.exp(logits - m), 0.0)
    return p / jnp.maximum(jnp.sum(p, axis=-1, keepdims=True), TINY)

def _hgrn2(q, f_logit, i_val, g_out, lb, onorm_g):
    bsz, seq = q.shape[0], q.shape[1]
    lb = lb.reshape(A_HEADS, A_DK)
    z = f_logit.astype(jnp.float32).reshape(bsz, seq, A_HEADS, A_DK)
    f = lb + (1.0 - lb) * jax.nn.sigmoid(z)
    log_f = jnp.log(jnp.maximum(f, TINY))
    k = (1.0 - lb) * jax.nn.sigmoid(-z)
    qf = q.astype(jnp.float32).reshape(bsz, seq, A_HEADS, A_DK) * (A_DK ** -0.5)
    v = i_val.astype(jnp.float32).reshape(bsz, seq, A_HEADS, A_DV)
    n_chunks = seq // HGRN_CHUNK

    def to_chunks(t):
        return t.reshape(bsz, n_chunks, HGRN_CHUNK, A_HEADS, -1).transpose(1, 0, 3, 2, 4)

    causal = jnp.tril(jnp.ones((HGRN_CHUNK, HGRN_CHUNK), dtype=bool))

    def step(state, inp):
        qc, kc, vc, gc = inp
        G = jnp.cumsum(gc, axis=2)
        o_inter = jnp.einsum('bhtk,bhkv->bhtv', qc * jnp.exp(G), state)
        diff = G[:, :, :, None, :] - G[:, :, None, :, :]
        decay = jnp.exp(jnp.where(causal[:, :, None], diff, NEG_BIG))
        scores = jnp.einsum('bhtk,bhsk,bhtsk->bhts', qc, kc, decay)
        o_intra = jnp.einsum('bhts,bhsv->bhtv', scores, vc)
        g_last = G[:, :, -1:, :]
        k_dec = kc * jnp.exp(g_last - G)
        state = state * jnp.exp(g_last[:, :, 0, :])[..., None] + jnp.einsum('bhsk,bhsv->bhkv', k_dec, vc)
        return state, o_inter + o_intra

    state0 = jnp.zeros((bsz, A_HEADS, A_DK, A_DV), jnp.float32)
    _, o = lax.scan(step, state0, (to_chunks(qf), to_chunks(k), to_chunks(v), to_chunks(log_f)))
    o = o.transpose(1, 0, 3, 2, 4).reshape(bsz, seq, A_HEADS, A_DV)
    gate = jax.nn.silu(g_out.astype(jnp.float32)).reshape(bsz, seq, A_HEADS, A_DV)
    o = _rmsnorm(o, onorm_g) * gate
    return o.reshape(bsz, seq, A_HEADS * A_DV)

def _nsa(q, k_cmp, v_cmp, k_slc, v_slc, k_win, v_win, gates, qn_g, kn_g, cmp_pos, cmp_w1, cmp_w2):
    bsz, seq = q.shape[0], q.shape[1]
    pos = jnp.arange(seq)
    qh = _rope_partial(_rmsnorm(q.reshape(bsz, seq, B_GROUPS, B_HPG, B_DH), qn_g), pos) * (B_DH ** -0.5)
    ks = _rope_partial(_rmsnorm(k_slc.reshape(bsz, seq, B_GROUPS, B_DH), kn_g), pos)
    kw = _rope_partial(_rmsnorm(k_win.reshape(bsz, seq, B_GROUPS, B_DH), kn_g), pos)
    vs = v_slc.astype(jnp.float32).reshape(bsz, seq, B_GROUPS, B_DH)
    vw = v_win.astype(jnp.float32).reshape(bsz, seq, B_GROUPS, B_DH)

    n_sub = CMP_BLOCK // CMP_STRIDE
    n_cmp = seq // CMP_STRIDE - n_sub + 1

    def compress(t, which):
        sub = t.astype(jnp.float32).reshape(bsz, seq // CMP_STRIDE, CMP_STRIDE, B_GROUPS, B_DH)
        blocks = jnp.concatenate([sub[:, m:m + n_cmp] for m in range(n_sub)], axis=2)
        blocks = blocks + cmp_pos[which][None, None, :, None, :]
        flat = blocks.transpose(0, 1, 3, 2, 4).reshape(bsz, n_cmp, B_GROUPS, CMP_BLOCK * B_DH)
        hidden = jax.nn.gelu(flat @ cmp_w1[which])
        return hidden @ cmp_w2[which]

    cmp_end = jnp.arange(n_cmp) * CMP_STRIDE + CMP_BLOCK - 1
    kc = _rope_partial(_rmsnorm(compress(k_cmp.reshape(bsz, seq, B_GROUPS, B_DH), 0), kn_g), cmp_end)
    vc = compress(v_cmp.reshape(bsz, seq, B_GROUPS, B_DH), 1)

    n_sel = seq // SEL_BLOCK
    ci = np.arange(n_cmp)[:, None]
    sj = np.arange(n_sel)[None, :]
    c_start = ci * CMP_STRIDE
    overlap = jnp.asarray(((c_start <= sj * SEL_BLOCK + SEL_BLOCK - 1)
                           & (c_start + CMP_BLOCK - 1 >= sj * SEL_BLOCK)).astype(np.float32))
    topk = min(SEL_TOPK, n_sel)
    kb = ks.reshape(bsz, n_sel, SEL_BLOCK, B_GROUPS, B_DH).transpose(0, 3, 1, 2, 4)
    vb = vs.reshape(bsz, n_sel, SEL_BLOCK, B_GROUPS, B_DH).transpose(0, 3, 1, 2, 4)
    kw_pad = jnp.pad(kw, ((0, 0), (WINDOW, 0), (0, 0), (0, 0)))
    vw_pad = jnp.pad(vw, ((0, 0), (WINDOW, 0), (0, 0), (0, 0)))
    gate = jax.nn.sigmoid(gates.astype(jnp.float32)).reshape(bsz, seq, 3, B_GROUPS, B_HPG)
    b_idx = jnp.arange(bsz)[:, None, None, None]
    g_idx = jnp.arange(B_GROUPS)[None, :, None, None]
    sel_off = jnp.arange(SEL_BLOCK)
    win_off = jnp.arange(WINDOW + NSA_QBLOCK)
    blk_ids = jnp.arange(n_sel)

    def block_fn(blk):
        q0 = blk * NSA_QBLOCK
        t = q0 + jnp.arange(NSA_QBLOCK)
        qb = lax.dynamic_slice_in_dim(qh, q0, NSA_QBLOCK, axis=1)
        s_c = jnp.einsum('bqghd,bngd->bghqn', qb, kc)
        p_c = _masked_softmax(s_c, cmp_end[None, :] <= t[:, None])
        o_c = jnp.einsum('bghqn,bngd->bqghd', p_c, vc)
        imp = jnp.einsum('bghqn,nj->bgqj', p_c, overlap)
        cur = (t // SEL_BLOCK)[:, None]
        forced = (blk_ids[None, :] == 0) | (blk_ids[None, :] == cur) | (blk_ids[None, :] == cur - 1)
        imp = jnp.where(forced, POS_BIG, imp)
        imp = jnp.where(blk_ids[None, :] * SEL_BLOCK > t[:, None], NEG_BIG, imp)
        vals, idx = lax.top_k(imp, topk)
        k_sel = kb[b_idx, g_idx, idx]
        v_sel = vb[b_idx, g_idx, idx]
        s_s = jnp.einsum('bqghd,bgqkld->bghqkl', qb, k_sel).reshape(bsz, B_GROUPS, B_HPG, NSA_QBLOCK, topk * SEL_BLOCK)
        key_pos = idx[..., None] * SEL_BLOCK + sel_off
        m_s = (key_pos <= t[None, None, :, None, None]) & (vals > NEG_BIG * 0.5)[..., None]
        m_s = m_s.reshape(bsz, B_GROUPS, 1, NSA_QBLOCK, topk * SEL_BLOCK)
        p_s = _masked_softmax(s_s, m_s).reshape(bsz, B_GROUPS, B_HPG, NSA_QBLOCK, topk, SEL_BLOCK)
        o_s = jnp.einsum('bghqkl,bgqkld->bqghd', p_s, v_sel)
        kwb = lax.dynamic_slice_in_dim(kw_pad, q0, WINDOW + NSA_QBLOCK, axis=1)
        vwb = lax.dynamic_slice_in_dim(vw_pad, q0, WINDOW + NSA_QBLOCK, axis=1)
        kpos = q0 - WINDOW + win_off
        m_w = (kpos[None, :] >= 0) & (kpos[None, :] <= t[:, None]) & (kpos[None, :] > t[:, None] - WINDOW)
        s_w = jnp.einsum('bqghd,bkgd->bghqk', qb, kwb)
        p_w = _masked_softmax(s_w, m_w)
        o_w = jnp.einsum('bghqk,bkgd->bqghd', p_w, vwb)
        gb = lax.dynamic_slice_in_dim(gate, q0, NSA_QBLOCK, axis=1)
        return gb[:, :, 0, :, :, None] * o_c + gb[:, :, 1, :, :, None] * o_s + gb[:, :, 2, :, :, None] * o_w

    out = lax.map(block_fn, jnp.arange(seq // NSA_QBLOCK))
    return out.transpose(1, 0, 2, 3, 4, 5).reshape(bsz, seq, B_HEADS * B_DH)

def _fox(q, k, v, f_logit, qn_g, kn_g, fb):
    bsz, seq = q.shape[0], q.shape[1]
    qh = _rmsnorm(q.reshape(bsz, seq, C_HEADS, C_DH), qn_g) * (C_DH ** -0.5)
    kh = _rmsnorm(k.reshape(bsz, seq, C_HEADS, C_DH), kn_g)
    vh = v.astype(jnp.float32).reshape(bsz, seq, C_HEADS, C_DH)
    log_f = jax.nn.log_sigmoid(f_logit.astype(jnp.float32) + fb.astype(jnp.float32))
    c = jnp.cumsum(log_f, axis=1).transpose(0, 2, 1)
    kpos = jnp.arange(seq)

    def block_fn(blk):
        q0 = blk * FOX_QBLOCK
        t = q0 + jnp.arange(FOX_QBLOCK)
        qb = lax.dynamic_slice_in_dim(qh, q0, FOX_QBLOCK, axis=1)
        cq = lax.dynamic_slice_in_dim(c, q0, FOX_QBLOCK, axis=2)
        s = jnp.einsum('bqhd,bkhd->bhqk', qb, kh) + cq[..., None] - c[:, :, None, :]
        p = _masked_softmax(s, kpos[None, :] <= t[:, None])
        return jnp.einsum('bhqk,bkhd->bqhd', p, vh)

    out = lax.map(block_fn, jnp.arange(seq // FOX_QBLOCK))
    return out.transpose(1, 0, 2, 3, 4).reshape(bsz, seq, C_HEADS * C_DH)

def first_inputs(seed: int = 0) -> dict:
    key = jax.random.key(seed)
    ks = jax.random.split(key, 17)

    def nrm(k, shape, scale):
        return jax.random.normal(k, shape, jnp.float32) * scale

    return {
        'x': nrm(ks[0], (BATCH, SEQ, D_MODEL), 1.0),
        'norm1_g': 1.0 + nrm(ks[1], (DEPTH, D_MODEL), 0.02),
        'w_in': nrm(ks[2], (DEPTH, D_MODEL, IN_WIDTH), D_MODEL ** -0.5),
        'hgrn_lb_logits': nrm(ks[3], (DEPTH, A_HEADS * A_DK), 0.1),
        'hgrn_onorm_g': 1.0 + nrm(ks[4], (DEPTH, A_DV), 0.02),
        'nsa_qn_g': 1.0 + nrm(ks[5], (DEPTH, B_DH), 0.02),
        'nsa_kn_g': 1.0 + nrm(ks[6], (DEPTH, B_DH), 0.02),
        'nsa_cmp_pos': nrm(ks[7], (DEPTH, 2, CMP_BLOCK, B_DH), 0.02),
        'nsa_cmp_w1': nrm(ks[8], (DEPTH, 2, CMP_BLOCK * B_DH, CMP_HIDDEN), (CMP_BLOCK * B_DH) ** -0.5),
        'nsa_cmp_w2': nrm(ks[9], (DEPTH, 2, CMP_HIDDEN, B_DH), CMP_HIDDEN ** -0.5),
        'fox_qn_g': 1.0 + nrm(ks[10], (DEPTH, C_DH), 0.02),
        'fox_kn_g': 1.0 + nrm(ks[11], (DEPTH, C_DH), 0.02),
        'fox_fb': 2.0 + nrm(ks[12], (DEPTH, C_HEADS), 0.1),
        'w_o': nrm(ks[13], (DEPTH, MIX_WIDTH, D_MODEL), MIX_WIDTH ** -0.5),
        'norm2_g': 1.0 + nrm(ks[14], (DEPTH, D_MODEL), 0.02),
        'w_up': nrm(ks[15], (DEPTH, D_MODEL, D_FF), D_MODEL ** -0.5),
        'w_down': nrm(ks[16], (DEPTH, D_FF, D_MODEL), D_FF ** -0.5),
    }

def first_block(x, norm1_g, w_in, hgrn_lb_logits, hgrn_onorm_g, nsa_qn_g, nsa_kn_g, nsa_cmp_pos,
              nsa_cmp_w1, nsa_cmp_w2, fox_qn_g, fox_kn_g, fox_fb, w_o, norm2_g, w_up, w_down):
    lb_p = jax.nn.softmax(hgrn_lb_logits.astype(jnp.float32), axis=0)
    lb_all = jnp.cumsum(lb_p, axis=0) - lb_p[0:1]
    split_at = [int(v) for v in np.cumsum(IN_SPLIT)[:-1]]
    for layer in range(DEPTH):
        h = _rmsnorm(x, norm1_g[layer]).astype(x.dtype)
        proj = h @ w_in[layer]
        (aq, af, ai, ag, bq, bkc, bvc, bks, bvs, bkw, bvw, bg,
         cq, ck, cv, cf) = jnp.split(proj, split_at, axis=-1)
        o_a = _hgrn2(aq, af, ai, ag, lb_all[layer], hgrn_onorm_g[layer])
        o_b = _nsa(bq, bkc, bvc, bks, bvs, bkw, bvw, bg, nsa_qn_g[layer], nsa_kn_g[layer],
                   nsa_cmp_pos[layer], nsa_cmp_w1[layer], nsa_cmp_w2[layer])
        o_c = _fox(cq, ck, cv, cf, fox_qn_g[layer], fox_kn_g[layer], fox_fb[layer])
        mix = jnp.concatenate([o_a, o_b, o_c], axis=-1).astype(x.dtype)
        x = x + (mix @ w_o[layer]).astype(x.dtype)
        h2 = _rmsnorm(x, norm2_g[layer]).astype(x.dtype)
        x = x + (jnp.square(jax.nn.relu(h2 @ w_up[layer])) @ w_down[layer]).astype(x.dtype)
    return x


GRID_W = 64
Q_BLOCK = 128

A_HEAD_DIM = 64
A_ROT = A_HEAD_DIM // 4
A_Q = A_HEADS * 2 * A_HEAD_DIM
A_K = A_HEADS * 2 * A_HEAD_DIM
A_V = A_HEADS * 2 * A_HEAD_DIM

B_NOPE = 64
B_ROPE = 32
B_V = 64
B_Q_RANK = 256
B_KV_RANK = 128

C_HEADS_2 = 16
C_HEAD_DIM = 64
C_WIDTH = C_HEADS_2 * C_HEAD_DIM
NA_ROWS = 8
NA_COLS = 16

N_GROUPS = 4
EXPERTS_PER_GROUP = 8
N_EXPERTS = N_GROUPS * EXPERTS_PER_GROUP
TOP_K = 2
D_EXPERT = 512
MOE_BLOCK = 128

DN_ALPHA = (2 * DEPTH) ** 0.25
DN_BETA = (8 * DEPTH) ** -0.25
LN_EPS = 1e-5
RMS_EPS = 1e-6

EVEN_IN = A_Q + A_K + A_V + B_Q_RANK + B_KV_RANK + B_ROPE
EVEN_SPLITS = (A_Q, A_Q + A_K, A_Q + A_K + A_V, A_Q + A_K + A_V + B_Q_RANK,
               A_Q + A_K + A_V + B_Q_RANK + B_KV_RANK)
EVEN_OUT = A_HEADS * 2 * A_HEAD_DIM + B_HEADS * B_V
N_EVEN = (DEPTH + 1) // 2
N_ODD = DEPTH // 2


def layer_norm(x, g, b):
    xf = x.astype(jnp.float32)
    mu = jnp.mean(xf, axis=-1, keepdims=True)
    var = jnp.mean(jnp.square(xf - mu), axis=-1, keepdims=True)
    y = (xf - mu) * lax.rsqrt(var + LN_EPS) * g.astype(jnp.float32) + b.astype(jnp.float32)
    return y.astype(x.dtype)

def rms_norm(x, g):
    xf = x.astype(jnp.float32)
    y = xf * lax.rsqrt(jnp.mean(xf * xf, axis=-1, keepdims=True) + RMS_EPS) * g.astype(jnp.float32)
    return y.astype(x.dtype)

def rope_tables(seq, rot_dim):
    inv_freq = ROPE_THETA ** (-jnp.arange(0, rot_dim, 2, dtype=jnp.float32) / rot_dim)
    ang = jnp.arange(seq, dtype=jnp.float32)[:, None] * inv_freq[None, :]
    return jnp.cos(ang), jnp.sin(ang)

def apply_rope(x, cos, sin):
    half = cos.shape[-1]
    r = 2 * half
    cos = cos.astype(x.dtype)
    sin = sin.astype(x.dtype)
    x1 = x[..., :half]
    x2 = x[..., half:r]
    return jnp.concatenate([x1 * cos - x2 * sin, x2 * cos + x1 * sin, x[..., r:]], axis=-1)

def diff_attention(q, k, v, lam, subln_g, lambda_init, cos, sin):
    B, S, H, _, d = q.shape
    nb = S // Q_BLOCK
    q = apply_rope(q.transpose(0, 2, 3, 1, 4), cos, sin)
    k = apply_rope(k.transpose(0, 2, 3, 1, 4), cos, sin)
    v = v.transpose(0, 2, 1, 3)
    q_blocks = q.reshape(B, H, 2, nb, Q_BLOCK, d).transpose(3, 0, 1, 2, 4, 5)
    scale = d ** -0.5

    def block(qb):
        s = jnp.einsum('bhmqd,bhmkd->bhmqk', qb, k).astype(jnp.float32) * scale
        p = jax.nn.softmax(s, axis=-1)
        w = p[:, :, 0] - lam * p[:, :, 1]
        return jnp.einsum('bhqk,bhke->bhqe', w.astype(v.dtype), v)

    o = lax.map(block, q_blocks)
    o = rms_norm(o, subln_g) * (1.0 - lambda_init)
    return o.transpose(1, 0, 3, 2, 4).reshape(B, S, H * 2 * d)

def latent_attention(c_q, c_kv, k_r, q_norm_g, w_uq, kv_norm_g, w_ukv, cos, sin):
    B, S, _ = c_q.shape
    H = B_HEADS
    nb = S // Q_BLOCK
    q = (rms_norm(c_q, q_norm_g) @ w_uq).reshape(B, S, H, B_NOPE + B_ROPE).transpose(0, 2, 1, 3)
    q_nope = q[..., :B_NOPE]
    q_rope = apply_rope(q[..., B_NOPE:], cos, sin)
    kv = (rms_norm(c_kv, kv_norm_g) @ w_ukv).reshape(B, S, H, B_NOPE + B_V).transpose(0, 2, 1, 3)
    k_nope = kv[..., :B_NOPE]
    v = kv[..., B_NOPE:]
    k_rope = apply_rope(k_r, cos, sin)
    qn_blocks = q_nope.reshape(B, H, nb, Q_BLOCK, B_NOPE).transpose(2, 0, 1, 3, 4)
    qr_blocks = q_rope.reshape(B, H, nb, Q_BLOCK, B_ROPE).transpose(2, 0, 1, 3, 4)
    scale = (B_NOPE + B_ROPE) ** -0.5

    def block(args):
        qn, qr = args
        s = (jnp.einsum('bhqd,bhkd->bhqk', qn, k_nope)
             + jnp.einsum('bhqr,bkr->bhqk', qr, k_rope)).astype(jnp.float32) * scale
        p = jax.nn.softmax(s, axis=-1)
        return jnp.einsum('bhqk,bhke->bhqe', p.astype(v.dtype), v)

    o = lax.map(block, (qn_blocks, qr_blocks))
    return o.transpose(1, 0, 3, 2, 4).reshape(B, S, H * B_V)

def neighbourhood_attention(q, k, v, rel_bias):
    B, S, H, d = q.shape
    rows = S // GRID_W
    kh = min(NA_ROWS, rows)
    kw = NA_COLS
    to_grid = lambda t: t.reshape(B, rows, GRID_W, H, d).transpose(0, 3, 1, 2, 4)
    qg, kg, vg = to_grid(q), to_grid(k), to_grid(v)
    cols = jnp.arange(GRID_W)
    col_start = jnp.clip(cols - kw // 2, 0, GRID_W - kw)
    col_idx = col_start[:, None] + jnp.arange(kw)[None, :]
    col_off = col_idx - cols[:, None] + (NA_COLS - 1)
    scale = d ** -0.5

    def row(args):
        r, q_row = args
        r0 = jnp.clip(r - kh // 2, 0, rows - kh)
        k_band = lax.dynamic_slice_in_dim(kg, r0, kh, axis=2)
        v_band = lax.dynamic_slice_in_dim(vg, r0, kh, axis=2)
        k_win = k_band[:, :, :, col_idx]
        v_win = v_band[:, :, :, col_idx]
        row_off = r0 + jnp.arange(kh) - r + (NA_ROWS - 1)
        bias = rel_bias[:, row_off[:, None, None], col_off[None]]
        bias = bias.transpose(0, 2, 1, 3).astype(jnp.float32)
        s = jnp.einsum('bhcd,bhicjd->bhcij', q_row, k_win).astype(jnp.float32) * scale + bias[None]
        p = jax.nn.softmax(s.reshape(B, H, GRID_W, kh * kw), axis=-1).reshape(B, H, GRID_W, kh, kw)
        return jnp.einsum('bhcij,bhicje->bhce', p.astype(v_win.dtype), v_win)

    o = lax.map(row, (jnp.arange(rows), qg.transpose(2, 0, 1, 3, 4)))
    return o.transpose(1, 0, 3, 2, 4).reshape(B, S, H * d)

def even_mixer(x, w_in, lam_q1, lam_k1, lam_q2, lam_k2, subln_g, q_norm_g, w_uq,
               kv_norm_g, w_ukv, w_o, lambda_init, rope_a, rope_b):
    B, S, _ = x.shape
    h = x @ w_in
    qa, ka, va, cq, ckv, kr = jnp.split(h, EVEN_SPLITS, axis=-1)
    f32 = jnp.float32
    lam = (jnp.exp(jnp.sum(lam_q1.astype(f32) * lam_k1.astype(f32)))
           - jnp.exp(jnp.sum(lam_q2.astype(f32) * lam_k2.astype(f32))) + lambda_init)
    a_out = diff_attention(qa.reshape(B, S, A_HEADS, 2, A_HEAD_DIM),
                           ka.reshape(B, S, A_HEADS, 2, A_HEAD_DIM),
                           va.reshape(B, S, A_HEADS, 2 * A_HEAD_DIM),
                           lam, subln_g, lambda_init, rope_a[0], rope_a[1])
    b_out = latent_attention(cq, ckv, kr, q_norm_g, w_uq, kv_norm_g, w_ukv, rope_b[0], rope_b[1])
    return jnp.concatenate([a_out, b_out], axis=-1) @ w_o

def odd_mixer(x, w_qkv, rel_bias, w_o):
    B, S, _ = x.shape
    q, k, v = jnp.split(x @ w_qkv, 3, axis=-1)
    shp = (B, S, C_HEADS_2, C_HEAD_DIM)
    o = neighbourhood_attention(q.reshape(shp), k.reshape(shp), v.reshape(shp), rel_bias)
    return o @ w_o

def hier_moe(x, w_rg, b_rg, w_re, b_re, w1, w3, w2):
    B, S, D = x.shape
    N = B * S
    xt = x.reshape(N, D)
    g_prob = jax.nn.softmax((xt @ w_rg).astype(jnp.float32) + b_rg.astype(jnp.float32), axis=-1)
    grp = jnp.argmax(g_prob, axis=-1).astype(jnp.int32)
    g_w = jnp.take_along_axis(g_prob, grp[:, None], axis=-1)
    e_logits = ((xt @ w_re).astype(jnp.float32) + b_re.astype(jnp.float32)).reshape(N, N_GROUPS, EXPERTS_PER_GROUP)
    idx = jnp.broadcast_to(grp[:, None, None], (N, 1, EXPERTS_PER_GROUP))
    e_logits = jnp.take_along_axis(e_logits, idx, axis=1)[:, 0]
    top_v, top_i = lax.top_k(e_logits, TOP_K)
    gate = jax.nn.softmax(top_v, axis=-1) * g_w
    expert = grp[:, None] * EXPERTS_PER_GROUP + top_i.astype(jnp.int32)
    A = N * TOP_K
    e_flat = expert.reshape(A)
    w_flat = gate.reshape(A)
    tok = jnp.repeat(jnp.arange(N, dtype=jnp.int32), TOP_K)
    order = jnp.argsort(e_flat)
    e_s, tok_s, w_s = e_flat[order], tok[order], w_flat[order]
    counts = jnp.bincount(e_flat, length=N_EXPERTS)
    start = jnp.cumsum(counts) - counts
    padded = (counts + MOE_BLOCK - 1) // MOE_BLOCK * MOE_BLOCK
    pad_end = jnp.cumsum(padded)
    pad_start = pad_end - padded
    dest = pad_start[e_s] + jnp.arange(A) - start[e_s]
    n_blocks = -(-A // MOE_BLOCK) + N_EXPERTS
    P = n_blocks * MOE_BLOCK
    slot_tok = jnp.full((P,), N, jnp.int32).at[dest].set(tok_s)
    slot_w = jnp.zeros((P,), jnp.float32).at[dest].set(w_s)
    block_exp = jnp.minimum(jnp.searchsorted(pad_end, jnp.arange(n_blocks) * MOE_BLOCK, side='right'),
                            N_EXPERTS - 1).astype(jnp.int32)
    x_pad = jnp.concatenate([xt, jnp.zeros((1, D), xt.dtype)], axis=0)

    def block(args):
        tids, e, w = args
        xb = x_pad[tids]
        hdn = jax.nn.silu(xb @ w1[e]) * (xb @ w3[e])
        return (hdn @ w2[e]) * w[:, None].astype(xb.dtype)

    y = lax.map(block, (slot_tok.reshape(n_blocks, MOE_BLOCK), block_exp,
                        slot_w.reshape(n_blocks, MOE_BLOCK)))
    out = jax.ops.segment_sum(y.reshape(P, D), slot_tok, num_segments=N + 1)[:N]
    return out.reshape(B, S, D)

def second_inputs(seed: int = 0) -> dict:
    key = jax.random.key(seed)
    ks = iter(jax.random.split(key, 32))
    nrm = lambda shape, scale: jax.random.normal(next(ks), shape, jnp.float32) * scale
    gain = lambda shape: 1.0 + nrm(shape, 0.02)
    D = D_MODEL
    return {
        "x": nrm((BATCH, SEQ, D), 1.0),
        "even_w_in": nrm((N_EVEN, D, EVEN_IN), D ** -0.5),
        "even_lam_q1": nrm((N_EVEN, A_HEAD_DIM), 0.1),
        "even_lam_k1": nrm((N_EVEN, A_HEAD_DIM), 0.1),
        "even_lam_q2": nrm((N_EVEN, A_HEAD_DIM), 0.1),
        "even_lam_k2": nrm((N_EVEN, A_HEAD_DIM), 0.1),
        "even_subln_g": gain((N_EVEN, 2 * A_HEAD_DIM)),
        "even_q_norm_g": gain((N_EVEN, B_Q_RANK)),
        "even_w_uq": nrm((N_EVEN, B_Q_RANK, B_HEADS * (B_NOPE + B_ROPE)), B_Q_RANK ** -0.5),
        "even_kv_norm_g": gain((N_EVEN, B_KV_RANK)),
        "even_w_ukv": nrm((N_EVEN, B_KV_RANK, B_HEADS * (B_NOPE + B_V)), B_KV_RANK ** -0.5),
        "even_w_o": nrm((N_EVEN, EVEN_OUT, D), EVEN_OUT ** -0.5 * DN_BETA),
        "odd_w_qkv": nrm((N_ODD, D, 3 * C_WIDTH), D ** -0.5),
        "odd_rel_bias": nrm((N_ODD, C_HEADS_2, 2 * NA_ROWS - 1, 2 * NA_COLS - 1), 0.02),
        "odd_w_o": nrm((N_ODD, C_WIDTH, D), C_WIDTH ** -0.5 * DN_BETA),
        "ln1_g": gain((DEPTH, D)),
        "ln1_b": nrm((DEPTH, D), 0.02),
        "ln2_g": gain((DEPTH, D)),
        "ln2_b": nrm((DEPTH, D), 0.02),
        "w_router_group": nrm((DEPTH, D, N_GROUPS), D ** -0.5),
        "b_router_group": nrm((DEPTH, N_GROUPS), 0.01),
        "w_router_expert": nrm((DEPTH, D, N_EXPERTS), D ** -0.5),
        "b_router_expert": nrm((DEPTH, N_EXPERTS), 0.01),
        "w_gate": nrm((DEPTH, N_EXPERTS, D, D_EXPERT), D ** -0.5),
        "w_up": nrm((DEPTH, N_EXPERTS, D, D_EXPERT), D ** -0.5),
        "w_down": nrm((DEPTH, N_EXPERTS, D_EXPERT, D), D_EXPERT ** -0.5 * DN_BETA),
    }

def second_block(x, even_w_in, even_lam_q1, even_lam_k1, even_lam_q2, even_lam_k2, even_subln_g,
              even_q_norm_g, even_w_uq, even_kv_norm_g, even_w_ukv, even_w_o,
              odd_w_qkv, odd_rel_bias, odd_w_o, ln1_g, ln1_b, ln2_g, ln2_b,
              w_router_group, b_router_group, w_router_expert, b_router_expert,
              w_gate, w_up, w_down):
    S = x.shape[1]
    rope_a = rope_tables(S, A_ROT)
    rope_b = rope_tables(S, B_ROPE)
    for i in range(DEPTH):
        j = i // 2
        if i % 2 == 0:
            lambda_init = 0.8 - 0.6 * math.exp(-0.3 * i)
            m = even_mixer(x, even_w_in[j], even_lam_q1[j], even_lam_k1[j], even_lam_q2[j],
                           even_lam_k2[j], even_subln_g[j], even_q_norm_g[j], even_w_uq[j],
                           even_kv_norm_g[j], even_w_ukv[j], even_w_o[j], lambda_init, rope_a, rope_b)
        else:
            m = odd_mixer(x, odd_w_qkv[j], odd_rel_bias[j], odd_w_o[j])
        x = layer_norm(DN_ALPHA * x + m, ln1_g[i], ln1_b[i])
        f = hier_moe(x, w_router_group[i], b_router_group[i], w_router_expert[i], b_router_expert[i],
                     w_gate[i], w_up[i], w_down[i])
        x = layer_norm(DN_ALPHA * x + f, ln2_g[i], ln2_b[i])
    return x


def setup_inputs(seed=0):
    out = dict(first_inputs(seed))
    for name, value in second_inputs(seed + 1).items():
        if name != "x":
            out[name + "_2"] = value
    return out


def reference(
    x, norm1_g, w_in, hgrn_lb_logits, hgrn_onorm_g, nsa_qn_g, nsa_kn_g, nsa_cmp_pos, nsa_cmp_w1,
    nsa_cmp_w2, fox_qn_g, fox_kn_g, fox_fb, w_o, norm2_g, w_up, w_down, even_w_in_2,
    even_lam_q1_2, even_lam_k1_2, even_lam_q2_2, even_lam_k2_2, even_subln_g_2, even_q_norm_g_2,
    even_w_uq_2, even_kv_norm_g_2, even_w_ukv_2, even_w_o_2, odd_w_qkv_2, odd_rel_bias_2,
    odd_w_o_2, ln1_g_2, ln1_b_2, ln2_g_2, ln2_b_2, w_router_group_2, b_router_group_2,
    w_router_expert_2, b_router_expert_2, w_gate_2, w_up_2, w_down_2,
):
    x = first_block(
        x, norm1_g, w_in, hgrn_lb_logits, hgrn_onorm_g, nsa_qn_g, nsa_kn_g, nsa_cmp_pos,
        nsa_cmp_w1, nsa_cmp_w2, fox_qn_g, fox_kn_g, fox_fb, w_o, norm2_g, w_up, w_down,
    )
    return second_block(
        x, even_w_in_2, even_lam_q1_2, even_lam_k1_2, even_lam_q2_2, even_lam_k2_2,
        even_subln_g_2, even_q_norm_g_2, even_w_uq_2, even_kv_norm_g_2, even_w_ukv_2,
        even_w_o_2, odd_w_qkv_2, odd_rel_bias_2, odd_w_o_2, ln1_g_2, ln1_b_2, ln2_g_2, ln2_b_2,
        w_router_group_2, b_router_group_2, w_router_expert_2, b_router_expert_2, w_gate_2,
        w_up_2, w_down_2,
    )


_drawn_inputs = setup_inputs


def setup_inputs(seed=0):
    import zlib

    import numpy as np

    out = dict(_drawn_inputs(seed))
    spreads = {}
    factors = {'hgrn_lb_logits': 2.873,
     'hgrn_onorm_g': 4.092,
     'nsa_qn_g': 8.0,
     'nsa_kn_g': 8.0,
     'nsa_cmp_pos': 5.445,
     'fox_qn_g': 5.579,
     'fox_kn_g': 6.067,
     'fox_fb': 27.41,
     'even_lam_q1_2': 7.242,
     'even_lam_k1_2': 8.0,
     'even_lam_q2_2': 8.0,
     'even_lam_k2_2': 6.391,
     'even_subln_g_2': 33.202,
     'even_q_norm_g_2': 8.0,
     'even_w_uq_2': 2.927,
     'even_kv_norm_g_2': 8.0,
     'odd_rel_bias_2': 43.86,
     'b_router_group_2': 6.918,
     'b_router_expert_2': 20.98}
    for name, (base, spread) in spreads.items():
        noise = np.random.default_rng([zlib.crc32(name.encode()), seed]).standard_normal(out[name].shape)
        drawn = base * np.exp(spread * noise) if base else spread * noise
        out[name] = jnp.asarray(drawn.astype(out[name].dtype))
    for name, factor in factors.items():
        out[name] = (out[name] * factor).astype(out[name].dtype)
    return out
```

```python
import math
from contextlib import ExitStack

import concourse.bass as bass
from concourse import mybir

F32 = mybir.dt.float32
F32R = mybir.dt.float32r
U32 = mybir.dt.uint32
ALU = mybir.AluOpType
ACT = mybir.ActivationFunctionType
AX = mybir.AxisListType

ADD, SUB, MUL, MAX, MIN = ALU.add, ALU.subtract, ALU.mult, ALU.max, ALU.min
NEG = -1e30
TINY = 1e-30
S, D = 512, 1024
CAP = 128
NBLK = (S - CAP + 127) // 128
ROWS = CAP + 128 * NBLK
NE = 32
BIG = 1 << 20

OFF = {}
_o = 0
for _n, _w in (("ident", 128), ("mask", 512), ("utri", 128), ("ustr", 128), ("ones", 128), ("hm", 1024),
               ("rope", 64), ("ropec", 16), ("cmadd", 128), ("cmmul", 128), ("tokid", 8)):
    OFF[_n] = (_o, _w)
    _o += _w
NCONST = _o


def constants():
    import numpy as np
    c = np.zeros((128, NCONST), np.float32)

    def at(name):
        o, w = OFF[name]
        return c[:, o:o + w]

    p = np.arange(128)
    at("ident")[:] = np.eye(128)
    at("mask")[:] = np.where(np.arange(512)[None, :] - 384 <= p[:, None], 0.0, NEG)
    at("utri")[:] = (p[:, None] <= p[None, :])
    at("ustr")[:] = (p[:, None] < p[None, :])
    at("ones")[:] = 1.0
    hm = at("hm").reshape(128, 8, 128)
    hm[:, 0] = np.eye(128)
    for i in range(7):
        L = 1 << i
        s, t = p[:, None], p[None, :]
        hm[:, 1 + i] = (s // (2 * L) == t // (2 * L)) & (s // L % 2 == 0) & (t // L % 2 == 1)
    c[:, OFF["hm"][0]:OFF["hm"][0] + 1024] = hm.reshape(128, 1024)
    inv = np.float32(500000.0) ** (-np.arange(0, 16, 2, dtype=np.float32) / np.float32(16))
    ang = np.arange(S, dtype=np.float32)[:, None] * inv[None, :].astype(np.float32)
    r = np.stack([np.cos(ang), np.sin(ang)], 1).reshape(4, 128, 16).transpose(1, 0, 2)
    c[:, OFF["rope"][0]:OFF["rope"][0] + 64] = r.reshape(128, 64)
    end = np.arange(31) * 16 + 31
    angc = end.astype(np.float32)[:, None] * inv[None, :]
    c[:31, OFF["ropec"][0]:OFF["ropec"][0] + 16] = np.concatenate([np.cos(angc), np.sin(angc)], 1)
    ok = np.zeros((128, 4, 32), bool)
    for t in range(4):
        ok[:, t, :31] = end[None, :] <= (128 * t + p)[:, None]
    c[:, OFF["cmadd"][0]:OFF["cmadd"][0] + 128] = np.where(ok, 0, NEG).reshape(128, 128)
    c[:, OFF["cmmul"][0]:OFF["cmmul"][0] + 128] = ok.reshape(128, 128)
    tok = 2 * (128 * np.arange(4)[None, :, None] + p[:, None, None]) + np.arange(2)[None, None, :]
    c[:, OFF["tokid"][0]:OFF["tokid"][0] + 8] = tok.reshape(128, 8)
    inv2 = np.float32(500000.0) ** (-np.arange(0, 32, 2, dtype=np.float32) / np.float32(32))
    ang2 = np.arange(S, dtype=np.float32)[:, None] * inv2[None, :]
    r2 = np.stack([np.cos(ang2), np.sin(ang2)], 1).reshape(4, 128, 32).transpose(1, 0, 2)
    return {"c_main": c, "c_rope2": np.ascontiguousarray(r2.reshape(128, 128).astype(np.float32)),
            "c_eio": np.tile(np.arange(32, dtype=np.float32)[None, :], (128, 1)),
            "c_big": np.full((ROWS, NE), BIG, np.uint32)}


class Sem:

    def __init__(self, handle):
        self.h, self.n = handle, 0

    def add(self, k):
        self.n += k
        return (self, self.n)


class Queue:

    def __init__(self, prog, name, chained):
        self.prog, self.name, self.chained = prog, name, chained
        self.sem = prog.sem("q_" + name)
        self.eng = {"pe": prog.nc.tensor, "dve": prog.nc.vector, "act": prog.nc.scalar,
                    "pool": prog.nc.gpsimd, "sp": prog.nc.sync}[name]
        self.seen = {}

    def wait(self, *deps):
        for sem, value in flat(deps):
            if self.seen.get(sem, 0) < value:
                self.seen[sem] = value
                self.eng.wait_ge(sem.h, value)

    def __call__(self, fn, *deps, chain=None):
        chain = self.chained if chain is None else chain
        self.wait(deps, self.last() if chain else ())
        tok = self.sem.add(1)
        fn(self.eng).then_inc(self.sem.h, 1)
        return tok

    def last(self):
        return (self.sem, self.sem.n)

    def dma(self, sem, fn, *deps):
        self.wait(deps)
        tok = sem.add(16)
        fn(self.eng).then_inc(sem.h, 16)
        return tok


def flat(x):
    if isinstance(x, tuple) and len(x) == 2 and isinstance(x[0], Sem):
        if x[1] > 0:
            yield x
        return
    for y in x:
        if y is not None:
            yield from flat(y)


class Ring:

    def __init__(self, bufs, free=()):
        self.bufs = bufs
        self.free = [free for _ in bufs]
        self.held = [False] * len(bufs)
        self.at = 0

    def take(self):
        for _ in self.bufs:
            i = self.at
            self.at = (self.at + 1) % len(self.bufs)
            if not self.held[i]:
                self.held[i] = True
                return i, self.bufs[i], self.free[i]
        raise RuntimeError("all held")

    def give(self, i, *toks):
        self.held[i] = False
        self.free[i] = toks


LAG = 2


def run_lagged(units):
    live = []
    units = iter(units)
    more = True
    while more or live:
        if more:
            try:
                live.append([next(units), 0])
            except StopIteration:
                more = False
        nxt = []
        for g in live:
            g[1] += 1
            if (g[1] - 1) % LAG:
                nxt.append(g)
                continue
            try:
                next(g[0])
                nxt.append(g)
            except StopIteration:
                pass
        live = nxt


class Program:
    def __init__(self, nc, ctx, A, out):
        self.nc, self.ctx, self.A, self.out = nc, ctx, A, out
        self.nsem = 0
        self.T = Queue(self, "pe", False)
        self.V = Queue(self, "dve", True)
        self.C = Queue(self, "act", True)
        self.G = Queue(self, "pool", True)
        self.Y = Queue(self, "sp", False)
        self.total = 52900
        at = (nc.sbuf_base + 31) // 32 * 32
        ctx.enter_context(nc.sbuf_tensor("arena", [128, self.total], F32))
        self.mem = nc.alloc_sbuf_tensor_at("mem", [128, self.total], F32, offset=at)
        self.at, self.rounded = at, {}
        self.memu = ctx.enter_context(nc.sbuf_tensor("memu", [128, 160], U32))
        self.banks = Ring([ctx.enter_context(nc.psum_tensor(f"ps{i}", [128, 512], F32)) for i in range(8)])
        self.osem = {n: ctx.enter_context(nc.semaphore("over_" + n)) for n in
                     ("idx", "w", "row", "gath", "turn", "xt", "up", "sig", "v", "down", "y", "out")}
        self.top = 0

    def sem(self, name):
        self.nsem += 1
        return Sem(self.ctx.enter_context(self.nc.semaphore(f"{name}_{self.nsem}")))

    def m(self, off, n, parts=128, p0=0):
        assert off + n <= self.total, (off, n)
        return self.mem[p0:p0 + parts, off:off + n]

    def r(self, off, n):
        assert off + n <= self.total and n <= 4096, (off, n)
        if (off, n) not in self.rounded:
            self.rounded[off, n] = self.nc.alloc_sbuf_tensor_at(f"r{off}_{n}", [128, n], F32R,
                                                                offset=self.at + 4 * off)
        return self.rounded[off, n][:, :]

    def alloc(self, n):
        o = self.top
        self.top += n
        assert self.top <= self.total, self.top
        return o

    def now(self):
        return (self.T.last(), self.V.last(), self.C.last(), self.G.last())

    def mm(self, out, pairs, *deps, start=True, stop=True, skip=False):
        def fn(e):
            n = len(pairs)
            for i, (a, b) in enumerate(pairs):
                r = e.matmul(out, a, b, start=(start and i == 0), stop=(stop and i == n - 1),
                             skip_group_check=skip)
            return r
        return self.T(fn, *deps)

    def tr(self, items, *deps):
        ident = self.ident

        def fn(e):
            for o, i in items:
                k = i.shape[0]
                r = e.transpose(o, i, ident[0:k, 0:k])
            return r
        return self.T(fn, *deps)

    def tt(self, out, a, b, op, *deps, q=None, **kw):
        return (q or self.V)(lambda e: e.tensor_tensor(out, a, b, op), *deps, **kw)

    def ts(self, out, a, s1, s2, op0, op1=None, *deps, q=None, **kw):
        if op1 is None:
            return (q or self.V)(lambda e: e.tensor_scalar(out, a, s1, None, op0), *deps, **kw)
        return (q or self.V)(lambda e: e.tensor_scalar(out, a, s1, s2, op0, op1), *deps, **kw)

    def stt(self, out, a, s, b, op0, op1, *deps, **kw):
        return self.V(lambda e: e.scalar_tensor_tensor(out, a, s, b, op0, op1), *deps, **kw)

    def act(self, out, a, f, *deps, chain=None, **kw):
        return self.C(lambda e: e.activation(out, a, f, **kw), *deps, chain=chain)

    def red(self, out, a, op, *deps, negate=False, chain=None):
        return self.V(lambda e: e.tensor_reduce(out, a, AX.X, op, negate=negate), *deps, chain=chain)

    def rec(self, out, a, *deps):
        return self.V(lambda e: e.reciprocal(out, a), *deps)

    def rsqrt(self, x, scale, eps, *deps):
        a = self.ts(x, x, scale, eps, MUL, ADD, *deps)
        a = self.act(x, x, ACT.Sqrt, a)
        return self.rec(x, x, a)

    def copy(self, out, a, *deps, **kw):
        return self.V(lambda e: e.tensor_copy(out, a), *deps, **kw)

    def load(self, pairs, *deps, q=None, name="ld"):
        q = q or self.Y
        s = self.sem(name)
        for o, i in pairs:
            tok = q.dma(s, (lambda o, i: lambda e: e.dma_start(o, i))(o, i), *deps)
        return tok

    def wstart(self, chunks, slots):
        self.chunks, self.wnext, self.wuse = chunks, 0, 0
        self.wsem = {}
        self.wready = {}
        for s in slots:
            self.wissue(s, ())

    def wissue(self, slot, deps):
        if self.wnext >= len(self.chunks):
            return
        i = self.wnext
        self.wnext += 1
        if slot not in self.wsem:
            self.wsem[slot] = self.sem("w")
        for fn in self.chunks[i](self.m(slot, 4096)):
            tok = self.Y.dma(self.wsem[slot], fn, *deps)
        self.wready[i] = (slot, tok)

    def wtake(self):
        slot, tok = self.wready[self.wuse]
        self.wuse += 1
        return slot, self.m(slot, 4096), tok

    def wgive(self, slot, *deps, keep=True):
        if keep:
            self.wissue(slot, deps)


def dram_chunk(src, k, cols, parts=128):
    c0, n = cols

    def make(buf):
        dst = buf[0:parts, 0:k * n].rearrange("p (k n) -> p k n", k=k)
        s = src[:, c0:c0 + n].rearrange("(k p) n -> p k n", p=parts)
        return [lambda e: e.dma_start(dst, s)]
    return make


def bc(ap, axis, n):
    a = ap.unsqueeze(axis)
    sh = list(a.shape)
    sh[axis] = n
    return a.broadcast_to(sh)


def weight_chunks(A):
    out = []
    for l in range(2):
        w = A["w_in"][l]
        out.append(dram_chunk(w, 8, (0, 512)))
        for c in range(512, 3100, 512):
            out.append(dram_chunk(w, 8, (c, min(512, 3100 - c))))
        for which in range(2):
            out.append(dram_chunk(A["nsa_cmp_w1"][l, which], 32, (0, 128), parts=64))
        for n in range(2):
            out.append(dram_chunk(A["w_o"][l], 8, (512 * n, 512)))
        for half in range(2):
            for c in range(4 * half, 4 * half + 4):
                out.append(dram_chunk(A["w_up"][l], 8, (512 * c, 512)))
            for n in range(2):
                for kq in range(2 * half, 2 * half + 2):
                    out.append(dram_chunk(A["w_down"][l, 1024 * kq:1024 * kq + 1024, :], 8, (512 * n, 512)))
    w = A["even_w_in_2"][0]
    for c in range(0, 1952, 512):
        out.append(dram_chunk(w, 8, (c, min(512, 1952 - c))))

    def mla(buf):
        a = buf[:, 0:1536].rearrange("p (k n) -> p k n", k=2)
        return [lambda e: e.dma_start(a, A["even_w_uq_2"][0].rearrange("(k p) n -> p k n", p=128)),
                lambda e: e.dma_start(buf[:, 1536:2560], A["even_w_ukv_2"][0])]
    out.append(mla)
    for n in range(2):
        out.append(dram_chunk(A["even_w_o_2"][0], 8, (512 * n, 512)))
    moe(A, out, 0)
    for c in range(6):
        out.append(dram_chunk(A["odd_w_qkv_2"][0], 8, (512 * c, 512)))
    for n in range(2):
        out.append(dram_chunk(A["odd_w_o_2"][0], 8, (512 * n, 512)))
    moe(A, out, 1)
    return out


def moe(A, out, l):
    for e in range(NE):
        out.append(dram_chunk(A["w_gate_2"][l, e], 8, (0, 512)))
        out.append(dram_chunk(A["w_up_2"][l, e], 8, (0, 512)))
        out.append(dram_chunk(A["w_down_2"][l, e], 4, (0, 1024)))


def build(nc, A, out):
    ctx = ExitStack()
    with ctx:
        P = Program(nc, ctx, A, out)
        setup(P)
        for l in range(2):
            first_layer(P, l)
        for l in range(2):
            second_layer(P, l)
        finish(P)


def setup(P):
    A = P.A
    P.X = P.m(P.alloc(4096), 4096).rearrange("p (t n) -> p t n", t=4)
    P.HTo = P.alloc(4096)
    P.HT = P.m(P.HTo, 4096).rearrange("p (k n) -> p k n", k=8)
    P.slots = [P.alloc(4096) for _ in range(3)]
    P.spare = P.alloc(4096)
    P.pieces = Ring([P.spare + 1024 * i for i in range(4)])
    co = P.alloc(NCONST)

    def const(name):
        o, w = OFF[name]
        return P.m(co + o, w)
    P.ident = const("ident")
    P.cmask, P.utri, P.ustr, P.ones = const("mask"), const("utri"), const("ustr"), const("ones")
    P.hm = const("hm").rearrange("p (l n) -> p l n", l=8)
    P.rope = const("rope").rearrange("p (t n) -> p t n", t=4)
    P.ropec = const("ropec")
    P.cmadd = const("cmadd").rearrange("p (t n) -> p t n", t=4)
    P.cmmul = const("cmmul").rearrange("p (t n) -> p t n", t=4)
    P.tokid = const("tokid")
    sm = P.alloc(1120)
    P.g = []
    n = 0

    def take(w):
        nonlocal n
        n += w
        return P.m(sm + n - w, w)
    pairs = [(P.m(co, NCONST), A["c_main"])]
    P.lg = take(4).rearrange("p (j l) -> p j l", j=2)
    pairs.append((P.lg.rearrange("p j l -> p (j l)"), A["hgrn_lb_logits"]))
    for l in range(2):
        g = {}
        g["g1"], g["g2"] = take(8), take(8)
        pairs.append((g["g1"], A["norm1_g"][l]))
        pairs.append((g["g2"], A["norm2_g"][l]))
        for nm in ("hgrn_onorm_g", "nsa_qn_g", "nsa_kn_g", "fox_qn_g", "fox_kn_g"):
            g[nm] = take(64)
            pairs.append((g[nm], A[nm][l].partition_broadcast(128)))
        g["fb"] = take(4)
        pairs.append((g["fb"], A["fox_fb"][l].partition_broadcast(128)))
        P.g.append(g)
    P.small = take(160)
    P.lbw = take(24)
    P.eps = take(4)
    assert n <= 1120
    xs = P.sem("x")
    for t in range(4):
        P.xload = P.Y.dma(xs, (lambda t: lambda e: e.dma_start(P.X[:, t, :], A["x"][0, 128 * t:128 * t + 128, :]))(t))
    P.cload = P.load(pairs)
    P.wstart(weight_chunks(A), P.slots)
    P.V(lambda e: e.memset(P.eps[:, 0:1], 0.0))
    P.L0 = P.top
    P.jA = P.m(P.L0, 0 + 512)
    P.V.wait(P.cload, P.xload)
    P.C.wait(P.cload, P.xload, P.V.last())
    P.T.wait(P.cload, P.xload)
    P.G.wait(P.cload, P.xload)
    w = P.lbw[:, 0:4].rearrange("p (j l) -> p j l", j=2)
    mx = P.lbw[:, 4:6]
    P.red(mx, P.lg, MAX)
    t = P.tt(w, P.lg, bc(mx, 2, 2), SUB)
    t = P.act(w, w, ACT.Exp, t)
    P.red(mx, w, ADD, t)
    P.rec(mx, mx)
    P.tt(w, w, bc(mx, 2, 2), MUL)
    P.lb = P.lbw[:, 8:12].rearrange("p (l j) -> p l j", l=2)
    P.tt(P.lb[:, 0, :], w[:, :, 0], w[:, :, 0], SUB)
    P.tt(P.lb[:, 1, :], w[:, :, 0], w[:, :, 1], ADD)
    P.tt(P.lb[:, 1, :], P.lb[:, 1, :], w[:, :, 0], SUB)
    P.olb = P.lbw[:, 12:16].rearrange("p (l j) -> p l j", l=2)
    P.ts(P.olb, P.lb, -1.0, 1.0, MUL, ADD)


def halves(P, off):
    return [P.r(off + 2048 * i, 2048).rearrange("p (k n) -> p k n", k=4) for i in range(2)]


def block(hs):
    return lambda kk: hs[kk // 4][:, kk % 4, :]


def transpose_x(P, src_of, scratch, norm=None, deps=(), lo=None, ready=()):
    done = []
    ring = Ring([P.m(scratch + 1024 * i, 1024) for i in range(2)], deps)
    tmp = Ring([P.m(scratch + 2048 + 512 * i, 512) for i in range(2)], deps)
    if lo is not None:
        hr, lr = halves(P, P.HTo), halves(P, lo)
    for t in range(4):
        if norm is not None:
            i, xn, fr = ring.take()
            ss = P.small[:, t:t + 1]
            P.act(xn, P.X[:, t, :], ACT.Square, fr, P.V.last(), accum_out=ss)
            r = P.rsqrt(ss, 1.0 / D, 1e-6, P.C.last())
            src = xn
            rd = P.act(xn, P.X[:, t, :], ACT.Copy, r, scale=ss)
        else:
            src, rd = src_of(t), ready
        for half in range(2):
            b, bank, bf = P.banks.take()
            v = bank[:, :].rearrange("p (k n) -> p k n", k=4)
            tk = P.tr([(v[:, k, :], src[:, 128 * (4 * half + k):128 * (4 * half + k) + 128]) for k in range(4)],
                      rd, bf)
            at = (slice(None), slice(4 * half, 4 * half + 4), slice(128 * t, 128 * t + 128))
            if lo is None:
                e = P.copy(P.HT[at], v, tk, deps, chain=False)
                P.banks.give(b, e)
                done.append(e)
                continue
            x = v
            if norm is not None:
                j, tb, tf = tmp.take()
                x = tb.rearrange("p (k n) -> p k n", k=4)
                e = P.tt(x, v, bc(norm[:, 4 * half:4 * half + 4], 2, 128), MUL, tk, tf, deps, chain=False)
                P.banks.give(b, e)
                tk2 = e
            else:
                tk2 = tk
            cut = (slice(None), slice(None), slice(128 * t, 128 * t + 128))
            h = P.act(hr[half][cut], x, ACT.Copy, tk2, deps, chain=False)
            e = P.tt(lr[half][cut], x, hr[half].bitcast(F32)[cut], SUB, tk2, h, deps, chain=False)
            if norm is not None:
                tmp.give(j, e)
            else:
                P.banks.give(b, e)
            done += [e, h]
        if norm is not None:
            ring.give(i, tk)
    return done


class Job:

    def __init__(self, mode, n, hi, lo, evac, acc=None, first=True, last=True, k=8):
        self.mode, self.n, self.hi, self.lo, self.evac = mode, n, hi, lo, evac
        self.acc, self.first, self.last, self.k = acc, first, last, k


def run_dense(P, jobs, ready):
    plan = [(job, kk) for job in jobs for kk in range(job.k)]
    made = []
    held = {}

    def make(i):
        job, kk = plan[i]
        if kk == 0:
            held["w"] = P.wtake()
        slot, buf, wt = held["w"]
        n = job.n
        w = buf[:, kk * n:kk * n + n]
        pi, po, pf = P.pieces.take()
        hi, lo = P.r(po, 512)[:, 0:n], P.r(po + 512, 512)[:, 0:n]
        hf = hi.bitcast(F32)
        h = P.act(hi, w, ACT.Copy, wt, pf, chain=False)
        e = P.tt(lo, w, hf, SUB, wt, pf, h, chain=False)
        if kk == job.k - 1:
            P.wgive(slot, h, e)
        made.append((pi, hi, lo, h, e))

    depth = len(P.pieces.bufs)
    for i in range(min(depth - 1, len(plan))):
        make(i)
    for i, (job, kk) in enumerate(plan):
        if i + depth - 1 < len(plan):
            make(i + depth - 1)
        if kk == 0 and job.first:
            job.acc[:] = [P.banks.take() for _ in range(4)]
        pi, wh, wl, h, e = made[i]
        xh, xl = job.hi(kk), job.lo(kk)
        n = job.n

        def fn(eng):
            for j in range(4):
                c = slice(128 * j, 128 * j + 128)
                if job.mode == "tok":
                    o = job.acc[j][1][:, 0:n]
                    pairs = ((xh[:, c], wh), (xh[:, c], wl), (xl[:, c], wh))
                else:
                    o = job.acc[j][1][:, :]
                    pairs = ((wh[:, c], xh), (wh[:, c], xl), (wl[:, c], xh))
                for m, (a, b) in enumerate(pairs):
                    r = eng.matmul(o, a, b, start=(job.first and kk == 0 and m == 0),
                                   stop=(job.last and kk == job.k - 1 and m == 2))
            return r
        tk = P.T(fn, h, e, ready, [a[2] for a in job.acc] if kk == 0 and job.first else ())
        P.pieces.give(pi, tk)
        if kk == job.k - 1 and job.last:
            for j in range(4):
                ev = job.evac(j, job.acc[j][1][:, 0:n], tk)
                P.banks.give(job.acc[j][0], ev)
    return tk


class Evac:

    def __init__(self, P):
        self.P, self.n = P, 0

    def __call__(self, out, a, *deps):
        self.n += 1
        if self.n % 2:
            return self.P.act(out, a, ACT.Copy, *deps, chain=False)
        return self.P.copy(out, a, *deps, chain=False)


def head_norm(P, x, n, d, gain, scratch, *deps):
    sq = scratch[:, 0:n * d].rearrange("p (n d) -> p n d", n=n)
    ss = P.small[:, 16:16 + n]
    P.tt(sq, x, x, MUL, *deps)
    P.red(ss, sq, ADD)
    P.rsqrt(ss, 1.0 / d, 1e-6)
    np_ = x.shape[0]
    P.tt(x, x, bc(ss, 2, d)[0:np_], MUL)
    return P.tt(x, x, bc(gain, 1, n)[0:np_], MUL)


def rope(P, x, n, half, cs, scratch, *deps):
    p = x.shape[0]
    a = scratch[0:p, 0:n * half].rearrange("p (n d) -> p n d", n=n)
    b = scratch[0:p, n * half:2 * n * half].rearrange("p (n d) -> p n d", n=n)
    c = scratch[0:p, 2 * n * half:3 * n * half].rearrange("p (n d) -> p n d", n=n)
    cos, sin = bc(cs[0:p, 0:half], 1, n), bc(cs[0:p, half:2 * half], 1, n)
    x1, x2 = x[:, :, 0:half], x[:, :, half:2 * half]
    P.tt(a, x1, cos, MUL, *deps)
    P.tt(b, x2, sin, MUL)
    P.tt(c, x1, sin, MUL)
    P.tt(x1, a, b, SUB)
    P.tt(a, x2, cos, MUL)
    return P.tt(x2, a, c, ADD)


def mark(P, name):
    pass


class Rings:
    def __init__(self, P, o, deps):
        def ring(n):
            nonlocal o
            r = Ring([P.m(o + 512 * i, 512) for i in range(n)], deps)
            o += 512 * n
            return r
        self.S, self.E, self.T, self.M = ring(3), ring(4), ring(3), ring(2)
        self.sc = 0

    SIZE = 12 * 512


def softmax_rows(P, R, qk, nk, mask, sums, negm, ready):
    b, bank, bf = P.banks.take()
    s = bank[:, 0:nk]
    tk = P.mm(s, qk, bf, ready)
    ei, eb, ef = R.E.take()
    if mask is not None:
        m, mdeps = mask
        si, sb, sf = R.S.take()
        v = P.V(lambda e: e.tensor_tensor_reduce(sb[:, 0:nk], s, m, -1.0, 3e38, ADD, MIN, negm), tk, sf, mdeps,
                chain=False)
        P.banks.give(b, v)
        x = P.act(eb[:, 0:nk], sb[:, 0:nk], ACT.Exp, v, ef, bias=negm, scale=-1.0, accum_out=sums, chain=False)
        R.S.give(si, x)
    else:
        v = P.red(negm, s, MAX, tk, negate=True, chain=False)
        x = P.act(eb[:, 0:nk], s, ACT.Exp, v, ef, bias=negm, accum_out=sums, chain=False)
        P.banks.give(b, x)
    return ei, eb, x


def turn_and_apply(P, R, ev, ei, eb, x, nk, vf, out, odeps, start, dv):
    n = nk // 128
    b, bank, bf = P.banks.take()
    tk = P.tr([(bank[:, 128 * i:128 * i + 128], eb[:, 128 * i:128 * i + 128]) for i in range(n)], x, bf)
    R.E.give(ei, tk)
    ti, tb, tf = R.T.take()
    c = ev(tb[:, 0:nk], bank[:, 0:nk], tk, tf)
    P.banks.give(b, c)
    yield None
    tk = P.mm(out, [(tb[:, 128 * i:128 * i + 128], vf(i)) for i in range(n)], c, odeps, start=start, skip=True)
    R.T.give(ti, tk)
    yield tk


def first_layer(P, l):
    A, g = P.A, P.g[l]
    ev = Evac(P)
    base = P.L0
    PJo = base
    PJ = P.m(PJo, 4 * 2588).rearrange("p (t n) -> p t n", t=4)
    MIXo = PJo + 4 * 2588
    MIX = P.m(MIXo, 4096).rearrange("p (t n) -> p t n", t=4)
    W = MIXo + 4096
    ph = P.now()
    hdone = transpose_x(P, None, W, norm=g["g1"], deps=ph, lo=MIXo)
    xn_done = P.now()

    hg = [P.m(W + 1024 * i, 1024).rearrange("p (j n) -> p j n", j=2) for i in range(8)]
    Qf, Ff, Kf, Pf, Sf, Qt, Kt, T1 = hg
    hik, lok = block(halves(P, P.HTo)), block(halves(P, MIXo))

    def gates(j, ps, tk):
        if j < 2:
            return P.act(Qf[:, j, :], ps, ACT.Copy, tk, xn_done, scale=0.125)
        jj = j - 2
        a = P.act(T1[:, jj, :], ps, ACT.Exp, tk, xn_done, scale=-1.0)
        c = P.act(Kf[:, jj, :], ps, ACT.Exp)
        P.ts(T1[:, jj, :], T1[:, jj, :], 1.0, None, ADD, None, a, xn_done)
        P.rec(T1[:, jj, :], T1[:, jj, :])
        P.ts(Ff[:, jj, :], T1[:, jj, :], P.olb[:, l, jj:jj + 1], P.lb[:, l, jj:jj + 1], MUL, ADD)
        P.ts(Ff[:, jj, :], Ff[:, jj, :], TINY, None, MAX)
        P.ts(Kf[:, jj, :], Kf[:, jj, :], 1.0, None, ADD, None, c)
        P.rec(Kf[:, jj, :], Kf[:, jj, :])
        P.ts(Kf[:, jj, :], Kf[:, jj, :], P.olb[:, l, jj:jj + 1], None, MUL)
        return c
    pjt = []

    def to_pj(c0, n):
        def evac(t, o, tk):
            r = ev(PJ[:, t, c0:c0 + n], o, tk, ph)
            pjt.append(r)
            return r
        return evac
    jobs = [Job("feat", 512, hik, lok, gates, acc=[])]
    for c0 in range(0, 2588, 512):
        n = min(512, 2588 - c0)
        jobs.append(Job("tok", n, hik, lok, to_pj(c0, n), acc=[]))
    run_dense(P, jobs, hdone)
    mark(P, 'proj')
    hgrn(P, l, PJ, MIX, hg, pjt, W)
    nsa(P, l, PJ, MIX, W)
    fox(P, l, PJ, MIX, W)

    add = lambda t, n, o, tk: P.tt(P.X[:, t, 512 * n:512 * n + 512], P.X[:, t, 512 * n:512 * n + 512], o, ADD, tk,
                                   chain=False)
    mix_out(P, MIX, add, base)
    ph = P.now()
    hlo = base + 16384
    hdone = transpose_x(P, None, hlo + 4096, norm=g["g2"], deps=ph, lo=hlo)
    ah = [P.r(base + 512 * i, 512) for i in range(16)]
    al = [P.r(base + 8192 + 512 * i, 512) for i in range(16)]
    R2 = Ring([P.m(hlo + 4096 + 512 * i, 512) for i in range(4)], P.now())
    read = ()
    for half in range(2):
        at = []

        def relu2(c):
            def evac(j, ps, tk):
                ri, rb, rf = R2.take()
                a = P.act(rb, ps, ACT.Relu, tk, rf, chain=False)
                s = P.tt(rb, rb, rb, MUL, a, chain=False)
                h = P.act(ah[4 * c + j], rb, ACT.Copy, s, read, ph, chain=False)
                e = P.tt(al[4 * c + j], rb, ah[4 * c + j].bitcast(F32), SUB, h, s, read, ph, chain=False)
                R2.give(ri, e)
                at.extend((h, e))
                return a
            return evac
        run_dense(P, [Job("feat", 512, hik, block(halves(P, hlo)), relu2(c), acc=[])
                      for c in range(4)], hdone)
        jobs = []
        for n in range(2):
            acc = []
            for kq in range(2):
                jobs.append(Job("tok", 512, (lambda kk, kq=kq: ah[8 * kq + kk]),
                                (lambda kk, kq=kq: al[8 * kq + kk]),
                                (lambda t, o, tk, n=n: add(t, n, o, tk)), acc=acc, first=kq == 0, last=kq == 1))
        read = run_dense(P, jobs, at)


def mix_out(P, MIX, evac, lo):
    ph = P.now()
    done = transpose_x(P, lambda t: MIX[:, t, :], 0, deps=ph, lo=lo, ready=ph)
    run_dense(P, [Job("tok", 512, block(halves(P, P.HTo)), block(halves(P, lo)),
                      (lambda t, o, tk, n=n: evac(t, n, o, tk)), acc=[]) for n in range(2)], done)


def hgrn(P, l, PJ, MIX, hg, pjt, W):
    g = P.g[l]
    Qf, Ff, Kf, Pf, Sf, Qt, Kt, T1 = hg
    flat_ = lambda a: a.rearrange("p j n -> p (j n)")
    P.copy(flat_(Pf), flat_(Ff))
    P.V(lambda e: e.memset(flat_(Sf), 1.0))
    acc = [P.banks.take() for _ in range(2)]
    first = [True, True]
    scratch_o = W + 8 * 1024
    AR = Ring([P.m(scratch_o + 512 * i, 512) for i in range(3)], P.now())
    used = ()

    def pv(h, items, c, last):
        b, bank, bf = acc[h // 2]

        def fn(e):
            for i, (a, s, t) in enumerate(items):
                o = bank[:, (h % 2) * 256 + 64 * t:(h % 2) * 256 + 64 * t + 64]
                r = e.matmul(o, a, PJ[:, s, 64 * h:64 * h + 64], start=(first[h // 2] and i == 0),
                             stop=(last and i == len(items) - 1), skip_group_check=True)
            return r
        st = first[h // 2]

        def fn2(e, st=st):
            for i, (a, s, t) in enumerate(items):
                o = bank[:, (h % 2) * 256 + 64 * t:(h % 2) * 256 + 64 * t + 64]
                r = e.matmul(o, a, PJ[:, s, 64 * h:64 * h + 64], start=(st and i == 0), stop=True,
                             skip_group_check=True)
            return r
        first[h // 2] = False
        return P.T(fn2, c, bf, pjt)

    def unit(q, k, h, lev, qk_ready):
        rows = slice(64 * (h % 2), 64 * (h % 2) + 64)
        j = h // 2
        b, bank, bf = P.banks.take()
        ai, ab, af = AR.take()
        if lev < 8:
            def fn(e):
                for t in range(4):
                    s = slice(128 * t, 128 * t + 128)
                    r = e.matmul(bank[:, s], k[rows, j, s], q[rows, j, s], start=True, stop=True)
                return r
            tk = P.T(fn, qk_ready, bf)
            units_read.append(tk)
            v4 = bank[:, :].rearrange("p (t n) -> p t n", t=4)
            c = P.tt(ab.rearrange("p (t n) -> p t n", t=4), v4, bc(P.hm[:, lev, :], 1, 4), MUL, tk, af, chain=False)
            items = [(ab[:, 128 * t:128 * t + 128], t, t) for t in range(4)]
        elif lev == 8:
            def fn(e):
                for i, (s, t) in enumerate(((0, 1), (2, 3))):
                    r = e.matmul(bank[:, 128 * i:128 * i + 128], k[rows, j, 128 * s:128 * s + 128],
                                 q[rows, j, 128 * t:128 * t + 128], start=True, stop=True)
                return r
            tk = P.T(fn, qk_ready, bf)
            units_read.append(tk)
            c = P.act(ab[:, 0:256], bank[:, 0:256], ACT.Copy, tk, af, chain=False)
            items = [(ab[:, 0:128], 0, 1), (ab[:, 128:256], 2, 3)]
        else:
            def fn(e):
                for s in range(2):
                    r = e.matmul(bank[:, 256 * s:256 * s + 256], k[rows, j, 128 * s:128 * s + 128],
                                 q[rows, j, 256:512], start=True, stop=True)
                return r
            tk = P.T(fn, qk_ready, bf)
            units_read.append(tk)
            c = P.act(ab, bank[:, :], ACT.Copy, tk, af, chain=False)
            items = [(ab[:, 256 * s + 128 * t:256 * s + 128 * t + 128], s, 2 + t) for s in range(2) for t in range(2)]
        P.banks.give(b, c)
        yield
        tk = pv(h, items, c, lev == 9)
        AR.give(ai, tk)

    units_read = []

    def all_units():
        ready = P.now()
        for h in range(4):
            yield unit(Qf, Kf, h, 0, ready)
        for lev in range(1, 10):
            L = 1 << (lev - 1)
            rd = list(units_read)
            P.tt(flat_(Qt), flat_(Qf), flat_(Pf), MUL, rd)
            kq = P.tt(flat_(Kt), flat_(Kf), flat_(Sf), MUL)
            if lev < 9:
                pv_ = flat_(Pf).rearrange("p (n two l) -> p n two l", two=2, l=L)
                sv_ = flat_(Sf).rearrange("p (n two l) -> p n two l", two=2, l=L)
                nb = 1024 // (2 * L)
                right = pv_[:, :, 1, L - 1:L].broadcast_to([128, nb, L])
                left = pv_[:, :, 0, L - 1:L].broadcast_to([128, nb, L])
                P.tt(sv_[:, :, 0, :], sv_[:, :, 0, :], right, MUL)
                P.tt(pv_[:, :, 1, :], pv_[:, :, 1, :], left, MUL)
            for h in range(4):
                yield unit(Qt, Kt, h, lev, kq)
    run_lagged(all_units())

    mark(P, 'hgrn levels')
    O = P.m(W, 1024)
    ph = P.now()
    for b in range(2):
        e = P.copy(O[:, 512 * b:512 * b + 512], acc[b][1][:, :], ph)
        P.banks.give(acc[b][0], e)
    head_norm(P, O.rearrange("p (n d) -> p n d", n=16), 16, 64, g["hgrn_onorm_g"], P.m(W + 1024, 1024))
    Ov = O.rearrange("p (h t d) -> p h t d", h=4, t=4)
    G = P.m(W + 2048, 1024).rearrange("p (t n) -> p t n", t=4)
    x = P.act(G, PJ[:, :, 256:512], ACT.Exp, ph, pjt, scale=-1.0)
    P.ts(G, G, 1.0, None, ADD, None, x)
    P.rec(G, G)
    P.tt(G, G, PJ[:, :, 256:512], MUL)
    for t in range(4):
        P.tt(MIX[:, t, 0:256].rearrange("p (h d) -> p h d", h=4), Ov[:, :, t, :],
             G[:, t, :].rearrange("p (h d) -> p h d", h=4), MUL)


def nsa(P, l, PJ, MIX, W):
    g = P.g[l]
    ev = Evac(P)
    ph = P.now()
    R = Rings(P, W, ph)
    o = W + Rings.SIZE
    QT = P.m(o, 2048).rearrange("p (i n) -> p i n", i=4)
    KT = P.m(o + 2048, 1024).rearrange("p (i n) -> p i n", i=2)
    TG = P.m(o + 3072, 1024, parts=64).rearrange("p (g n) -> p g n", g=2)
    sc = P.m(o + 3072, 1024)
    qk = []
    for t in range(4):
        q = PJ[:, t, 512:1024].rearrange("p (n d) -> p n d", n=8)
        head_norm(P, q, 8, 64, g["nsa_qn_g"], sc, ph)
        rope(P, q, 8, 8, P.rope[:, t, :], sc)
        for c in (1280, 1536):
            k = PJ[:, t, c:c + 128].rearrange("p (n d) -> p n d", n=2)
            head_norm(P, k, 2, 64, g["nsa_kn_g"], sc)
            r = rope(P, k, 2, 8, P.rope[:, t, :], sc)
        b, bank, bf = P.banks.take()
        b2, bank2, bf2 = P.banks.take()
        v = bank[:, :].rearrange("p (i n) -> p i n", i=4)
        qq = PJ[:, t, 512:1024].rearrange("p (g i d) -> p i g d", g=2, i=4)
        qc = P.m(W, 512)
        c = P.copy(qc.rearrange("p (i g d) -> p i g d", i=4, g=2), qq, qk[-1:])
        tk = P.tr([(v[:, i, :], qc[:, 128 * i:128 * i + 128]) for i in range(4)]
                  + [(bank2[:, 128 * i:128 * i + 128], PJ[:, t, c_:c_ + 128]) for i, c_ in enumerate((1280, 1536))],
                  c, bf, bf2)
        qk.append(tk)
        e = P.act(QT[:, :, 128 * t:128 * t + 128], v, ACT.Copy, tk, ph, scale=0.125)
        P.banks.give(b, e)
        e = P.act(KT[:, :, 128 * t:128 * t + 128],
                  bank2[:, 0:256].rearrange("p (i n) -> p i n", i=2), ACT.Copy, tk, ph)
        P.banks.give(b2, e)
    qkr = P.now()
    mark(P, 'nsa qk prep')
    gs = P.m(P.HTo, 96).rearrange("p (t n) -> p t n", t=4)
    x = P.act(gs, PJ[:, :, 1792:1816], ACT.Exp, qkr, scale=-1.0)
    P.ts(gs, gs, 1.0, None, ADD, None, x)
    gr = P.rec(gs, gs)

    H0 = P.HTo + 96
    w2 = P.m(H0, 128).rearrange("p (w n) -> p w n", w=2)
    pos = P.m(H0 + 128, 64, parts=64).rearrange("p (w n) -> p w n", w=2)
    pr = P.m(H0 + 192, 64, parts=32)
    cw = P.load([(w2, P.A["nsa_cmp_w2"][l].rearrange("w k n -> k w n"))], ph)
    hid = P.m(H0 + 256, 64)
    u2 = P.m(H0 + 320, 64)
    kc = P.m(H0 + 384, 128)
    KC = P.m(H0 + 512, 32)
    VB = [P.m(H0 + 544 + 256 * i, 256) for i in range(2)]
    zz = P.V(lambda e: e.memset(P.m(H0 + 256, 800), 0.0), qkr)
    sc2 = P.m(H0 + 1056, 256)
    posb = P.m(H0 + 1312, 1)
    for which in range(2):
        pl = P.load([(pr, P.A["nsa_cmp_pos"][l, which])], P.now())
        b, bank, bf = P.banks.take()
        tk = P.tr([(bank[0:64, 0:32], pr)], pl, bf)
        e = P.copy(pos[:, which, :], bank[0:64, 0:32], tk)
        P.banks.give(b, e)
        for gg in range(2):
            b, bank, bf = P.banks.take()
            c = 1024 + 128 * which + 64 * gg
            tk = P.tr([(bank[0:64, 128 * t:128 * t + 128], PJ[:, t, c:c + 64]) for t in range(4)], bf, P.V.last())
            tg = P.copy(TG[:, gg, :], bank[0:64, :], tk, P.T.last())
            P.banks.give(b, tg)
        slot, buf, wt = P.wtake()
        w1 = buf[0:64, :].rearrange("p (l n) -> p l n", l=32)
        b, bank, bf = P.banks.take()
        ho = bank[:, 0:62].rearrange("p (g n) -> p g n", g=2)
        tk = P.mm(ho, [(w1[:, i, :], TG[:, :, i:i + 16 * 30 + 1:16]) for i in range(32)], wt, tg, bf)
        b2, bank2, bf2 = P.banks.take()
        tk2 = P.mm(bank2[:, 0:1], [(w1[:, i, :], pos[:, which, i:i + 1]) for i in range(32)], e, bf2)
        P.wgive(slot, tk2)
        pb = P.copy(posb, bank2[:, 0:1], tk2, zz)
        P.banks.give(b2, pb)
        hv = hid.rearrange("p (g n) -> p g n", g=2)
        P.V(lambda e: e.memset(hid, 0.0), P.now())
        x = P.ts(hv[:, :, 0:31], ho, posb, None, ADD, None, tk, P.T.last())
        P.banks.give(b, x)
        P.tt(u2, hid, hid, MUL)
        P.ts(u2, u2, 0.044715, 1.0, MUL, ADD)
        x = P.tt(u2, u2, hid, MUL)
        x = P.act(u2, u2, ACT.Tanh, x, scale=math.sqrt(2.0 / math.pi))
        P.ts(u2, u2, 1.0, 0.5, ADD, MUL, x)
        h = P.tt(hid, u2, hid, MUL)
        if which == 0:
            b, bank, bf = P.banks.take()

            def fn(e, bank=bank):
                for gg in range(2):
                    r = e.matmul(bank[0:31, 64 * gg:64 * gg + 64], hv[:, gg, 0:31], w2[:, 0, :], start=True, stop=True)
                return r
            tk = P.T(fn, h, bf, cw)
            e = P.copy(kc[0:31, :], bank[0:31, 0:128], tk)
            P.banks.give(b, e)
            kv = kc[0:31, :].rearrange("p (g d) -> p g d", g=2)
            sq = sc2[0:31, 0:128].rearrange("p (n d) -> p n d", n=2)
            ss = P.small[0:31, 16:18]
            P.tt(sq, kv, kv, MUL)
            P.red(ss, sq, ADD)
            P.rsqrt(ss, 1.0 / 64, 1e-6)
            P.tt(kv, kv, bc(ss, 2, 64), MUL)
            P.tt(kv, kv, bc(g["nsa_kn_g"][0:31, :], 1, 2), MUL)
            r = rope(P, kv, 2, 8, P.ropec, sc2)
            b, bank, bf = P.banks.take()
            tk = P.tr([(bank[:, 0:31], kc[0:31, :])], r, bf)
            e = P.copy(KC[:, 0:31], bank[:, 0:31], tk)
            P.banks.give(b, e)
        else:
            hr = P.m(H0 + 1344, 256).rearrange("p (g i n) -> p g i n", g=2, i=4)
            r = P.copy(hr, bc(hv, 2, 4), P.now())
            b, bank, bf = P.banks.take()

            def fn(e, bank=bank):
                for gg in range(2):
                    r = e.matmul(bank[:, 64 * gg:64 * gg + 64], hr[:, gg].rearrange("p i n -> p (i n)"), w2[:, 1, :],
                                 start=True, stop=True)
                return r
            tk = P.T(fn, r, bf, cw)
            for gg in range(2):
                for i in range(4):
                    e = P.copy(VB[gg][32 * i:32 * i + 32, 64 * i:64 * i + 64],
                               bank[32 * i:32 * i + 32, 64 * gg:64 * gg + 64], tk)
            P.banks.give(b, e)
    cready = P.now()
    mark(P, 'nsa compress')

    SUM = P.m(H0 + 1600, 192)
    TMP = P.m(H0 + 1792, 512)

    def units():
        for t in range(4):
            st = {}
            yield cmp_unit(t, st)
            for kind in range(2):
                yield from (att(t, kind, i, st) for i in range(8))
            yield fin(t, st)

    def cmp_unit(t, st):
        ei, eb, ef = R.E.take()
        s = eb[:, 0:256].rearrange("p (h n) -> p h n", h=8)
        mx = SUM[:, 0:8]
        v31 = s[:, :, 0:31]
        P.V(lambda e: e.memset(eb[:, 0:256], 0.0), ef)
        for gg in range(2):
            b, bank, bf = P.banks.take()
            v = bank[:, 0:128].rearrange("p (h n) -> p h n", h=4)

            def fn(e):
                for h in range(4):
                    rows = slice(64 * gg, 64 * gg + 64)
                    r = e.matmul(v[:, h, 0:31], QT[rows, h, 128 * t:128 * t + 128], KC[rows, 0:31],
                                 start=True, stop=True)
                return r
            tk = P.T(fn, bf, cready)
            e = P.tt(s[:, 4 * gg:4 * gg + 4, 0:31], v[:, :, 0:31], bc(P.cmadd[:, t, 0:31], 1, 4), ADD, tk)
            P.banks.give(b, e)
        P.red(mx, v31, MAX)
        x = P.tt(v31, v31, bc(mx, 2, 31), SUB)
        x = P.act(v31, v31, ACT.Exp, x)
        P.tt(v31, v31, bc(P.cmmul[:, t, 0:31], 1, 8), MUL, x)
        P.red(mx, v31, ADD)
        P.ts(mx, mx, TINY, None, MAX)
        P.rec(mx, mx)
        x = P.tt(v31, v31, bc(mx, 2, 31), MUL)
        yield
        b, bank, bf = P.banks.take()
        tk = P.tr([(bank[:, 128 * i:128 * i + 128], eb[:, 128 * i:128 * i + 128]) for i in range(2)], x, bf)
        R.E.give(ei, tk)
        ti, tb, tf = R.T.take()
        c = ev(tb[:, 0:256], bank[:, 0:256], tk, tf)
        P.banks.give(b, c)
        yield
        b, bank, bf = P.banks.take()

        def fn(e):
            for gg in range(2):
                r = e.matmul(bank[:, 256 * gg:256 * gg + 256], tb[:, 128 * gg:128 * gg + 128], VB[gg],
                             start=True, stop=True)
            return r
        tk = P.T(fn, c, bf)
        R.T.give(ti, tk)
        dst = MIX[:, t, 256:768].rearrange("p (h d) -> p h d", h=8)
        e = P.tt(dst, bank[:, :].rearrange("p (h d) -> p h d", h=8), bc(gs[:, t, 0:8], 2, 64), MUL, tk, gr)
        P.banks.give(b, e)

    def att(t, kind, i, st):
        h = i
        gg = h // 4
        rows = slice(64 * gg, 64 * gg + 64)
        nk = 128 * (t + 1)
        if i == 0:
            st[kind] = P.banks.take()
        ob = st[kind]
        k = 8 * kind + h
        ei, eb, x = softmax_rows(P, R, [(QT[rows, h % 4, 128 * t:128 * t + 128], KT[rows, kind, 0:nk])], nk,
                                 (P.cmask[:, 384 - 128 * t:512], ()), SUM[:, 16 + 16 * (t % 2) + k:17 + 16 * (t % 2) + k],
                                 SUM[:, 64 + 16 * (t % 2) + k:65 + 16 * (t % 2) + k], qkr)
        yield
        vc = (1408, 1664)[kind] + 64 * gg
        for tk in turn_and_apply(P, R, ev, ei, eb, x, nk, lambda j: PJ[:, j, vc:vc + 64],
                                 ob[1][:, 64 * h:64 * h + 64], ob[2], h == 0, 64):
            if tk is None:
                yield
        st["tk"] = tk

    def fin(t, st):
        yield
        yield
        yield
        for kind in range(2):
            r = SUM[:, 16 + 16 * (t % 2) + 8 * kind:24 + 16 * (t % 2) + 8 * kind]
            P.rec(r, r, st["tk"], P.C.last())
            P.tt(r, r, gs[:, t, 8 + 8 * kind:16 + 8 * kind], MUL)
            ob = st[kind]
            tv = TMP.rearrange("p (h d) -> p h d", h=8)
            e = P.tt(tv, ob[1][:, :].rearrange("p (h d) -> p h d", h=8), bc(r, 2, 64), MUL)
            P.banks.give(ob[0], e)
            P.tt(MIX[:, t, 256:768], MIX[:, t, 256:768], TMP, ADD)

    run_lagged(units())


def fox(P, l, PJ, MIX, W):
    g = P.g[l]
    ev = Evac(P)
    ph = P.now()
    R = Rings(P, W, ph)
    o = W + Rings.SIZE
    QT = P.m(o, 1024).rearrange("p (i n) -> p i n", i=2)
    KT = P.m(o + 1024, 1024).rearrange("p (i n) -> p i n", i=2)
    NC = P.m(P.HTo, 2048).rearrange("p (h n) -> p h n", h=4)
    H0 = P.HTo + 2048
    sc = P.m(o + 2048, 512)
    for t in range(4):
        for c, gn in ((1816, "fox_qn_g"), (2072, "fox_kn_g")):
            r = head_norm(P, PJ[:, t, c:c + 256].rearrange("p (n d) -> p n d", n=4), 4, 64, g[gn], sc, ph)
        b, bank, bf = P.banks.take()
        tk = P.tr([(bank[:, 128 * i:128 * i + 128], PJ[:, t, 1816 + 128 * i:1816 + 128 * i + 128]) for i in range(4)],
                  r, bf)
        v = bank[:, :].rearrange("p (i n) -> p i n", i=4)
        P.act(QT[:, :, 128 * t:128 * t + 128], v[:, 0:2, :], ACT.Copy, tk, ph, scale=0.125)
        e = P.act(KT[:, :, 128 * t:128 * t + 128], v[:, 2:4, :], ACT.Copy)
        P.banks.give(b, e)
    z = P.m(H0, 16)
    lf = P.m(H0 + 16, 16)
    zv = z.rearrange("p (t h) -> p t h", t=4)
    P.tt(zv, PJ[:, :, 2584:2588], bc(g["fb"], 1, 4), ADD, ph)
    P.ts(lf, z, -1.0, None, MUL)
    x = P.tt(lf, lf, z, MIN)
    x = P.act(lf, lf, ACT.Exp, x)
    x = P.ts(lf, lf, 1.0, None, ADD, None, x)
    x = P.act(lf, lf, ACT.Ln, x)
    P.ts(z, z, 0.0, None, MIN)
    x = P.tt(lf, z, lf, SUB, x)
    lv = lf.rearrange("p (t h) -> p t h", t=4)
    b, bank, bf = P.banks.take()
    cq = P.m(H0 + 32, 16)

    def fn(e):
        for t in range(4):
            for j in range(t + 1):
                r = e.matmul(bank[:, 4 * t:4 * t + 4], P.utri if j == t else P.ones, lv[:, j, :],
                             start=(j == 0), stop=(j == t))
        return r
    tk = P.T(fn, x, bf)
    cr = P.copy(cq, bank[:, 0:16], tk)
    P.banks.give(b, cr)
    lb = P.m(H0 + 64, 512)
    for h in range(4):
        r = P.copy(lb.rearrange("p (t n) -> p t n", t=4), bc(lv[:, :, h], 2, 128), P.T.last())
        b, bank, bf = P.banks.take()

        def fn(e, bank=bank):
            for t in range(4):
                for j in range(t + 1):
                    r = e.matmul(bank[:, 128 * t:128 * t + 128], lb[:, 128 * j:128 * j + 128],
                                 P.utri if j == t else P.ones, start=(j == 0), stop=(j == t))
            return r
        tk = P.T(fn, r, bf)
        e = P.act(NC[:, h, :], bank[:, :], ACT.Copy, tk, ph, scale=-1.0)
        P.banks.give(b, e)
    ready = P.now()
    mark(P, 'fox prep')
    SUM = P.m(H0 + 576, 64)

    def units():
        for t in range(4):
            st = {}
            for h in range(4):
                yield att(t, h, st)
            yield fin(t, st)

    def att(t, h, st):
        rows = slice(64 * (h % 2), 64 * (h % 2) + 64)
        nk = 128 * (t + 1)
        if h == 0:
            st["o"] = P.banks.take()
        ob = st["o"]
        mi, mb, mf = R.M.take()
        m = P.stt(mb[:, 0:nk], NC[:, h, 0:nk], cq[:, 4 * t + h:4 * t + h + 1], P.cmask[:, 384 - 128 * t:512],
                  ADD, ADD, mf, ready)
        k = 4 * (t % 2) + h
        ei, eb, x = softmax_rows(P, R, [(QT[rows, h // 2, 128 * t:128 * t + 128], KT[rows, h // 2, 0:nk])], nk,
                                 (mb[:, 0:nk], m), SUM[:, k:k + 1], SUM[:, 16 + k:17 + k], ready)
        R.M.give(mi, x)
        yield
        vc = 2328 + 64 * h
        for tk in turn_and_apply(P, R, ev, ei, eb, x, nk, lambda j: PJ[:, j, vc:vc + 64],
                                 ob[1][:, 64 * h:64 * h + 64], ob[2], h == 0, 64):
            if tk is None:
                yield
        st["tk"] = tk

    def fin(t, st):
        yield
        yield
        yield
        r = SUM[:, 4 * (t % 2):4 * (t % 2) + 4]
        P.rec(r, r, st["tk"], P.C.last())
        ob = st["o"]
        e = P.tt(MIX[:, t, 768:1024].rearrange("p (h d) -> p h d", h=4),
                 ob[1][:, 0:256].rearrange("p (h d) -> p h d", h=4), bc(r, 2, 64), MUL)
        P.banks.give(ob[0], e)

    run_lagged(units())



def layer_norm(P, t, gb, bb, deps, junk):
    x = P.X[:, t, :]
    s = P.small[:, 40 + 4 * t:44 + 4 * t]
    P.red(s[:, 0:1], x, ADD, deps)
    r = P.ts(s[:, 0:1], s[:, 0:1], -1.0 / D, None, MUL)
    a = P.act(x, x, ACT.Identity, r, bias=s[:, 0:1])
    a = P.act(junk, x, ACT.Square, accum_out=s[:, 1:2])
    P.rsqrt(s[:, 1:2], 1.0 / D, 1e-5, a)
    P.ts(x, x, s[:, 1:2], None, MUL)
    P.tt(x, x, gb, MUL)
    return P.tt(x, x, bb, ADD)


def ln_all(P, l, names, o):
    ph = P.now()
    gb, bb = P.m(o, 1024), P.m(o + 1024, 1024)
    junk = P.m(o + 2048, 1024)
    ld = P.load([(gb, P.A[names[0]][l].partition_broadcast(128)), (bb, P.A[names[1]][l].partition_broadcast(128))], ph)
    for t in range(4):
        layer_norm(P, t, gb, bb, (ld, ph), junk)


def second_layer(P, l):
    o = P.L0
    alpha = 4 ** 0.25
    add = lambda t, n, ps, tk: P.stt(P.X[:, t, 512 * n:512 * n + 512], P.X[:, t, 512 * n:512 * n + 512], alpha,
                                     ps, MUL, ADD, tk, chain=False)
    if l == 0:
        MIX, lo = even_mixer(P), o
    else:
        MIX, lo = odd_mixer(P), o + 12288
    mix_out(P, MIX, add, lo)
    ln_all(P, l, ("ln1_g_2", "ln1_b_2"), o)
    experts(P, l)
    ln_all(P, l, ("ln2_g_2", "ln2_b_2"), o)


def even_mixer(P):
    A = P.A
    ev = Evac(P)
    o = P.L0
    ph = P.now()
    hd = transpose_x(P, lambda t: P.X[:, t, :], 0, deps=ph, lo=o + 7808, ready=ph)
    QKV = P.m(o, 6144).rearrange("p (t n) -> p t n", t=4)
    LC = P.m(o + 6144, 1664).rearrange("p (t n) -> p t n", t=4)
    MIX = P.m(o + 7808, 4096).rearrange("p (t n) -> p t n", t=4)
    ro = o + 11904
    R = Rings(P, ro, ph)
    w0 = ro + Rings.SIZE
    hik, lok = block(halves(P, P.HTo)), block(halves(P, o + 7808))

    def to(c):
        if c < 3:
            return lambda t, ps, tk: ev(QKV[:, t, 512 * c:512 * c + 512], ps, tk, ph)
        return lambda t, ps, tk: ev(LC[:, t, :], ps, tk, ph)
    run_dense(P, [Job("tok", 512 if c < 3 else 416, hik, lok, to(c), acc=[])
                  for c in range(4)], hd)
    pr = P.now()
    mark(P, 'proj')
    QT = P.m(w0, 2048).rearrange("p (i n) -> p i n", i=4)
    KT = P.m(w0 + 2048, 2048).rearrange("p (i n) -> p i n", i=4)
    HB = P.HTo
    sc = P.m(HB, 512)
    lam4 = P.m(HB + 512, 256).rearrange("p (w n) -> p w n", w=4)
    lam = P.m(HB + 768, 8)
    sg = P.m(HB + 776, 128)
    r2 = P.m(HB + 904, 128).rearrange("p (t n) -> p t n", t=4)
    qg = P.m(HB + 1032, 256)
    kg = P.m(HB + 1288, 128)
    pl = P.load([(lam4[:, i, :], A[f"even_lam_{n}_2"][0].partition_broadcast(128))
                 for i, n in enumerate(("q1", "k1", "q2", "k2"))]
                + [(sg, A["even_subln_g_2"][0].partition_broadcast(128)),
                   (P.m(HB + 904, 128), A["c_rope2"]),
                   (qg, A["even_q_norm_g_2"][0].partition_broadcast(128)),
                   (kg, A["even_kv_norm_g_2"][0].partition_broadcast(128))], pr)
    pv = lam4.rearrange("p (a b) n -> p a b n", a=2)
    P.tt(pv[:, :, 0, :], pv[:, :, 0, :], pv[:, :, 1, :], MUL, pl, pr)
    x = P.red(lam[:, 0:2], pv[:, :, 0, :], ADD)
    x = P.act(lam[:, 0:2], lam[:, 0:2], ACT.Exp, x)
    P.tt(lam[:, 2:3], lam[:, 1:2], lam[:, 0:1], SUB, x)
    lam_init = 0.8 - 0.6 * math.exp(-0.3 * 0)
    P.ts(lam[:, 2:3], lam[:, 2:3], -lam_init, None, ADD)
    nlam = lam[:, 2:3]
    P.ts(sg, sg, 1.0 - lam_init, None, MUL)
    for t in range(4):
        r = rope(P, QKV[:, t, 0:1024].rearrange("p (n d) -> p n d", n=16), 16, 8, P.rope[:, t, :], sc)
        for q, dst, scale in ((0, QT, 0.125), (1, KT, 1.0)):
            b, bank, bf = P.banks.take()
            tk = P.tr([(bank[:, 128 * i:128 * i + 128], QKV[:, t, 512 * q + 128 * i:512 * q + 128 * i + 128])
                       for i in range(4)], r, bf)
            e = P.act(dst[:, :, 128 * t:128 * t + 128], bank[:, :].rearrange("p (i n) -> p i n", i=4), ACT.Copy,
                      tk, ph, scale=scale)
            P.banks.give(b, e)
    ready = P.now()
    SUM = P.m(HB + 1416, 64)
    obs = {}

    def units():
        for t in range(4):
            for h in range(4):
                yield att(t, h)
            yield fin(t)

    def att(t, h):
        if h == 0:
            obs[t] = P.banks.take()
        ob = obs[t]
        k = 8 * ((4 * t + h) % 4)
        es = []
        for m in range(2):
            rows = slice(64 * m, 64 * m + 64)
            es.append(softmax_rows(P, R, [(QT[rows, h, 128 * t:128 * t + 128], KT[rows, h, :])], 512, None,
                                   SUM[:, k + m:k + m + 1], SUM[:, k + 2 + m:k + 3 + m], ready))
        (e0, b0, x0), (e1, b1, x1) = es
        P.rec(SUM[:, k:k + 2], SUM[:, k:k + 2], x0, x1)
        c = P.tt(SUM[:, k + 1:k + 2], SUM[:, k + 1:k + 2], nlam, MUL)
        x = P.act(b1, b1, ACT.Copy, c, scale=SUM[:, k + 1:k + 2])
        x = P.stt(b0, b0, SUM[:, k:k + 1], b1, MUL, ADD, x)
        R.E.give(e1, x)
        yield
        for tk in turn_and_apply(P, R, ev, e0, b0, x, 512, lambda j: QKV[:, j, 1024 + 128 * h:1024 + 128 * h + 128],
                                 ob[1][:, 128 * h:128 * h + 128], ob[2], h == 0, 128):
            if tk is None:
                yield
        obs[t] = ob[0:3] + (tk,)

    def fin(t):
        yield
        yield
        yield
        ob = obs[t]
        dst = MIX[:, t, 0:512]
        e = P.copy(dst, ob[1][:, :], ob[3], ph)
        P.banks.give(ob[0], e)
        head_norm(P, dst.rearrange("p (h d) -> p h d", h=4), 4, 128, sg, sc)

    run_lagged(units())

    mark(P, 'diff')
    ph = P.now()
    slot, buf, wt = P.wtake()
    wuq = buf[:, 0:1536].rearrange("p (k n) -> p k n", k=2)
    wukv = buf[:, 1536:2560]
    UQ = P.m(o, 3072).rearrange("p (t n) -> p t n", t=4)
    QT2o = o + 3072
    QT2 = P.m(QT2o, 2048, parts=96).rearrange("p (i n) -> p i n", i=4)
    UKV = P.m(w0, 4096).rearrange("p (t n) -> p t n", t=4)
    KT2 = P.m(P.HTo + 2048, 2048, parts=96).rearrange("p (i n) -> p i n", i=4)
    kf = P.m(o + 5120, 384)
    for t in range(4):
        for c, n, gn in ((0, 256, qg), (256, 128, kg)):
            r = head_norm(P, LC[:, t, c:c + n].unsqueeze(1), 1, n, gn, sc, ph)
        rr = rope(P, LC[:, t, 384:416].unsqueeze(1), 1, 16, r2[:, t, :], sc)
        b, bank, bf = P.banks.take()
        tk = P.tr([(bank[:, 128 * i:128 * i + 128], LC[:, t, 128 * i:128 * i + 128]) for i in range(3)], r, bf)
        LT = P.m(ro, 384)
        c = P.copy(LT, bank[:, 0:384], tk, P.T.last())
        P.banks.give(b, c)
        for c0, n in ((0, 512), (512, 256)):
            b, bank, bf = P.banks.take()
            tk = P.mm(bank[:, 0:n], [(LT[:, 128 * k:128 * k + 128], wuq[:, k, c0:c0 + n]) for k in range(2)],
                      c, bf, wt)
            P.banks.give(b, P.act(UQ[:, t, c0:c0 + n], bank[:, 0:n], ACT.Copy, tk, ph))
        for c0 in (0, 512):
            b, bank, bf = P.banks.take()
            tk = P.mm(bank[:, :], [(LT[:, 256:384], wukv[:, c0:c0 + 512])], c, bf)
            P.banks.give(b, P.act(UKV[:, t, c0:c0 + 512], bank[:, :], ACT.Copy, tk, ph))
        rope(P, UQ[:, t, :].rearrange("p (h d) -> p h d", h=8)[:, :, 64:96], 8, 16, r2[:, t, :], sc, P.C.last())
    P.wgive(slot, tk)
    scale = (96.0) ** -0.5
    mark(P, 'mla proj')
    for hg in range(2):
        mark(P, 'hg')
        R = Rings(P, ro, P.now())
        for t in range(4):
            ph = P.now()
            kv = kf.rearrange("p (h d) -> p h d", h=4)
            uk = UKV[:, t, 512 * hg:512 * hg + 512].rearrange("p (h d) -> p h d", h=4)
            P.copy(kv[:, :, 0:64], uk[:, :, 0:64], ph)
            r = P.copy(kv[:, :, 64:96], bc(LC[:, t, 384:416], 1, 4))
            for q in range(2):
                b, bank, bf = P.banks.take()
                src = (lambda i: UQ[:, t, 384 * hg + 96 * i:384 * hg + 96 * i + 96]) if q == 0 else \
                    (lambda i: kf[:, 96 * i:96 * i + 96])
                tk = P.tr([(bank[0:96, 128 * i:128 * i + 128], src(i)) for i in range(4)], r, bf)
                e = P.act((QT2, KT2)[q][:, :, 128 * t:128 * t + 128],
                          bank[0:96, :].rearrange("p (i n) -> p i n", i=4), ACT.Copy, tk, ph,
                          scale=(scale, 1.0)[q])
                P.banks.give(b, e)
        ready = P.now()
        mark(P, 'mla prep')
        ob2 = {}

        def att2(t, i):
            if i == 0:
                ob2[t] = P.banks.take()
            ob = ob2[t]
            k = 4 * (t % 2) + i
            ei, eb, x = softmax_rows(P, R, [(QT2[:, i, 128 * t:128 * t + 128], KT2[:, i, :])], 512, None,
                                     SUM[:, k:k + 1], SUM[:, 16 + k:17 + k], ready)
            yield
            c0 = 128 * (4 * hg + i) + 64
            for tk in turn_and_apply(P, R, ev, ei, eb, x, 512, lambda j: UKV[:, j, c0:c0 + 64],
                                     ob[1][:, 64 * i:64 * i + 64], ob[2], i == 0, 64):
                if tk is None:
                    yield
            ob2[t] = ob[0:3] + (tk,)

        def fin2(t):
            yield
            yield
            yield
            ob = ob2[t]
            r = SUM[:, 4 * (t % 2):4 * (t % 2) + 4]
            P.rec(r, r, ob[3], P.C.last())
            c0 = 512 + 256 * hg
            e = P.tt(MIX[:, t, c0:c0 + 256].rearrange("p (h d) -> p h d", h=4),
                     ob[1][:, 0:256].rearrange("p (h d) -> p h d", h=4), bc(r, 2, 64), MUL)
            P.banks.give(ob[0], e)

        def units2():
            for t in range(4):
                for i in range(4):
                    yield att2(t, i)
                yield fin2(t)
        run_lagged(units2())
    return MIX


def odd_mixer(P):
    A = P.A
    ev = Evac(P)
    o = P.L0
    ph = P.now()
    hd = transpose_x(P, lambda t: P.X[:, t, :], 0, deps=ph, lo=o + 12288, ready=ph)
    QKV = P.m(o, 12288).rearrange("p (t n) -> p t n", t=4)
    ro = o + 12288
    hik, lok = block(halves(P, P.HTo)), block(halves(P, o + 12288))
    run_dense(P, [Job("tok", 512, hik, lok,
                      (lambda t, ps, tk, c=c: ev(QKV[:, t, 512 * c:512 * c + 512], ps, tk, ph)), acc=[])
                  for c in range(6)], hd)
    ready = P.now()
    mark(P, 'proj')
    R = Rings(P, ro, ready)
    w0 = ro + Rings.SIZE
    TB = Ring([P.m(w0 + 896 * i, 896) for i in range(2)], ready)
    QK = Ring([P.m(P.HTo + 1024 * i, 1024) for i in range(3)], ready)
    SUM = P.m(P.HTo + 3072, 128)
    rel = A["rel"]
    rsem = [P.sem("rel") for _ in range(2)]
    qkt, tbt = {}, {}

    def load_bias(h):
        i, tb, f = TB.take()
        P.Y.dma(rsem[i], lambda e: e.dma_start(tb[0:64, :], rel[h, :, 1:15, :].rearrange("c j n -> c (j n)")), f, ready)
        tk = P.Y.dma(rsem[i], lambda e: e.dma_start(tb[64:128, :], rel[h, :, 0:14, :].rearrange("c j n -> c (j n)")), f)
        tbt[h] = (i, tb, tk)

    def prep(hp):
        qi, qb, qf = QK.take()
        toks = []
        for q in range(2):
            b, bank, bf = P.banks.take()
            tk = P.tr([(bank[:, 128 * t:128 * t + 128],
                        QKV[:, t, 1024 * q + 128 * hp:1024 * q + 128 * hp + 128]) for t in range(4)], ready, bf)
            e = P.act(qb[:, 512 * q:512 * q + 512], bank[:, :], ACT.Copy, tk, qf, scale=(0.125, 1.0)[q], chain=False)
            P.banks.give(b, e)
            toks.append(e)
        qkt[hp] = (qi, qb, toks)
        yield

    load_bias(0)

    def units():
        yield prep(0)
        for hp in range(8):
            if hp < 7:
                yield prep(hp + 1)
            for hh in range(2):
                if 2 * hp + hh + 1 < 16:
                    load_bias(2 * hp + hh + 1)
                st = {}
                for t in range(4):
                    yield att(hp, hh, t, st)
                yield fin(hp, hh, st)

    def att(hp, hh, t, st):
        h = 2 * hp + hh
        if t == 0:
            st["o"] = P.banks.take()
        ob = st["o"]
        qi, qb, qtok = qkt[hp]
        ti, tb, ttok = tbt[h]
        rows = slice(64 * hh, 64 * hh + 64)
        k = 4 * (h % 2) + t
        s0 = 64 * (6 - 2 * t)
        ei, eb, x = softmax_rows(P, R, [(qb[rows, 128 * t:128 * t + 128], qb[rows, 512:1024])], 512,
                                 (tb[:, s0:s0 + 512], ttok), SUM[:, k:k + 1], SUM[:, 16 + k:17 + k], qtok)
        if t == 3:
            TB.give(ti, x)
            if hh == 1:
                QK.give(qi, x)
        yield
        for tk in turn_and_apply(P, R, ev, ei, eb, x, 512, lambda j: QKV[:, j, 2048 + 64 * h:2048 + 64 * h + 64],
                                 ob[1][:, 64 * t:64 * t + 64], ob[2], t == 0, 64):
            if tk is None:
                yield
        st["tk"] = tk

    def fin(hp, hh, st):
        h = 2 * hp + hh
        yield
        yield
        yield
        r = SUM[:, 4 * (h % 2):4 * (h % 2) + 4]
        P.rec(r, r, st["tk"], P.C.last())
        ob = st["o"]
        e = P.tt(QKV[:, :, 64 * h:64 * h + 64], ob[1][:, 0:256].rearrange("p (t d) -> p t d", t=4),
                 bc(r, 2, 64), MUL)
        P.banks.give(ob[0], e)

    run_lagged(units())
    return QKV


def experts(P, l):
    A = P.A
    o = P.L0
    ph = P.now()
    hd = transpose_x(P, lambda t: P.X[:, t, :], 0, deps=ph, ready=ph)
    xs = P.sem("xd")
    for t in range(4):
        xd = P.Y.dma(xs, (lambda t: lambda e: e.dma_start(P.xd[128 * t:128 * t + 128, :], P.X[:, t, :]))(t), ph)
    ini = P.load([(P.tab[l][:, :], A["c_big"])])
    wr = P.m(o, 288).rearrange("p (k n) -> p k n", k=8)
    rb = P.m(o + 288, 36)
    ei = P.m(o + 324, 32)
    wl = P.load([(wr[:, :, 0:4], A["w_router_group_2"][l].rearrange("(k p) n -> p k n", p=128)),
                 (wr[:, :, 4:36], A["w_router_expert_2"][l].rearrange("(k p) n -> p k n", p=128)),
                 (rb[:, 0:4], A["b_router_group_2"][l].partition_broadcast(128)),
                 (rb[:, 4:36], A["b_router_expert_2"][l].partition_broadcast(128)),
                 (ei, A["c_eio"])], ph)
    b, bank, bf = P.banks.take()

    def fn(e):
        for t in range(4):
            for k in range(8):
                r = e.matmul(bank[:, 36 * t:36 * t + 36], P.HT[:, k, 128 * t:128 * t + 128], wr[:, k, :],
                             start=(k == 0), stop=(k == 7))
        return r
    tk = P.T(fn, hd, wl, bf)
    lg = P.m(o + 400, 144).rearrange("p (t n) -> p t n", t=4)
    e = P.tt(lg, bank[:, 0:144].rearrange("p (t n) -> p t n", t=4), bc(rb, 1, 4), ADD, tk, ph)
    P.banks.give(b, e)
    gp = P.m(o + 544, 8)
    m8 = P.m(o + 552, 8)
    ex = P.m(o + 560, 8)
    goh = P.m(o + 568, 4)
    oh = P.m(o + 600, 128 * 2).rearrange("p (k t n) -> p k t n", k=2, t=4)
    ml = P.m(o + 860, 64)
    gt = P.m(P.HTo + 3900, 8).rearrange("p (t k) -> p t k", t=4)
    idf = P.m(o + 924, 8)
    sc1 = P.m(o + 940, 8)
    i8 = P.memu[:, 128:136]
    P.V(lambda e: e.memset(gp, -3e38), hd)
    for t in range(4):
        P.copy(gp[:, 0:4], lg[:, t, 0:4])
        P.V(lambda e: e.max(m8, gp))
        P.V(lambda e: e.max_index(i8, m8, gp))
        P.copy(idf, i8)
        P.ts(goh, ei[:, 0:4], idf[:, 0:1], None, ALU.is_equal)
        nm = P.ts(sc1[:, 0:1], m8[:, 0:1], -1.0, None, MUL)
        x = P.act(ex[:, 0:4], lg[:, t, 0:4], ACT.Exp, nm, bias=sc1[:, 0:1], accum_out=sc1[:, 1:2])
        mv = ml[:, 0:32].rearrange("p (g n) -> p g n", g=4)
        P.tt(mv, lg[:, t, 4:36].rearrange("p (g n) -> p g n", g=4), bc(goh, 2, 8), MUL)
        P.ts(goh, goh, 1.0, 1e30, SUB, MUL)
        P.tt(mv, mv, bc(goh, 2, 8), ADD)
        P.V(lambda e: e.max(m8, ml[:, 0:32]))
        P.V(lambda e: e.max_index(i8, m8, ml[:, 0:32]))
        P.copy(idf, i8)
        for k in range(2):
            P.ts(oh[:, k, t, :], ei, idf[:, k:k + 1], None, ALU.is_equal)
        y = P.tt(sc1[:, 2:3], m8[:, 1:2], m8[:, 0:1], SUB)
        y = P.act(sc1[:, 3:4], sc1[:, 2:3], ACT.Exp, y)
        P.ts(sc1[:, 4:5], sc1[:, 3:4], 1.0, None, ADD, None, y, x)
        P.tt(sc1[:, 4:5], sc1[:, 4:5], sc1[:, 1:2], MUL)
        P.rec(gt[:, t, 0:1], sc1[:, 4:5])
        P.tt(gt[:, t, 1:2], gt[:, t, 0:1], sc1[:, 3:4], MUL)
    ohs = P.m(o + 1000, 128).rearrange("p (t n) -> p t n", t=4)
    r = P.tt(ohs, oh[:, 0], oh[:, 1], ADD)
    b, bank, bf = P.banks.take()

    def fn(e):
        for t in range(4):
            for j in range(t + 1):
                r = e.matmul(bank[:, 32 * t:32 * t + 32], P.ustr if j == t else P.ones, ohs[:, j, :],
                             start=(j == 0), stop=(j == t))
        for j in range(4):
            r = e.matmul(bank[:, 128:160], P.ones, ohs[:, j, :], start=(j == 0), stop=(j == 3))
        return r
    tk = P.T(fn, r, bf)
    rk = P.m(o + 1130, 160)
    e = P.copy(rk, bank[:, 0:160], tk)
    P.banks.give(b, e)
    P.ts(rk[:, 0:128], rk[:, 0:128], 32.0, None, MUL)
    P.tt(rk[:, 0:128].rearrange("p (t n) -> p t n", t=4), rk[:, 0:128].rearrange("p (t n) -> p t n", t=4),
         bc(ei, 1, 4), ADD)
    du = P.memu[:, 136:144]
    tu = P.memu[:, 144:152]
    for k in range(2):
        P.tt(oh[:, k], oh[:, k], rk[:, 0:128].rearrange("p (t n) -> p t n", t=4), MUL)
        P.red(idf.rearrange("p (t k) -> p t k", t=4)[:, :, k], oh[:, k], ADD)
    P.copy(tu, P.tokid)
    d = P.copy(du, idf)
    cnt = P.memu[0:1, 152:153]
    mc = P.m(o + 1290, 1)
    P.red(mc, rk[:, 128:160], MAX)
    P.copy(P.memu[:, 64:96], rk[:, 128:160])
    P.cnt_ready = P.copy(P.memu[:, 152:153], mc)
    ss = P.sem("scat")
    for t in range(4):
        for k in range(2):
            i = 2 * t + k
            sct = P.G.dma(ss, (lambda i: lambda e: e.indirect_dma_start(
                P.tab[l].rearrange("r (e u) -> (r e) u", u=1), bass.IndirectOffsetOnAxis(du[:, i:i + 1], 0),
                tu[:, i:i + 1], None))(i), d, ini)
    IDX = P.memu[:, 0:64].rearrange("p (a e) -> p a e", a=2)
    il = P.load([(IDX[0:CAP, 0, :], P.tab[l][0:CAP, :])], sct, P.now())
    hx = P.V(lambda e: e.tensor_single_scalar(IDX[0:CAP, 1, :], IDX[0:CAP, 0, :], 1, ALU.logical_shift_right), il)

    mark(P, 'router')
    o1 = o + 1300
    XG = Ring([P.m(o1 + 1024 * i, 1024) for i in range(2)])
    XT = Ring([P.m(o1 + 2048 + 8 * CAP * i, 8 * CAP) for i in range(2)])
    HD = Ring([P.m(o1 + 4096 + 512 * i, 512) for i in range(2)])
    SG = Ring([P.m(o1 + 5120 + 512 * i, 512) for i in range(2)])
    YY = Ring([P.m(o1 + 6144 + 1024 * i, 1024) for i in range(2)])
    xtra = [P.spare]
    P.wissue(P.spare, (ph,))
    e0 = o1 + 8192
    while e0 + 4096 <= P.total:
        xtra.append(e0)
        P.wissue(e0, (ph,))
        e0 += 4096
    gsem = [P.sem("gx") for _ in range(2)]
    ysem = [P.sem("ys") for _ in range(2)]
    z = [P.V((lambda b_: lambda e: e.memset(b_, 0.0))(b_), ph) for b_ in XG.bufs]
    ev = Evac(P)
    gath = {}
    ytok = []

    def gather(e_):
        gi, gb, gf = XG.take()
        tk = P.G.dma(gsem[gi], lambda e: e.indirect_dma_start(
            gb[0:CAP, :], None, P.xd[:, :], bass.IndirectOffsetOnAxis(IDX[0:CAP, 1, e_:e_ + 1], 0),
            bounds_check=S - 1, oob_is_err=False), gf, hx, xd, z)
        gath[e_] = (gi, gb, tk)

    def turn(e_):
        gi, gb, gtk = gath[e_]
        xi, xb, xf = XT.take()
        xv = xb.rearrange("p (k n) -> p k n", k=8)
        cs = []
        for half in range(2):
            b, bank, bf = P.banks.take()
            v = bank[:, 0:4 * CAP].rearrange("p (k n) -> p k n", k=4)
            tk = P.tr([(v[:, k, :], gb[0:CAP, 128 * (4 * half + k):128 * (4 * half + k) + 128]) for k in range(4)],
                      gtk, bf)
            c = ev(xv[:, 4 * half:4 * half + 4, :], v, tk, xf)
            P.banks.give(b, c)
            cs.append(c)
        XG.give(gi, tk)
        return xi, xv, cs

    gather(0)
    gather(1)
    nxt = turn(0)
    ngive = P.wnext + 0

    def up(e_, cur):
        xi, xv, cs = cur
        outs = []
        for _ in range(2):
            slot, buf, wt = P.wtake()
            w = buf.rearrange("p (k n) -> p k n", k=8)
            b, bank, bf = P.banks.take()

            def fn(e, bank=bank, w=w):
                for c in range(4):
                    for k in range(8):
                        r = e.matmul(bank[:, CAP * c:CAP * c + CAP], w[:, k, 128 * c:128 * c + 128], xv[:, k, :],
                                     start=(k == 0), stop=(k == 7))
                return r
            tk = P.T(fn, wt, bf, cs)
            give(slot, tk)
            outs.append((b, bank, tk))
        XT.give(xi, tk)
        (b0, g_, t0), (b1, u_, t1) = outs
        si, sb, sf = SG.take()
        n = 4 * CAP
        x = P.act(sb[:, 0:n], g_[:, 0:n], ACT.Exp, t0, sf, scale=-1.0, chain=False)
        P.ts(sb[:, 0:n], sb[:, 0:n], 1.0, None, ADD, None, x)
        P.rec(sb[:, 0:n], sb[:, 0:n])
        x = P.tt(sb[:, 0:n], sb[:, 0:n], g_[:, 0:n], MUL)
        P.banks.give(b0, x)
        hi, hb, hf = HD.take()
        x = P.tt(hb[:, 0:n], sb[:, 0:n], u_[:, 0:n], MUL, t1, hf)
        P.banks.give(b1, x)
        SG.give(si, x)
        return hi, hb, x

    def down(e_, hi, hb, x):
        slot, buf, wt = P.wtake()
        w = buf.rearrange("p (k n) -> p k n", k=4)
        yi, yb, yf = YY.take()
        es = []
        for n in range(2):
            b, bank, bf = P.banks.take()
            tk = P.mm(bank[0:CAP, :], [(hb[:, CAP * k:CAP * k + CAP], w[:, k, 512 * n:512 * n + 512]) for k in range(4)],
                      wt, bf, x)
            c = ev(yb[0:CAP, 512 * n:512 * n + 512], bank[0:CAP, :], tk, yf)
            P.banks.give(b, c)
            es.append(c)
        give(slot, tk)
        HD.give(hi, tk)
        y = P.G.dma(ysem[yi], lambda e: e.indirect_dma_start(
            P.yd[:, :], bass.IndirectOffsetOnAxis(IDX[0:CAP, 0, e_:e_ + 1], 0), yb[0:CAP, :], None,
            bounds_check=2 * S - 1, oob_is_err=False), es)
        YY.give(yi, y)
        ytok.append(y)

    def give(slot, tk):
        P.wgive(slot, tk, keep=slot not in xtra or P.wnext < P.wuse_end)

    P.wuse_end = P.wuse + 3 * NE
    for e_ in range(NE):
        cur = nxt
        hdn = up(e_, cur)
        if e_ + 1 < NE:
            nxt = turn(e_ + 1)
        if e_ + 2 < NE:
            gather(e_ + 2)
        down(e_, *hdn)
    mark(P, 'experts')
    for q in (P.T, P.V, P.C, P.G, P.Y):
        q.wait(P.now(), ytok[-2:])
    overflow(P, l, IDX, xtra, XG.bufs[0], P.m(o1 + 2048, 1024), HD.bufs[0], SG.bufs[0], YY.bufs[0])
    ph = P.now()
    P.pieces.free = [ph] * 4
    YB = P.m(o, 8192).rearrange("p (t k n) -> p t k n", t=4, k=2)
    P.idle_extra = None
    yl = P.load([(YB[:, t], P.yd[256 * t:256 * t + 256, :].rearrange("(p k) n -> p k n", k=2)) for t in range(4)],
                ytok, ph)
    alpha = 4 ** 0.25
    for t in range(4):
        x = P.X[:, t, :]
        P.ts(x, x, alpha, None, MUL, None, yl, ph)
        for k in range(2):
            P.stt(x, YB[:, t, k, :], gt[:, t, k:k + 1], x, MUL, ADD)


def overflow(P, l, IDX, xtra, XGb, XTb, HDb, SGb, YYb):
    nc, A = P.nc, P.A
    nc.all_engine_barrier()
    for q in (P.T, P.V, P.C, P.G, P.Y):
        q.wait(P.cnt_ready)
    nc.all_engine_barrier()
    most = nc.values_load(P.memu[0:1, 152:153], min_val=0, max_val=512)
    with nc.If(most > CAP):
        with nc.Fori(0, NE) as e_:
            have = nc.values_load(P.memu[0:1, 64:64 + NE][:, bass.ds(e_, 1)], min_val=0, max_val=512)
            with nc.If(have > CAP):
                with nc.Fori(0, NBLK) as r_:
                    with nc.If(have > r_ * 128 + CAP):
                        overflow_block(P, l, e_, r_, xtra, XGb, XTb, HDb, SGb, YYb)
    nc.all_engine_barrier()


def overflow_block(P, l, e_, r_, slots, XGb, XTb, HDb, SGb, YYb):
    nc, A = P.nc, P.A
    T, V, C, G, Y = nc.tensor, nc.vector, nc.scalar, nc.gpsimd, nc.sync
    s = P.osem
    wg, wu, wd = (P.m(x, 4096) for x in slots[0:3])
    oi, ox = P.memu[:, 153:154], P.memu[:, 154:155]
    nc.all_engine_barrier()
    Y.dma_start(oi, P.tab[l][bass.ds(r_ * 128 + CAP, 128), bass.ds(e_, 1)],
                allow_slow_non_contiguous=True).then_inc(s["idx"], 16)
    for buf, name, k in ((wg, "w_gate_2", 8), (wu, "w_up_2", 8), (wd, "w_down_2", 4)):
        Y.dma_start(buf.rearrange("p (k n) -> p k n", k=k),
                    A[name][l][bass.ds(e_, 1)].rearrange("o (k p) n -> p (o k) n", p=128)).then_inc(s["w"], 16)
    V.wait_ge(s["idx"], 16)
    V.tensor_single_scalar(ox, oi, 1, ALU.logical_shift_right).then_inc(s["row"], 1)
    V.memset(XGb, 0.0).then_inc(s["row"], 1)
    G.wait_ge(s["row"], 2)
    G.indirect_dma_start(XGb, None, P.xd[:, :], bass.IndirectOffsetOnAxis(ox, 0),
                         bounds_check=S - 1, oob_is_err=False).then_inc(s["gath"], 16)
    T.wait_ge(s["gath"], 16)
    T.wait_ge(s["w"], 48)
    xv = XTb.rearrange("p (k n) -> p k n", k=8)
    bk = [b for b in P.banks.bufs[0:6]]
    for half in range(2):
        for k in range(4):
            t = T.transpose(bk[half][:, 128 * k:128 * k + 128],
                            XGb[:, 128 * (4 * half + k):128 * (4 * half + k) + 128], P.ident)
        t.then_inc(s["turn"], 1)
    for half in range(2):
        V.wait_ge(s["turn"], half + 1)
        V.tensor_copy(xv[:, 4 * half:4 * half + 4, :],
                      bk[half][:, :].rearrange("p (k n) -> p k n", k=4)).then_inc(s["xt"], 1)
    T.wait_ge(s["xt"], 2)
    for buf, bank in ((wg, bk[2]), (wu, bk[3])):
        w = buf.rearrange("p (k n) -> p k n", k=8)
        for c in range(4):
            for k in range(8):
                t = T.matmul(bank[:, 128 * c:128 * c + 128], w[:, k, 128 * c:128 * c + 128], xv[:, k, :],
                             start=(k == 0), stop=(k == 7))
        t.then_inc(s["up"], 1)
    C.wait_ge(s["up"], 1)
    C.activation(SGb, bk[2][:, :], ACT.Exp, scale=-1.0).then_inc(s["sig"], 1)
    V.wait_ge(s["sig"], 1)
    V.tensor_scalar(SGb, SGb, 1.0, None, ADD).then_inc(s["v"], 1)
    V.wait_ge(s["v"], 1)
    V.reciprocal(SGb, SGb).then_inc(s["v"], 1)
    V.wait_ge(s["v"], 2)
    V.tensor_tensor(SGb, SGb, bk[2][:, :], MUL).then_inc(s["v"], 1)
    V.wait_ge(s["v"], 3)
    V.wait_ge(s["up"], 2)
    V.tensor_tensor(HDb, SGb, bk[3][:, :], MUL).then_inc(s["v"], 1)
    T.wait_ge(s["v"], 4)
    w = wd.rearrange("p (k n) -> p k n", k=4)
    for n in range(2):
        for k in range(4):
            t = T.matmul(bk[4 + n][:, :], HDb[:, 128 * k:128 * k + 128], w[:, k, 512 * n:512 * n + 512],
                         start=(k == 0), stop=(k == 3))
        t.then_inc(s["down"], 1)
    for n in range(2):
        V.wait_ge(s["down"], n + 1)
        V.tensor_copy(YYb[:, 512 * n:512 * n + 512], bk[4 + n][:, :]).then_inc(s["y"], 1)
    G.wait_ge(s["y"], 2)
    G.indirect_dma_start(P.yd[:, :], bass.IndirectOffsetOnAxis(oi, 0), YYb, None,
                         bounds_check=2 * S - 1, oob_is_err=False).then_inc(s["out"], 16)
    G.wait_ge(s["out"], 16)
    nc.all_engine_barrier()
    ids = sorted(h.num for h in s.values())
    assert ids == list(range(ids[0], ids[0] + len(ids)))
    G.dma_reset(range(ids[0], ids[0] + len(ids)))
    G.sem_clear(range(ids[0], ids[0] + len(ids)))
    nc.all_engine_barrier()


def finish(P):
    s = P.sem("out")
    ph = P.now()
    for t in range(4):
        tk = P.Y.dma(s, (lambda t: lambda e: e.dma_start(P.out[0, 128 * t:128 * t + 128, :], P.X[:, t, :]))(t), ph)
    P.Y.wait(tk)


_INS = ['x', 'norm1_g', 'w_in', 'hgrn_lb_logits', 'hgrn_onorm_g', 'nsa_qn_g', 'nsa_kn_g', 'nsa_cmp_pos', 'nsa_cmp_w1',
        'nsa_cmp_w2', 'fox_qn_g', 'fox_kn_g', 'fox_fb', 'w_o', 'norm2_g', 'w_up', 'w_down', 'even_w_in_2',
        'even_lam_q1_2', 'even_lam_k1_2', 'even_lam_q2_2', 'even_lam_k2_2', 'even_subln_g_2', 'even_q_norm_g_2',
        'even_w_uq_2', 'even_kv_norm_g_2', 'even_w_ukv_2', 'even_w_o_2', 'odd_w_qkv_2',
        'odd_w_o_2', 'ln1_g_2', 'ln1_b_2', 'ln2_g_2', 'ln2_b_2', 'w_router_group_2', 'b_router_group_2',
        'w_router_expert_2', 'b_router_expert_2', 'w_gate_2', 'w_up_2', 'w_down_2']


def kernel(**inputs):
    import numpy as np
    import concourse.bacc as bacc
    from concourse.bass_utils import run_bass_kernel_spmd

    nc = bacc.Bacc("TRN2", target_bir_lowering=False, num_devices=1)
    data = {n: np.ascontiguousarray(inputs[n]) for n in _INS}
    data.update(constants())
    for n in ("norm1_g", "norm2_g"):
        data[n] = np.ascontiguousarray(data[n].reshape(2, 8, 128).transpose(0, 2, 1))
    data["hgrn_lb_logits"] = np.ascontiguousarray(data["hgrn_lb_logits"].reshape(2, 2, 128).transpose(2, 1, 0).reshape(128, 4))
    rb = np.asarray(inputs["odd_rel_bias_2"])[0]
    rel = np.full((16, 64, 15, 64), NEG, np.float32)
    for c in range(64):
        c0 = min(max(c - 8, 0), 48)
        rel[:, c, :, c0:c0 + 16] = rb[:, :, c0 - c + 15:c0 - c + 31]
    data["rel"] = rel
    arrays, A = {}, {}
    for n, a in data.items():
        arrays[f"in_{n}"] = a
        A[n] = nc.dram_tensor(f"in_{n}", a.shape, mybir.dt.from_np(a.dtype), kind="ExternalInput").ap()
    out = nc.dram_tensor("out_0", (1, S, D), F32, kind="ExternalOutput").ap()
    scr = {"xd": nc.dram_tensor("xd", (S, D), F32, kind="Internal").ap(),
           "yd": nc.dram_tensor("yd", (2 * S, D), F32, kind="Internal").ap(),
           "tab": [nc.dram_tensor(f"tab{i}", (ROWS, NE), U32, kind="Internal").ap() for i in range(2)]}
    Program.xd, Program.yd, Program.tab = scr["xd"], scr["yd"], scr["tab"]
    build(nc, A, out)
    r = run_bass_kernel_spmd(nc, [arrays], core_ids=[0])
    return r.results[0]["out_0"]
```

```python
import math
from contextlib import ExitStack

import concourse.bass as bass
from concourse import mybir

F32 = mybir.dt.float32
F32R = mybir.dt.float32r
U32 = mybir.dt.uint32
ALU = mybir.AluOpType
ACT = mybir.ActivationFunctionType
AX = mybir.AxisListType

ADD, SUB, MUL, MAX, MIN = ALU.add, ALU.subtract, ALU.mult, ALU.max, ALU.min
NEG = -1e30
TINY = 1e-30
S, D = 512, 1024
CAP = 128
NBLK = (S - CAP + 127) // 128
ROWS = CAP + 128 * NBLK
NE = 32
BIG = 1 << 20

OFF = {}
_o = 0
for _n, _w in (("ident", 128), ("mask", 512), ("utri", 128), ("ustr", 128), ("ones", 128), ("hm", 1024),
               ("rope", 64), ("ropec", 16), ("cmadd", 128), ("cmmul", 128), ("tokid", 8)):
    OFF[_n] = (_o, _w)
    _o += _w
NCONST = _o


def constants():
    import numpy as np
    c = np.zeros((128, NCONST), np.float32)

    def at(name):
        o, w = OFF[name]
        return c[:, o:o + w]

    p = np.arange(128)
    at("ident")[:] = np.eye(128)
    at("mask")[:] = np.where(np.arange(512)[None, :] - 384 <= p[:, None], 0.0, NEG)
    at("utri")[:] = (p[:, None] <= p[None, :])
    at("ustr")[:] = (p[:, None] < p[None, :])
    at("ones")[:] = 1.0
    hm = at("hm").reshape(128, 8, 128)
    hm[:, 0] = np.eye(128)
    for i in range(7):
        L = 1 << i
        s, t = p[:, None], p[None, :]
        hm[:, 1 + i] = (s // (2 * L) == t // (2 * L)) & (s // L % 2 == 0) & (t // L % 2 == 1)
    c[:, OFF["hm"][0]:OFF["hm"][0] + 1024] = hm.reshape(128, 1024)
    inv = np.float32(500000.0) ** (-np.arange(0, 16, 2, dtype=np.float32) / np.float32(16))
    ang = np.arange(S, dtype=np.float32)[:, None] * inv[None, :].astype(np.float32)
    r = np.stack([np.cos(ang), np.sin(ang)], 1).reshape(4, 128, 16).transpose(1, 0, 2)
    c[:, OFF["rope"][0]:OFF["rope"][0] + 64] = r.reshape(128, 64)
    end = np.arange(31) * 16 + 31
    angc = end.astype(np.float32)[:, None] * inv[None, :]
    c[:31, OFF["ropec"][0]:OFF["ropec"][0] + 16] = np.concatenate([np.cos(angc), np.sin(angc)], 1)
    ok = np.zeros((128, 4, 32), bool)
    for t in range(4):
        ok[:, t, :31] = end[None, :] <= (128 * t + p)[:, None]
    c[:, OFF["cmadd"][0]:OFF["cmadd"][0] + 128] = np.where(ok, 0, NEG).reshape(128, 128)
    c[:, OFF["cmmul"][0]:OFF["cmmul"][0] + 128] = ok.reshape(128, 128)
    tok = 2 * (128 * np.arange(4)[None, :, None] + p[:, None, None]) + np.arange(2)[None, None, :]
    c[:, OFF["tokid"][0]:OFF["tokid"][0] + 8] = tok.reshape(128, 8)
    inv2 = np.float32(500000.0) ** (-np.arange(0, 32, 2, dtype=np.float32) / np.float32(32))
    ang2 = np.arange(S, dtype=np.float32)[:, None] * inv2[None, :]
    r2 = np.stack([np.cos(ang2), np.sin(ang2)], 1).reshape(4, 128, 32).transpose(1, 0, 2)
    return {"c_main": c, "c_rope2": np.ascontiguousarray(r2.reshape(128, 128).astype(np.float32)),
            "c_eio": np.tile(np.arange(32, dtype=np.float32)[None, :], (128, 1)),
            "c_big": np.full((ROWS, NE), BIG, np.uint32)}


class Sem:

    def __init__(self, handle):
        self.h, self.n = handle, 0

    def add(self, k):
        self.n += k
        return (self, self.n)


class Queue:

    def __init__(self, prog, name, chained):
        self.prog, self.name, self.chained = prog, name, chained
        self.sem = prog.sem("q_" + name)
        self.eng = {"pe": prog.nc.tensor, "dve": prog.nc.vector, "act": prog.nc.scalar,
                    "pool": prog.nc.gpsimd, "sp": prog.nc.sync}[name]
        self.seen = {}

    def wait(self, *deps):
        for sem, value in flat(deps):
            if self.seen.get(sem, 0) < value:
                self.seen[sem] = value
                self.eng.wait_ge(sem.h, value)

    def __call__(self, fn, *deps, chain=None):
        chain = self.chained if chain is None else chain
        self.wait(deps, self.last() if chain else ())
        tok = self.sem.add(1)
        fn(self.eng).then_inc(self.sem.h, 1)
        return tok

    def last(self):
        return (self.sem, self.sem.n)

    def dma(self, sem, fn, *deps):
        self.wait(deps)
        tok = sem.add(16)
        fn(self.eng).then_inc(sem.h, 16)
        return tok


def flat(x):
    if isinstance(x, tuple) and len(x) == 2 and isinstance(x[0], Sem):
        if x[1] > 0:
            yield x
        return
    for y in x:
        if y is not None:
            yield from flat(y)


class Ring:

    def __init__(self, bufs, free=()):
        self.bufs = bufs
        self.free = [free for _ in bufs]
        self.held = [False] * len(bufs)
        self.at = 0

    def take(self):
        for _ in self.bufs:
            i = self.at
            self.at = (self.at + 1) % len(self.bufs)
            if not self.held[i]:
                self.held[i] = True
                return i, self.bufs[i], self.free[i]
        raise RuntimeError("all held")

    def give(self, i, *toks):
        self.held[i] = False
        self.free[i] = toks


LAG = 2


def run_lagged(units, step=None):
    live = []
    units = iter(units)
    more = True
    while more or live:
        if more:
            try:
                live.append([next(units), 0])
            except StopIteration:
                more = False
        if step is not None:
            step()
        nxt = []
        for g in live:
            g[1] += 1
            if (g[1] - 1) % LAG:
                nxt.append(g)
                continue
            try:
                next(g[0])
                nxt.append(g)
            except StopIteration:
                pass
        live = nxt


class Program:
    def __init__(self, nc, ctx, A, out):
        self.nc, self.ctx, self.A, self.out = nc, ctx, A, out
        self.nsem = 0
        self.T = Queue(self, "pe", False)
        self.V = Queue(self, "dve", True)
        self.C = Queue(self, "act", True)
        self.G = Queue(self, "pool", True)
        self.Y = Queue(self, "sp", False)
        self.total = 52900
        at = (nc.sbuf_base + 31) // 32 * 32
        ctx.enter_context(nc.sbuf_tensor("arena", [128, self.total], F32))
        self.mem = nc.alloc_sbuf_tensor_at("mem", [128, self.total], F32, offset=at)
        self.at, self.rounded = at, {}
        self.memu = ctx.enter_context(nc.sbuf_tensor("memu", [128, 160], U32))
        self.banks = Ring([ctx.enter_context(nc.psum_tensor(f"ps{i}", [128, 512], F32)) for i in range(8)])
        self.osem = {n: ctx.enter_context(nc.semaphore("over_" + n)) for n in
                     ("idx", "w", "row", "gath", "turn", "xt", "up", "sig", "v", "down", "y", "out")}
        self.top = 0
        self.aside = None

    def sem(self, name):
        self.nsem += 1
        return Sem(self.ctx.enter_context(self.nc.semaphore(f"{name}_{self.nsem}")))

    def m(self, off, n, parts=128, p0=0):
        assert off + n <= self.total, (off, n)
        return self.mem[p0:p0 + parts, off:off + n]

    def step_aside(self):
        if self.aside is None:
            return
        wait, gen = self.aside
        if wait > 0:
            self.aside = (wait - 1, gen)
            return
        try:
            next(gen)
        except StopIteration:
            self.aside = None

    def finish_aside(self):
        while self.aside is not None:
            self.step_aside()

    def r(self, off, n):
        assert off + n <= self.total and n <= 4096, (off, n)
        if (off, n) not in self.rounded:
            self.rounded[off, n] = self.nc.alloc_sbuf_tensor_at(f"r{off}_{n}", [128, n], F32R,
                                                                offset=self.at + 4 * off)
        return self.rounded[off, n][:, :]

    def alloc(self, n):
        o = self.top
        self.top += n
        assert self.top <= self.total, self.top
        return o

    def now(self):
        return (self.T.last(), self.V.last(), self.C.last(), self.G.last())

    def mm(self, out, pairs, *deps, start=True, stop=True, skip=False):
        def fn(e):
            n = len(pairs)
            for i, (a, b) in enumerate(pairs):
                r = e.matmul(out, a, b, start=(start and i == 0), stop=(stop and i == n - 1),
                             skip_group_check=skip)
            return r
        return self.T(fn, *deps)

    def tr(self, items, *deps):
        ident = self.ident

        def fn(e):
            for o, i in items:
                k = i.shape[0]
                r = e.transpose(o, i, ident[0:k, 0:k])
            return r
        return self.T(fn, *deps)

    def tt(self, out, a, b, op, *deps, q=None, **kw):
        return (q or self.V)(lambda e: e.tensor_tensor(out, a, b, op), *deps, **kw)

    def ts(self, out, a, s1, s2, op0, op1=None, *deps, q=None, **kw):
        if op1 is None:
            return (q or self.V)(lambda e: e.tensor_scalar(out, a, s1, None, op0), *deps, **kw)
        return (q or self.V)(lambda e: e.tensor_scalar(out, a, s1, s2, op0, op1), *deps, **kw)

    def stt(self, out, a, s, b, op0, op1, *deps, **kw):
        return self.V(lambda e: e.scalar_tensor_tensor(out, a, s, b, op0, op1), *deps, **kw)

    def act(self, out, a, f, *deps, chain=None, **kw):
        return self.C(lambda e: e.activation(out, a, f, **kw), *deps, chain=chain)

    def red(self, out, a, op, *deps, negate=False, chain=None):
        return self.V(lambda e: e.tensor_reduce(out, a, AX.X, op, negate=negate), *deps, chain=chain)

    def rec(self, out, a, *deps):
        return self.V(lambda e: e.reciprocal(out, a), *deps)

    def rsqrt(self, x, scale, eps, *deps):
        a = self.ts(x, x, scale, eps, MUL, ADD, *deps)
        a = self.act(x, x, ACT.Sqrt, a)
        return self.rec(x, x, a)

    def copy(self, out, a, *deps, **kw):
        return self.V(lambda e: e.tensor_copy(out, a), *deps, **kw)

    def load(self, pairs, *deps, q=None, name="ld"):
        q = q or self.Y
        s = self.sem(name)
        for o, i in pairs:
            tok = q.dma(s, (lambda o, i: lambda e: e.dma_start(o, i))(o, i), *deps)
        return tok

    def wstart(self, chunks, slots):
        self.chunks, self.wnext, self.wuse = chunks, 0, 0
        self.wsem = {}
        self.wready = {}
        for s in slots:
            self.wissue(s, ())

    def wissue(self, slot, deps):
        if self.wnext >= len(self.chunks):
            return
        i = self.wnext
        self.wnext += 1
        if slot not in self.wsem:
            self.wsem[slot] = self.sem("w")
        for fn in self.chunks[i](self.m(slot, 4096)):
            tok = self.Y.dma(self.wsem[slot], fn, *deps)
        self.wready[i] = (slot, tok)

    def wtake(self):
        slot, tok = self.wready[self.wuse]
        self.wuse += 1
        return slot, self.m(slot, 4096), tok

    def wgive(self, slot, *deps, keep=True):
        if keep:
            self.wissue(slot, deps)


def dram_chunk(src, k, cols, parts=128):
    c0, n = cols

    def make(buf):
        dst = buf[0:parts, 0:k * n].rearrange("p (k n) -> p k n", k=k)
        s = src[:, c0:c0 + n].rearrange("(k p) n -> p k n", p=parts)
        return [lambda e: e.dma_start(dst, s)]
    return make


def bc(ap, axis, n):
    a = ap.unsqueeze(axis)
    sh = list(a.shape)
    sh[axis] = n
    return a.broadcast_to(sh)


def weight_chunks(A):
    out = []
    for l in range(2):
        w = A["w_in"][l]
        for c in (1024, 1536, 2048, 2560, 3072, 512, 0):
            out.append(dram_chunk(w, 8, (c, min(512, 3100 - c))))
        for which in range(2):
            out.append(dram_chunk(A["nsa_cmp_w1"][l, which], 32, (0, 128), parts=64))
        for n in range(2):
            out.append(dram_chunk(A["w_o"][l], 8, (512 * n, 512)))
        for half in range(2):
            for c in range(4 * half, 4 * half + 4):
                out.append(dram_chunk(A["w_up"][l], 8, (512 * c, 512)))
            for n in range(2):
                for kq in range(2 * half, 2 * half + 2):
                    out.append(dram_chunk(A["w_down"][l, 1024 * kq:1024 * kq + 1024, :], 8, (512 * n, 512)))
    w = A["even_w_in_2"][0]
    for c in range(0, 1952, 512):
        out.append(dram_chunk(w, 8, (c, min(512, 1952 - c))))

    def mla(buf):
        a = buf[:, 0:1536].rearrange("p (k n) -> p k n", k=2)
        return [lambda e: e.dma_start(a, A["even_w_uq_2"][0].rearrange("(k p) n -> p k n", p=128)),
                lambda e: e.dma_start(buf[:, 1536:2560], A["even_w_ukv_2"][0])]
    out.append(mla)
    for n in range(2):
        out.append(dram_chunk(A["even_w_o_2"][0], 8, (512 * n, 512)))
    moe(A, out, 0)
    for c in range(6):
        out.append(dram_chunk(A["odd_w_qkv_2"][0], 8, (512 * c, 512)))
    for n in range(2):
        out.append(dram_chunk(A["odd_w_o_2"][0], 8, (512 * n, 512)))
    moe(A, out, 1)
    return out


def moe(A, out, l):
    for e in range(NE):
        out.append(dram_chunk(A["w_gate_2"][l, e], 8, (0, 512)))
        out.append(dram_chunk(A["w_up_2"][l, e], 8, (0, 512)))
        out.append(dram_chunk(A["w_down_2"][l, e], 4, (0, 1024)))


def build(nc, A, out):
    ctx = ExitStack()
    with ctx:
        P = Program(nc, ctx, A, out)
        setup(P)
        for l in range(2):
            first_layer(P, l)
        for l in range(2):
            second_layer(P, l)
        finish(P)


def setup(P):
    A = P.A
    P.X = P.m(P.alloc(4096), 4096).rearrange("p (t n) -> p t n", t=4)
    P.HTo = P.alloc(4096)
    P.HT = P.m(P.HTo, 4096).rearrange("p (k n) -> p k n", k=8)
    P.slots = [P.alloc(4096) for _ in range(3)]
    P.spare = P.alloc(4096)
    P.pieces = Ring([P.spare + 1024 * i for i in range(4)])
    co = P.alloc(NCONST)

    def const(name):
        o, w = OFF[name]
        return P.m(co + o, w)
    P.ident = const("ident")
    P.cmask, P.utri, P.ustr, P.ones = const("mask"), const("utri"), const("ustr"), const("ones")
    P.hm = const("hm").rearrange("p (l n) -> p l n", l=8)
    P.rope = const("rope").rearrange("p (t n) -> p t n", t=4)
    P.ropec = const("ropec")
    P.cmadd = const("cmadd").rearrange("p (t n) -> p t n", t=4)
    P.cmmul = const("cmmul").rearrange("p (t n) -> p t n", t=4)
    P.tokid = const("tokid")
    sm = P.alloc(1120)
    P.g = []
    n = 0

    def take(w):
        nonlocal n
        n += w
        return P.m(sm + n - w, w)
    pairs = [(P.m(co, NCONST), A["c_main"])]
    P.lg = take(4).rearrange("p (j l) -> p j l", j=2)
    pairs.append((P.lg.rearrange("p j l -> p (j l)"), A["hgrn_lb_logits"]))
    for l in range(2):
        g = {}
        g["g1"], g["g2"] = take(8), take(8)
        pairs.append((g["g1"], A["norm1_g"][l]))
        pairs.append((g["g2"], A["norm2_g"][l]))
        for nm in ("hgrn_onorm_g", "nsa_qn_g", "nsa_kn_g", "fox_qn_g", "fox_kn_g"):
            g[nm] = take(64)
            pairs.append((g[nm], A[nm][l].partition_broadcast(128)))
        g["fb"] = take(4)
        pairs.append((g["fb"], A["fox_fb"][l].partition_broadcast(128)))
        P.g.append(g)
    P.small = take(160)
    P.lbw = take(24)
    P.eps = take(4)
    assert n <= 1120
    xs = P.sem("x")
    for t in range(4):
        P.xload = P.Y.dma(xs, (lambda t: lambda e: e.dma_start(P.X[:, t, :], A["x"][0, 128 * t:128 * t + 128, :]))(t))
    P.cload = P.load(pairs)
    P.wstart(weight_chunks(A), P.slots)
    P.V(lambda e: e.memset(P.eps[:, 0:1], 0.0))
    P.L0 = P.top
    P.jA = P.m(P.L0, 0 + 512)
    P.V.wait(P.cload, P.xload)
    P.C.wait(P.cload, P.xload, P.V.last())
    P.T.wait(P.cload, P.xload)
    P.G.wait(P.cload, P.xload)
    w = P.lbw[:, 0:4].rearrange("p (j l) -> p j l", j=2)
    mx = P.lbw[:, 4:6]
    P.red(mx, P.lg, MAX)
    t = P.tt(w, P.lg, bc(mx, 2, 2), SUB)
    t = P.act(w, w, ACT.Exp, t)
    P.red(mx, w, ADD, t)
    P.rec(mx, mx)
    P.tt(w, w, bc(mx, 2, 2), MUL)
    P.lb = P.lbw[:, 8:12].rearrange("p (l j) -> p l j", l=2)
    P.tt(P.lb[:, 0, :], w[:, :, 0], w[:, :, 0], SUB)
    P.tt(P.lb[:, 1, :], w[:, :, 0], w[:, :, 1], ADD)
    P.tt(P.lb[:, 1, :], P.lb[:, 1, :], w[:, :, 0], SUB)
    P.olb = P.lbw[:, 12:16].rearrange("p (l j) -> p l j", l=2)
    P.ts(P.olb, P.lb, -1.0, 1.0, MUL, ADD)


def halves(P, off):
    return [P.r(off + 2048 * i, 2048).rearrange("p (k n) -> p k n", k=4) for i in range(2)]


def block(hs):
    return lambda kk: hs[kk // 4][:, kk % 4, :]


def transpose_x(P, src_of, scratch, norm=None, deps=(), lo=None, ready=()):
    done = []
    ring = Ring([P.m(scratch + 1024 * i, 1024) for i in range(2)], deps)
    tmp = Ring([P.m(scratch + 2048 + 512 * i, 512) for i in range(2)], deps)
    if lo is not None:
        hr, lr = halves(P, P.HTo), halves(P, lo)
    if norm is not None:
        x_done = P.V.last()
        for t in range(4):
            sq = P.act(ring.bufs[t % 2], P.X[:, t, :], ACT.Square, deps, x_done, accum_out=P.small[:, t:t + 1])
        scaled = P.rsqrt(P.small[:, 0:4], 1.0 / D, 1e-6, sq)
        ring.free = [(deps, sq)] * 2
    for t in range(4):
        if norm is not None:
            i, xn, fr = ring.take()
            src = xn
            rd = P.act(xn, P.X[:, t, :], ACT.Copy, scaled, fr, scale=P.small[:, t:t + 1], chain=False)
        else:
            src, rd = src_of(t), ready
        for half in range(2):
            b, bank, bf = P.banks.take()
            v = bank[:, :].rearrange("p (k n) -> p k n", k=4)
            tk = P.tr([(v[:, k, :], src[:, 128 * (4 * half + k):128 * (4 * half + k) + 128]) for k in range(4)],
                      rd, bf)
            at = (slice(None), slice(4 * half, 4 * half + 4), slice(128 * t, 128 * t + 128))
            if lo is None:
                e = P.copy(P.HT[at], v, tk, deps, chain=False)
                P.banks.give(b, e)
                done.append(e)
                continue
            x = v
            if norm is not None:
                j, tb, tf = tmp.take()
                x = tb.rearrange("p (k n) -> p k n", k=4)
                e = P.tt(x, v, bc(norm[:, 4 * half:4 * half + 4], 2, 128), MUL, tk, tf, deps, chain=False)
                P.banks.give(b, e)
                tk2 = e
            else:
                tk2 = tk
            cut = (slice(None), slice(None), slice(128 * t, 128 * t + 128))
            h = P.act(hr[half][cut], x, ACT.Copy, tk2, deps, chain=False)
            e = P.tt(lr[half][cut], x, hr[half].bitcast(F32)[cut], SUB, tk2, h, deps, chain=False)
            if norm is not None:
                tmp.give(j, e)
            else:
                P.banks.give(b, e)
            done += [e, h]
        if norm is not None:
            ring.give(i, tk)
    return done


class Job:

    def __init__(self, mode, n, hi, lo, evac, acc=None, first=True, last=True, k=8):
        self.mode, self.n, self.hi, self.lo, self.evac = mode, n, hi, lo, evac
        self.acc, self.first, self.last, self.k = acc, first, last, k


def run_dense(P, jobs, ready):
    plan = [(job, kk) for job in jobs for kk in range(job.k)]
    made = []
    held = {}

    def make(i):
        job, kk = plan[i]
        if kk == 0:
            held["w"] = P.wtake()
        slot, buf, wt = held["w"]
        n = job.n
        w = buf[:, kk * n:kk * n + n]
        pi, po, pf = P.pieces.take()
        hi, lo = P.r(po, 512)[:, 0:n], P.r(po + 512, 512)[:, 0:n]
        hf = hi.bitcast(F32)
        h = P.act(hi, w, ACT.Copy, wt, pf, chain=False)
        e = P.tt(lo, w, hf, SUB, wt, pf, h, chain=False)
        if kk == job.k - 1:
            P.wgive(slot, h, e)
        made.append((pi, hi, lo, h, e))

    depth = len(P.pieces.bufs)
    for i in range(min(depth - 1, len(plan))):
        make(i)
    for i, (job, kk) in enumerate(plan):
        if i + depth - 1 < len(plan):
            make(i + depth - 1)
        if kk == 0 and job.first:
            job.acc[:] = [P.banks.take() for _ in range(4)]
        pi, wh, wl, h, e = made[i]
        xh, xl = job.hi(kk), job.lo(kk)
        n = job.n

        def fn(eng):
            for j in range(4):
                c = slice(128 * j, 128 * j + 128)
                if job.mode == "tok":
                    o = job.acc[j][1][:, 0:n]
                    pairs = ((xh[:, c], wh), (xh[:, c], wl), (xl[:, c], wh))
                else:
                    o = job.acc[j][1][:, :]
                    pairs = ((wh[:, c], xh), (wh[:, c], xl), (wl[:, c], xh))
                for m, (a, b) in enumerate(pairs):
                    r = eng.matmul(o, a, b, start=(job.first and kk == 0 and m == 0),
                                   stop=(job.last and kk == job.k - 1 and m == 2))
            return r
        tk = P.T(fn, h, e, ready, [a[2] for a in job.acc] if kk == 0 and job.first else ())
        P.pieces.give(pi, tk)
        for _ in range(3 if P.aside is not None and P.aside[0] == 0 else 1):
            P.step_aside()
        if kk == job.k - 1 and job.last:
            for j in range(4):
                ev = job.evac(j, job.acc[j][1][:, 0:n], tk)
                P.banks.give(job.acc[j][0], ev)
    return tk


class Evac:

    def __init__(self, P):
        self.P, self.n = P, 0

    def __call__(self, out, a, *deps):
        self.n += 1
        if self.n % 2:
            return self.P.act(out, a, ACT.Copy, *deps, chain=False)
        return self.P.copy(out, a, *deps, chain=False)


def run(gen):
    for r in gen:
        pass
    return r


def head_norm(P, *a):
    return run(head_norm_steps(P, *a))


def head_norm_steps(P, x, n, d, gain, scratch, *deps):
    np_ = x.shape[0]
    sq = scratch[0:np_, 0:n * d].rearrange("p (n d) -> p n d", n=n)
    ss = P.small[0:np_, 16:16 + n]
    yield P.act(sq, x, ACT.Square, P.V.last(), *deps)
    P.red(ss, sq, ADD, P.C.last(), *deps)
    yield P.ts(ss, ss, 1.0 / d, 1e-6, MUL, ADD)
    P.act(ss, ss, ACT.Sqrt, P.V.last())
    yield P.rec(ss, ss, P.C.last())
    yield P.tt(x, x, bc(ss, 2, d), MUL)
    yield P.tt(x, x, bc(gain[0:np_], 1, n), MUL)


def rope(P, *a):
    return run(rope_steps(P, *a))


def rope_steps(P, x, n, half, cs, scratch, *deps):
    p = x.shape[0]
    a = scratch[0:p, 0:n * half].rearrange("p (n d) -> p n d", n=n)
    b = scratch[0:p, n * half:2 * n * half].rearrange("p (n d) -> p n d", n=n)
    c = scratch[0:p, 2 * n * half:3 * n * half].rearrange("p (n d) -> p n d", n=n)
    cos, sin = bc(cs[0:p, 0:half], 1, n), bc(cs[0:p, half:2 * half], 1, n)
    x1, x2 = x[:, :, 0:half], x[:, :, half:2 * half]
    P.tt(a, x1, cos, MUL, P.C.last(), *deps)
    P.tt(b, x2, sin, MUL)
    yield P.tt(c, x1, sin, MUL)
    P.tt(x1, a, b, SUB)
    P.tt(a, x2, cos, MUL)
    yield P.tt(x2, a, c, ADD)


def attention_norms(P, l, PJ, sc, pjt):
    g = P.g[l]
    for t in range(4):
        q = PJ[:, t, 512:1024].rearrange("p (n d) -> p n d", n=8)
        yield from head_norm_steps(P, q, 8, 64, g["nsa_qn_g"], sc, list(pjt))
        yield from rope_steps(P, q, 8, 8, P.rope[:, t, :], sc)
    for t in range(4):
        for c in (1280, 1536):
            k = PJ[:, t, c:c + 128].rearrange("p (n d) -> p n d", n=2)
            yield from head_norm_steps(P, k, 2, 64, g["nsa_kn_g"], sc, list(pjt))
            yield from rope_steps(P, k, 2, 8, P.rope[:, t, :], sc)
    for t in range(4):
        for c, gn in ((1816, "fox_qn_g"), (2072, "fox_kn_g")):
            yield from head_norm_steps(P, PJ[:, t, c:c + 256].rearrange("p (n d) -> p n d", n=4), 4, 64, g[gn], sc,
                                       list(pjt))


def mark(P, name):
    pass


class Rings:
    def __init__(self, P, o, deps):
        def ring(n):
            nonlocal o
            r = Ring([P.m(o + 512 * i, 512) for i in range(n)], deps)
            o += 512 * n
            return r
        self.S, self.E, self.T, self.M = ring(3), ring(4), ring(3), ring(2)
        self.sc = 0

    SIZE = 12 * 512


def softmax_rows(P, R, qk, nk, mask, sums, negm, ready):
    b, bank, bf = P.banks.take()
    s = bank[:, 0:nk]
    tk = P.mm(s, qk, bf, ready)
    ei, eb, ef = R.E.take()
    if mask is not None:
        m, mdeps = mask
        si, sb, sf = R.S.take()
        v = P.V(lambda e: e.tensor_tensor_reduce(sb[:, 0:nk], s, m, -1.0, 3e38, ADD, MIN, negm), tk, sf, mdeps,
                chain=False)
        P.banks.give(b, v)
        x = P.act(eb[:, 0:nk], sb[:, 0:nk], ACT.Exp, v, ef, bias=negm, scale=-1.0, accum_out=sums, chain=False)
        R.S.give(si, x)
    else:
        v = P.red(negm, s, MAX, tk, negate=True, chain=False)
        x = P.act(eb[:, 0:nk], s, ACT.Exp, v, ef, bias=negm, accum_out=sums, chain=False)
        P.banks.give(b, x)
    return ei, eb, x


def turn_and_apply(P, R, ev, ei, eb, x, nk, vf, out, odeps, start, dv):
    n = nk // 128
    b, bank, bf = P.banks.take()
    tk = P.tr([(bank[:, 128 * i:128 * i + 128], eb[:, 128 * i:128 * i + 128]) for i in range(n)], x, bf)
    R.E.give(ei, tk)
    ti, tb, tf = R.T.take()
    c = ev(tb[:, 0:nk], bank[:, 0:nk], tk, tf)
    P.banks.give(b, c)
    yield None
    tk = P.mm(out, [(tb[:, 128 * i:128 * i + 128], vf(i)) for i in range(n)], c, odeps, start=start, skip=True)
    R.T.give(ti, tk)
    yield tk


def first_layer(P, l):
    A, g = P.A, P.g[l]
    ev = Evac(P)
    base = P.L0
    PJo = base
    PJ = P.m(PJo, 4 * 2588).rearrange("p (t n) -> p t n", t=4)
    MIXo = PJo + 4 * 2588
    MIX = P.m(MIXo, 4096).rearrange("p (t n) -> p t n", t=4)
    W = MIXo + 4096
    ph = P.now()
    hdone = transpose_x(P, None, W, norm=g["g1"], deps=ph, lo=MIXo)
    xn_done = P.now()

    hg = [P.m(W + 1024 * i, 1024).rearrange("p (j n) -> p j n", j=2) for i in range(6)]
    Qf, Kf, Ff, Sf, T1, Kt = hg
    hik, lok = block(halves(P, P.HTo)), block(halves(P, MIXo))

    def gates(j, ps, tk):
        if j < 2:
            return P.act(Qf[:, j, :], ps, ACT.Copy, tk, xn_done, scale=0.125)
        jj = j - 2
        a = P.act(T1[:, jj, :], ps, ACT.Exp, tk, xn_done, scale=-1.0)
        c = P.act(Kf[:, jj, :], ps, ACT.Exp)
        P.ts(T1[:, jj, :], T1[:, jj, :], 1.0, None, ADD, None, a, xn_done)
        P.rec(T1[:, jj, :], T1[:, jj, :])
        P.ts(Ff[:, jj, :], T1[:, jj, :], P.olb[:, l, jj:jj + 1], P.lb[:, l, jj:jj + 1], MUL, ADD)
        P.ts(Ff[:, jj, :], Ff[:, jj, :], TINY, None, MAX)
        P.ts(Kf[:, jj, :], Kf[:, jj, :], 1.0, None, ADD, None, c)
        P.rec(Kf[:, jj, :], Kf[:, jj, :])
        P.ts(Kf[:, jj, :], Kf[:, jj, :], P.olb[:, l, jj:jj + 1], None, MUL)
        return c
    pjt = []

    def to_pj(c0, n):
        def evac(t, o, tk):
            r = ev(PJ[:, t, c0:c0 + n], o, tk, ph)
            pjt.append(r)
            return r
        return evac
    jobs = []
    for c0 in (512, 1024, 1536, 2048, 2560, 0):
        n = min(512, 2588 - c0)
        jobs.append(Job("tok", n, hik, lok, to_pj(c0, n), acc=[]))
    jobs.append(Job("feat", 512, hik, lok, gates, acc=[]))
    P.aside = (14, attention_norms(P, l, PJ, P.m(W + 6144, 1024), pjt))
    run_dense(P, jobs, hdone)
    P.finish_aside()
    N = NsaPrep(P, l, PJ, W)
    P.aside = (0, N.run())
    mark(P, 'proj')
    hgrn(P, l, PJ, MIX, hg, pjt, W)
    P.finish_aside()
    nsa(P, l, PJ, MIX, W, N)
    fox(P, l, PJ, MIX, W)

    add = lambda t, n, o, tk: P.tt(P.X[:, t, 512 * n:512 * n + 512], P.X[:, t, 512 * n:512 * n + 512], o, ADD, tk,
                                   chain=False)
    mix_out(P, MIX, add, base)
    ph = P.now()
    hlo = base + 16384
    hdone = transpose_x(P, None, hlo + 4096, norm=g["g2"], deps=ph, lo=hlo)
    ah = [P.r(base + 512 * i, 512) for i in range(16)]
    al = [P.r(base + 8192 + 512 * i, 512) for i in range(16)]
    R2 = Ring([P.m(hlo + 4096 + 512 * i, 512) for i in range(4)], P.now())
    read = ()
    for half in range(2):
        at = []

        def relu2(c):
            def evac(j, ps, tk):
                ri, rb, rf = R2.take()
                a = P.act(rb, ps, ACT.Relu, tk, rf, chain=False)
                s = P.tt(rb, rb, rb, MUL, a, chain=False)
                h = P.act(ah[4 * c + j], rb, ACT.Copy, s, read, ph, chain=False)
                e = P.tt(al[4 * c + j], rb, ah[4 * c + j].bitcast(F32), SUB, h, s, read, ph, chain=False)
                R2.give(ri, e)
                at.extend((h, e))
                return a
            return evac
        run_dense(P, [Job("feat", 512, hik, block(halves(P, hlo)), relu2(c), acc=[])
                      for c in range(4)], hdone)
        jobs = []
        for n in range(2):
            acc = []
            for kq in range(2):
                jobs.append(Job("tok", 512, (lambda kk, kq=kq: ah[8 * kq + kk]),
                                (lambda kk, kq=kq: al[8 * kq + kk]),
                                (lambda t, o, tk, n=n: add(t, n, o, tk)), acc=acc, first=kq == 0, last=kq == 1))
        read = run_dense(P, jobs, at)


def mix_out(P, MIX, evac, lo):
    ph = P.now()
    done = transpose_x(P, lambda t: MIX[:, t, :], 0, deps=ph, lo=lo, ready=ph)
    run_dense(P, [Job("tok", 512, block(halves(P, P.HTo)), block(halves(P, lo)),
                      (lambda t, o, tk, n=n: evac(t, n, o, tk)), acc=[]) for n in range(2)], done)


def hgrn(P, l, PJ, MIX, hg, pjt, W):
    g = P.g[l]
    Qf, Kf, Pf, Sf = hg[0:4]
    pairs = (hg[4:6], [P.m(P.L0 + 4 * 2588 + 1024 * i, 1024).rearrange("p (j n) -> p j n", j=2) for i in range(2)])
    flat_ = lambda a: a.rearrange("p j n -> p (j n)")
    P.V(lambda e: e.memset(flat_(Sf), 1.0))
    acc = [P.banks.take() for _ in range(2)]
    first = [True, True]
    scratch_o = W + 6 * 1024
    AR = Ring([P.m(scratch_o + 512 * i, 512) for i in range(3)], P.now())
    WS = [P.m(P.L0 + 4 * 2588 + 2048 + 512 * i, 512) for i in range(4)]
    ws_free = P.now()
    summed = [(), (), (), ()]

    def pv(h, items, c):
        b, bank, bf = acc[h // 2]
        st = first[h // 2]

        def fn(e, st=st):
            for i, (a, s, t) in enumerate(items):
                o = bank[:, (h % 2) * 256 + 64 * t:(h % 2) * 256 + 64 * t + 64]
                r = e.matmul(o, a, PJ[:, s, 64 * h:64 * h + 64], start=(st and i == 0), stop=True,
                             skip_group_check=True)
            return r
        first[h // 2] = False
        return P.T(fn, c, bf, pjt)

    def unit(q, k, h, lev, qk_ready):
        rows = slice(64 * (h % 2), 64 * (h % 2) + 64)
        j = h // 2
        b, bank, bf = P.banks.take()
        ai, ab, af = AR.take()
        if lev < 8:
            def fn(e):
                for t in range(4):
                    s = slice(128 * t, 128 * t + 128)
                    r = e.matmul(bank[:, s], k[rows, j, s], q[rows, j, s], start=True, stop=True)
                return r
            tk = P.T(fn, qk_ready, bf)
            units_read.append(tk)
            v4 = bank[:, :].rearrange("p (t n) -> p t n", t=4)
            w = WS[h] if lev == 0 else ab
            c = P.tt(w.rearrange("p (t n) -> p t n", t=4), v4, bc(P.hm[:, lev, :], 1, 4), MUL, tk, af, ws_free,
                     chain=False)
            P.banks.give(b, c)
            if lev:
                yield
                c = P.tt(WS[h], WS[h], ab, ADD, c, summed[h], chain=False)
            AR.give(ai, c)
            summed[h] = c
            if lev == 7:
                yield
                pv(h, [(WS[h][:, 128 * t:128 * t + 128], t, t) for t in range(4)], c)
            return
        elif lev == 8:
            def fn(e):
                for i, (s, t) in enumerate(((0, 1), (2, 3))):
                    r = e.matmul(bank[:, 128 * i:128 * i + 128], k[rows, j, 128 * s:128 * s + 128],
                                 q[rows, j, 128 * t:128 * t + 128], start=True, stop=True)
                return r
            tk = P.T(fn, qk_ready, bf)
            units_read.append(tk)
            c = P.act(ab[:, 0:256], bank[:, 0:256], ACT.Copy, tk, af, chain=False)
            items = [(ab[:, 0:128], 0, 1), (ab[:, 128:256], 2, 3)]
        else:
            def fn(e):
                for s in range(2):
                    r = e.matmul(bank[:, 256 * s:256 * s + 256], k[rows, j, 128 * s:128 * s + 128],
                                 q[rows, j, 256:512], start=True, stop=True)
                return r
            tk = P.T(fn, qk_ready, bf)
            units_read.append(tk)
            c = P.act(ab, bank[:, :], ACT.Copy, tk, af, chain=False)
            items = [(ab[:, 256 * s + 128 * t:256 * s + 128 * t + 128], s, 2 + t) for s in range(2) for t in range(2)]
        P.banks.give(b, c)
        yield
        tk = pv(h, items, c)
        AR.give(ai, tk)

    units_read = []

    def all_units():
        ready = pair_free = P.now()
        def products(lev):
            L = 1 << (lev - 1)
            Qt, Kt = pairs[lev % 2]
            rd = list(units_read)[0:4 * (lev - 1)]
            P.tt(flat_(Qt), flat_(Qf), flat_(Pf), MUL, rd, pair_free)
            kq = P.tt(flat_(Kt), flat_(Kf), flat_(Sf), MUL)
            if lev < 9:
                pv_ = flat_(Pf).rearrange("p (n two l) -> p n two l", two=2, l=L)
                sv_ = flat_(Sf).rearrange("p (n two l) -> p n two l", two=2, l=L)
                nb = 1024 // (2 * L)
                right = pv_[:, :, 1, L - 1:L].broadcast_to([128, nb, L])
                left = pv_[:, :, 0, L - 1:L].broadcast_to([128, nb, L])
                P.tt(sv_[:, :, 0, :], sv_[:, :, 0, :], right, MUL)
                P.tt(pv_[:, :, 1, :], pv_[:, :, 1, :], left, MUL)
            return kq
        for lev in range(10):
            Qt, Kt = pairs[lev % 2] if lev else (Qf, Kf)
            q = kq if lev else ready
            for h in range(4):
                yield unit(Qt, Kt, h, lev, q)
                if h == (1 if lev else 0) and lev < 9:
                    kq = products(lev + 1)
    run_lagged(all_units(), P.step_aside)

    mark(P, 'hgrn levels')
    O = P.m(W, 1024)
    ph = P.now()
    for b in range(2):
        e = P.copy(O[:, 512 * b:512 * b + 512], acc[b][1][:, :], ph)
        P.banks.give(acc[b][0], e)
    head_norm(P, O.rearrange("p (n d) -> p n d", n=16), 16, 64, g["hgrn_onorm_g"], P.m(W + 1024, 1024))
    Ov = O.rearrange("p (h t d) -> p h t d", h=4, t=4)
    G = P.m(W + 2048, 1024).rearrange("p (t n) -> p t n", t=4)
    x = P.act(G, PJ[:, :, 256:512], ACT.Exp, ph, pjt, scale=-1.0)
    P.ts(G, G, 1.0, None, ADD, None, x)
    P.rec(G, G)
    P.tt(G, G, PJ[:, :, 256:512], MUL)
    for t in range(4):
        P.tt(MIX[:, t, 0:256].rearrange("p (h d) -> p h d", h=4), Ov[:, :, t, :],
             G[:, t, :].rearrange("p (h d) -> p h d", h=4), MUL)


class NsaPrep:

    def __init__(self, P, l, PJ, W):
        self.P, self.l, self.PJ, self.W = P, l, PJ, W

    def run(self):
        P, l, PJ, W = self.P, self.l, self.PJ, self.W
        g = P.g[l]
        ph = P.now()
        QT = self.QT = P.m(W + 7680, 2048).rearrange("p (i n) -> p i n", i=4)
        KT = self.KT = P.m(P.HTo, 1024).rearrange("p (i n) -> p i n", i=2)
        TG = P.m(P.HTo + 1024, 1024, parts=64).rearrange("p (g n) -> p g n", g=2)
        qcs = Ring([P.m(W + 9728, 512)], ph)
        for t in range(4):
            qq = PJ[:, t, 512:1024].rearrange("p (g i d) -> p i g d", g=2, i=4)
            qi, qc, qf = qcs.take()
            c = P.copy(qc.rearrange("p (i g d) -> p i g d", i=4, g=2), qq, qf, ph)
            yield
            b, bank, bf = P.banks.take()
            v = bank[:, :].rearrange("p (i n) -> p i n", i=4)
            tk = P.tr([(v[:, i, :], qc[:, 128 * i:128 * i + 128]) for i in range(4)], c, bf)
            qcs.give(qi, tk)
            e = P.act(QT[:, :, 128 * t:128 * t + 128], v, ACT.Copy, tk, ph, scale=0.125)
            P.banks.give(b, e)
            yield
        for t in range(4):
            b2, bank2, bf2 = P.banks.take()
            tk = P.tr([(bank2[:, 128 * i:128 * i + 128], PJ[:, t, c_:c_ + 128]) for i, c_ in enumerate((1280, 1536))],
                      ph, bf2)
            e = P.act(KT[:, :, 128 * t:128 * t + 128],
                      bank2[:, 0:256].rearrange("p (i n) -> p i n", i=2), ACT.Copy, tk, ph)
            P.banks.give(b2, e)
            yield
        gs = self.gs = P.m(P.HTo + 2048, 96).rearrange("p (t n) -> p t n", t=4)
        x = P.act(gs, PJ[:, :, 1792:1816], ACT.Exp, ph, scale=-1.0)
        P.ts(gs, gs, 1.0, None, ADD, None, x)
        gr = self.gr = P.rec(gs, gs)

        H0 = P.HTo + 2144
        w2 = P.m(H0, 128).rearrange("p (w n) -> p w n", w=2)
        pos = P.m(H0 + 128, 64, parts=64).rearrange("p (w n) -> p w n", w=2)
        cw = P.load([(w2, P.A["nsa_cmp_w2"][l].rearrange("w k n -> k w n"))], ph)
        prl = [P.load([(P.m(H0 + 192 + 1408 * which, 64, parts=32), P.A["nsa_cmp_pos"][l, which])], ph) for which in range(2)]
        hid = P.m(H0 + 256, 64)
        u2 = P.m(H0 + 320, 64)
        kc = P.m(H0 + 384, 128)
        KC = self.KC = P.m(H0 + 512, 32)
        VB = self.VB = [P.m(H0 + 544 + 256 * i, 256) for i in range(2)]
        zz = P.V(lambda e: e.memset(P.m(H0 + 256, 800), 0.0), ph)
        sc2 = P.m(H0 + 1056, 256)
        posb = P.m(H0 + 1312, 1)
        for which in range(2):
            pl = prl[which]
            pr = P.m(H0 + 192 + 1408 * which, 64, parts=32)
            b, bank, bf = P.banks.take()
            tk = P.tr([(bank[0:64, 0:32], pr)], pl, bf)
            e = P.copy(pos[:, which, :], bank[0:64, 0:32], tk)
            P.banks.give(b, e)
            for gg in range(2):
                b, bank, bf = P.banks.take()
                c = 1024 + 128 * which + 64 * gg
                tk = P.tr([(bank[0:64, 128 * t:128 * t + 128], PJ[:, t, c:c + 64]) for t in range(4)], bf, P.V.last())
                tg = P.copy(TG[:, gg, :], bank[0:64, :], tk, P.T.last())
                P.banks.give(b, tg)
                yield
                yield
            slot, buf, wt = P.wtake()
            w1 = buf[0:64, :].rearrange("p (l n) -> p l n", l=32)
            b, bank, bf = P.banks.take()
            ho = bank[:, 0:62].rearrange("p (g n) -> p g n", g=2)
            tk = P.mm(ho, [(w1[:, i, :], TG[:, :, i:i + 16 * 30 + 1:16]) for i in range(32)], wt, tg, bf)
            b2, bank2, bf2 = P.banks.take()
            tk2 = P.mm(bank2[:, 0:1], [(w1[:, i, :], pos[:, which, i:i + 1]) for i in range(32)], e, bf2)
            P.wgive(slot, tk2)
            yield
            yield
            pb = P.copy(posb, bank2[:, 0:1], tk2, zz)
            P.banks.give(b2, pb)
            hv = hid.rearrange("p (g n) -> p g n", g=2)
            P.V(lambda e: e.memset(hid, 0.0), P.now())
            x = P.ts(hv[:, :, 0:31], ho, posb, None, ADD, None, tk, P.T.last())
            P.banks.give(b, x)
            P.tt(u2, hid, hid, MUL)
            P.ts(u2, u2, 0.044715, 1.0, MUL, ADD)
            x = P.tt(u2, u2, hid, MUL)
            yield
            x = P.act(u2, u2, ACT.Tanh, x, scale=math.sqrt(2.0 / math.pi))
            P.ts(u2, u2, 1.0, 0.5, ADD, MUL, x)
            yield
            h = P.tt(hid, u2, hid, MUL)
            yield
            yield
            if which == 0:
                b, bank, bf = P.banks.take()

                def fn(e, bank=bank):
                    for gg in range(2):
                        r = e.matmul(bank[0:31, 64 * gg:64 * gg + 64], hv[:, gg, 0:31], w2[:, 0, :], start=True, stop=True)
                    return r
                tk = P.T(fn, h, bf, cw)
                e = P.copy(kc[0:31, :], bank[0:31, 0:128], tk)
                P.banks.give(b, e)
                yield
                kv = kc[0:31, :].rearrange("p (g d) -> p g d", g=2)
                sq = sc2[0:31, 0:128].rearrange("p (n d) -> p n d", n=2)
                ss = P.small[0:31, 16:18]
                P.tt(sq, kv, kv, MUL)
                P.red(ss, sq, ADD)
                P.rsqrt(ss, 1.0 / 64, 1e-6)
                P.tt(kv, kv, bc(ss, 2, 64), MUL)
                P.tt(kv, kv, bc(g["nsa_kn_g"][0:31, :], 1, 2), MUL)
                yield
                r = rope(P, kv, 2, 8, P.ropec, sc2)
                yield
                yield
                b, bank, bf = P.banks.take()
                tk = P.tr([(bank[:, 0:31], kc[0:31, :])], r, bf)
                e = P.copy(KC[:, 0:31], bank[:, 0:31], tk)
                P.banks.give(b, e)
            else:
                hr = P.m(H0 + 1344, 256).rearrange("p (g i n) -> p g i n", g=2, i=4)
                r = P.copy(hr, bc(hv, 2, 4), P.now())
                yield
                yield
                b, bank, bf = P.banks.take()

                def fn(e, bank=bank):
                    for gg in range(2):
                        r = e.matmul(bank[:, 64 * gg:64 * gg + 64], hr[:, gg].rearrange("p i n -> p (i n)"), w2[:, 1, :],
                                     start=True, stop=True)
                    return r
                tk = P.T(fn, r, bf, cw)
                for gg in range(2):
                    for i in range(4):
                        e = P.copy(VB[gg][32 * i:32 * i + 32, 64 * i:64 * i + 64],
                                   bank[32 * i:32 * i + 32, 64 * gg:64 * gg + 64], tk)
                P.banks.give(b, e)


def nsa(P, l, PJ, MIX, W, N):
    ev = Evac(P)
    QT, KT, KC, VB, gs, gr = N.QT, N.KT, N.KC, N.VB, N.gs, N.gr
    cready = qkr = ph = P.now()
    R = Rings(P, W, ph)

    SUM = P.m(P.HTo + 2144 + 1664, 192)
    TMP = P.m(W + 9728, 512)

    def units():
        for t in range(4):
            st = {}
            yield cmp_unit(t, st)
            for kind in range(2):
                yield from (att(t, kind, i, st) for i in range(8))
            yield fin(t, st)

    def cmp_unit(t, st):
        ei, eb, ef = R.E.take()
        s = eb[:, 0:256].rearrange("p (h n) -> p h n", h=8)
        mx = SUM[:, 0:8]
        v31 = s[:, :, 0:31]
        P.V(lambda e: e.memset(eb[:, 0:256], 0.0), ef)
        for gg in range(2):
            b, bank, bf = P.banks.take()
            v = bank[:, 0:128].rearrange("p (h n) -> p h n", h=4)

            def fn(e):
                for h in range(4):
                    rows = slice(64 * gg, 64 * gg + 64)
                    r = e.matmul(v[:, h, 0:31], QT[rows, h, 128 * t:128 * t + 128], KC[rows, 0:31],
                                 start=True, stop=True)
                return r
            tk = P.T(fn, bf, cready)
            e = P.tt(s[:, 4 * gg:4 * gg + 4, 0:31], v[:, :, 0:31], bc(P.cmadd[:, t, 0:31], 1, 4), ADD, tk)
            P.banks.give(b, e)
        P.red(mx, v31, MAX)
        x = P.tt(v31, v31, bc(mx, 2, 31), SUB)
        x = P.act(v31, v31, ACT.Exp, x)
        P.tt(v31, v31, bc(P.cmmul[:, t, 0:31], 1, 8), MUL, x)
        P.red(mx, v31, ADD)
        P.ts(mx, mx, TINY, None, MAX)
        P.rec(mx, mx)
        x = P.tt(v31, v31, bc(mx, 2, 31), MUL)
        yield
        b, bank, bf = P.banks.take()
        tk = P.tr([(bank[:, 128 * i:128 * i + 128], eb[:, 128 * i:128 * i + 128]) for i in range(2)], x, bf)
        R.E.give(ei, tk)
        ti, tb, tf = R.T.take()
        c = ev(tb[:, 0:256], bank[:, 0:256], tk, tf)
        P.banks.give(b, c)
        yield
        b, bank, bf = P.banks.take()

        def fn(e):
            for gg in range(2):
                r = e.matmul(bank[:, 256 * gg:256 * gg + 256], tb[:, 128 * gg:128 * gg + 128], VB[gg],
                             start=True, stop=True)
            return r
        tk = P.T(fn, c, bf)
        R.T.give(ti, tk)
        dst = MIX[:, t, 256:768].rearrange("p (h d) -> p h d", h=8)
        e = P.tt(dst, bank[:, :].rearrange("p (h d) -> p h d", h=8), bc(gs[:, t, 0:8], 2, 64), MUL, tk, gr)
        P.banks.give(b, e)

    def att(t, kind, i, st):
        h = i
        gg = h // 4
        rows = slice(64 * gg, 64 * gg + 64)
        nk = 128 * (t + 1)
        if i == 0:
            st[kind] = P.banks.take()
        ob = st[kind]
        k = 8 * kind + h
        ei, eb, x = softmax_rows(P, R, [(QT[rows, h % 4, 128 * t:128 * t + 128], KT[rows, kind, 0:nk])], nk,
                                 (P.cmask[:, 384 - 128 * t:512], ()), SUM[:, 16 + 16 * (t % 2) + k:17 + 16 * (t % 2) + k],
                                 SUM[:, 64 + 16 * (t % 2) + k:65 + 16 * (t % 2) + k], qkr)
        yield
        vc = (1408, 1664)[kind] + 64 * gg
        for tk in turn_and_apply(P, R, ev, ei, eb, x, nk, lambda j: PJ[:, j, vc:vc + 64],
                                 ob[1][:, 64 * h:64 * h + 64], ob[2], h == 0, 64):
            if tk is None:
                yield
        st["tk"] = tk

    def fin(t, st):
        yield
        yield
        yield
        for kind in range(2):
            r = SUM[:, 16 + 16 * (t % 2) + 8 * kind:24 + 16 * (t % 2) + 8 * kind]
            P.rec(r, r, st["tk"], P.C.last())
            P.tt(r, r, gs[:, t, 8 + 8 * kind:16 + 8 * kind], MUL)
            ob = st[kind]
            tv = TMP.rearrange("p (h d) -> p h d", h=8)
            e = P.tt(tv, ob[1][:, :].rearrange("p (h d) -> p h d", h=8), bc(r, 2, 64), MUL)
            P.banks.give(ob[0], e)
            P.tt(MIX[:, t, 256:768], MIX[:, t, 256:768], TMP, ADD)

    run_lagged(units())


def fox(P, l, PJ, MIX, W):
    g = P.g[l]
    ev = Evac(P)
    ph = P.now()
    R = Rings(P, W, ph)
    o = W + Rings.SIZE
    QT = P.m(o, 1024).rearrange("p (i n) -> p i n", i=2)
    KT = P.m(o + 1024, 1024).rearrange("p (i n) -> p i n", i=2)
    NC = P.m(P.HTo, 2048).rearrange("p (h n) -> p h n", h=4)
    H0 = P.HTo + 2048
    sc = P.m(o + 2048, 512)
    for t in range(4):
        r = ph
        b, bank, bf = P.banks.take()
        tk = P.tr([(bank[:, 128 * i:128 * i + 128], PJ[:, t, 1816 + 128 * i:1816 + 128 * i + 128]) for i in range(4)],
                  r, bf)
        v = bank[:, :].rearrange("p (i n) -> p i n", i=4)
        P.act(QT[:, :, 128 * t:128 * t + 128], v[:, 0:2, :], ACT.Copy, tk, ph, scale=0.125)
        e = P.act(KT[:, :, 128 * t:128 * t + 128], v[:, 2:4, :], ACT.Copy)
        P.banks.give(b, e)
    z = P.m(H0, 16)
    lf = P.m(H0 + 16, 16)
    zv = z.rearrange("p (t h) -> p t h", t=4)
    P.tt(zv, PJ[:, :, 2584:2588], bc(g["fb"], 1, 4), ADD, ph)
    P.ts(lf, z, -1.0, None, MUL)
    x = P.tt(lf, lf, z, MIN)
    x = P.act(lf, lf, ACT.Exp, x)
    x = P.ts(lf, lf, 1.0, None, ADD, None, x)
    x = P.act(lf, lf, ACT.Ln, x)
    P.ts(z, z, 0.0, None, MIN)
    x = P.tt(lf, z, lf, SUB, x)
    lv = lf.rearrange("p (t h) -> p t h", t=4)
    b, bank, bf = P.banks.take()
    cq = P.m(H0 + 32, 16)

    def fn(e):
        for t in range(4):
            for j in range(t + 1):
                r = e.matmul(bank[:, 4 * t:4 * t + 4], P.utri if j == t else P.ones, lv[:, j, :],
                             start=(j == 0), stop=(j == t))
        return r
    tk = P.T(fn, x, bf)
    cr = P.copy(cq, bank[:, 0:16], tk)
    P.banks.give(b, cr)
    lb = P.m(H0 + 64, 512)
    for h in range(4):
        r = P.copy(lb.rearrange("p (t n) -> p t n", t=4), bc(lv[:, :, h], 2, 128), P.T.last())
        b, bank, bf = P.banks.take()

        def fn(e, bank=bank):
            for t in range(4):
                for j in range(t + 1):
                    r = e.matmul(bank[:, 128 * t:128 * t + 128], lb[:, 128 * j:128 * j + 128],
                                 P.utri if j == t else P.ones, start=(j == 0), stop=(j == t))
            return r
        tk = P.T(fn, r, bf)
        e = P.act(NC[:, h, :], bank[:, :], ACT.Copy, tk, ph, scale=-1.0)
        P.banks.give(b, e)
    ready = P.now()
    mark(P, 'fox prep')
    SUM = P.m(H0 + 576, 64)

    def units():
        for t in range(4):
            st = {}
            for h in range(4):
                yield att(t, h, st)
            yield fin(t, st)

    def att(t, h, st):
        rows = slice(64 * (h % 2), 64 * (h % 2) + 64)
        nk = 128 * (t + 1)
        if h == 0:
            st["o"] = P.banks.take()
        ob = st["o"]
        mi, mb, mf = R.M.take()
        m = P.stt(mb[:, 0:nk], NC[:, h, 0:nk], cq[:, 4 * t + h:4 * t + h + 1], P.cmask[:, 384 - 128 * t:512],
                  ADD, ADD, mf, ready)
        k = 4 * (t % 2) + h
        ei, eb, x = softmax_rows(P, R, [(QT[rows, h // 2, 128 * t:128 * t + 128], KT[rows, h // 2, 0:nk])], nk,
                                 (mb[:, 0:nk], m), SUM[:, k:k + 1], SUM[:, 16 + k:17 + k], ready)
        R.M.give(mi, x)
        yield
        vc = 2328 + 64 * h
        for tk in turn_and_apply(P, R, ev, ei, eb, x, nk, lambda j: PJ[:, j, vc:vc + 64],
                                 ob[1][:, 64 * h:64 * h + 64], ob[2], h == 0, 64):
            if tk is None:
                yield
        st["tk"] = tk

    def fin(t, st):
        yield
        yield
        yield
        r = SUM[:, 4 * (t % 2):4 * (t % 2) + 4]
        P.rec(r, r, st["tk"], P.C.last())
        ob = st["o"]
        e = P.tt(MIX[:, t, 768:1024].rearrange("p (h d) -> p h d", h=4),
                 ob[1][:, 0:256].rearrange("p (h d) -> p h d", h=4), bc(r, 2, 64), MUL)
        P.banks.give(ob[0], e)

    run_lagged(units())



def ln_load(P, l, names, o, deps):
    gb, bb = P.m(o, 1024), P.m(o + 1024, 1024)
    return gb, bb, P.load([(gb, P.A[names[0]][l].partition_broadcast(128)),
                           (bb, P.A[names[1]][l].partition_broadcast(128))], deps)


def layer_norm(P, gains, ready=()):
    gb, bb, ld = gains
    st = P.small[:, 64:112].rearrange("p (t k n) -> p t k n", t=4, k=2)
    mv = P.small[:, 112:120].rearrange("p (t n) -> p t n", t=4)
    for t in range(4):
        for k in range(2):
            P.V(lambda e: e.bn_stats(st[:, t, k, :], P.X[:, t, 512 * k:512 * k + 512]), ready, chain=(t == 0))
    for t in range(4):
        P.V(lambda e: e.bn_aggr(mv[:, t, :], st[:, t].rearrange("p k n -> p (k n)")), chain=(t == 0))
    var = mv[:, :, 1]
    P.rsqrt(var, 1.0, 1e-5)
    nb = P.small[:, 120:124]
    P.tt(nb, mv[:, :, 0], var, MUL)
    r = P.ts(nb, nb, -1.0, None, MUL)
    a = [P.act(P.X[:, t, :], P.X[:, t, :], ACT.Identity, r, bias=nb[:, t:t + 1], scale=mv[:, t, 1:2], chain=False)
         for t in range(4)]
    g = [P.tt(P.X[:, t, :], P.X[:, t, :], gb, MUL, a[t], ld, chain=False) for t in range(4)]
    for t in range(4):
        P.tt(P.X[:, t, :], P.X[:, t, :], bb, ADD, g[t], chain=False)
    return P.V.last()


def second_layer(P, l):
    o = P.L0
    alpha = 4 ** 0.25
    add = lambda t, n, ps, tk: P.stt(P.X[:, t, 512 * n:512 * n + 512], P.X[:, t, 512 * n:512 * n + 512], alpha,
                                     ps, MUL, ADD, tk, chain=False)
    if l == 0:
        MIX, lo = even_mixer(P), o
    else:
        MIX, lo = odd_mixer(P), o + 12288
    gains = ln_load(P, l, ("ln1_g_2", "ln1_b_2"), o + 22300, P.now())
    mix_out(P, MIX, add, lo)
    layer_norm(P, gains)
    gains = experts(P, l)
    layer_norm(P, gains)


def even_mixer(P):
    A = P.A
    ev = Evac(P)
    o = P.L0
    ph = P.now()
    hd = transpose_x(P, lambda t: P.X[:, t, :], 0, deps=ph, lo=o + 7808, ready=ph)
    QKV = P.m(o, 6144).rearrange("p (t n) -> p t n", t=4)
    LC = P.m(o + 6144, 1664).rearrange("p (t n) -> p t n", t=4)
    MIX = P.m(o + 7808, 4096).rearrange("p (t n) -> p t n", t=4)
    ro = o + 11904
    R = Rings(P, ro, ph)
    w0 = ro + Rings.SIZE
    hik, lok = block(halves(P, P.HTo)), block(halves(P, o + 7808))

    def to(c):
        if c < 3:
            return lambda t, ps, tk: ev(QKV[:, t, 512 * c:512 * c + 512], ps, tk, ph)
        return lambda t, ps, tk: ev(LC[:, t, :], ps, tk, ph)
    run_dense(P, [Job("tok", 512 if c < 3 else 416, hik, lok, to(c), acc=[])
                  for c in range(4)], hd)
    pr = P.now()
    mark(P, 'proj')
    QT = P.m(w0, 2048).rearrange("p (i n) -> p i n", i=4)
    KT = P.m(w0 + 2048, 2048).rearrange("p (i n) -> p i n", i=4)
    HB = P.HTo
    sc = P.m(HB, 512)
    lam4 = P.m(HB + 512, 256).rearrange("p (w n) -> p w n", w=4)
    lam = P.m(HB + 768, 8)
    sg = P.m(HB + 776, 128)
    r2 = P.m(HB + 904, 128).rearrange("p (t n) -> p t n", t=4)
    qg = P.m(HB + 1032, 256)
    kg = P.m(HB + 1288, 128)
    pl = P.load([(lam4[:, i, :], A[f"even_lam_{n}_2"][0].partition_broadcast(128))
                 for i, n in enumerate(("q1", "k1", "q2", "k2"))]
                + [(sg, A["even_subln_g_2"][0].partition_broadcast(128)),
                   (P.m(HB + 904, 128), A["c_rope2"]),
                   (qg, A["even_q_norm_g_2"][0].partition_broadcast(128)),
                   (kg, A["even_kv_norm_g_2"][0].partition_broadcast(128))], pr)
    pv = lam4.rearrange("p (a b) n -> p a b n", a=2)
    P.tt(pv[:, :, 0, :], pv[:, :, 0, :], pv[:, :, 1, :], MUL, pl, pr)
    x = P.red(lam[:, 0:2], pv[:, :, 0, :], ADD)
    x = P.act(lam[:, 0:2], lam[:, 0:2], ACT.Exp, x)
    P.tt(lam[:, 2:3], lam[:, 1:2], lam[:, 0:1], SUB, x)
    lam_init = 0.8 - 0.6 * math.exp(-0.3 * 0)
    P.ts(lam[:, 2:3], lam[:, 2:3], -lam_init, None, ADD)
    nlam = lam[:, 2:3]
    P.ts(sg, sg, 1.0 - lam_init, None, MUL)
    for t in range(4):
        r = rope(P, QKV[:, t, 0:1024].rearrange("p (n d) -> p n d", n=16), 16, 8, P.rope[:, t, :], sc)
        for q, dst, scale in ((0, QT, 0.125), (1, KT, 1.0)):
            b, bank, bf = P.banks.take()
            tk = P.tr([(bank[:, 128 * i:128 * i + 128], QKV[:, t, 512 * q + 128 * i:512 * q + 128 * i + 128])
                       for i in range(4)], r, bf)
            e = P.act(dst[:, :, 128 * t:128 * t + 128], bank[:, :].rearrange("p (i n) -> p i n", i=4), ACT.Copy,
                      tk, ph, scale=scale)
            P.banks.give(b, e)
    ready = P.now()
    SUM = P.m(HB + 1416, 64)
    obs = {}

    def units():
        for t in range(4):
            for h in range(4):
                yield att(t, h)
            yield fin(t)

    def att(t, h):
        if h == 0:
            obs[t] = P.banks.take()
        ob = obs[t]
        k = 8 * ((4 * t + h) % 4)
        es = []
        for m in range(2):
            rows = slice(64 * m, 64 * m + 64)
            es.append(softmax_rows(P, R, [(QT[rows, h, 128 * t:128 * t + 128], KT[rows, h, :])], 512, None,
                                   SUM[:, k + m:k + m + 1], SUM[:, k + 2 + m:k + 3 + m], ready))
        (e0, b0, x0), (e1, b1, x1) = es
        P.rec(SUM[:, k:k + 2], SUM[:, k:k + 2], x0, x1)
        c = P.tt(SUM[:, k + 1:k + 2], SUM[:, k + 1:k + 2], nlam, MUL)
        x = P.act(b1, b1, ACT.Copy, c, scale=SUM[:, k + 1:k + 2])
        x = P.stt(b0, b0, SUM[:, k:k + 1], b1, MUL, ADD, x)
        R.E.give(e1, x)
        yield
        for tk in turn_and_apply(P, R, ev, e0, b0, x, 512, lambda j: QKV[:, j, 1024 + 128 * h:1024 + 128 * h + 128],
                                 ob[1][:, 128 * h:128 * h + 128], ob[2], h == 0, 128):
            if tk is None:
                yield
        obs[t] = ob[0:3] + (tk,)

    def fin(t):
        yield
        yield
        yield
        ob = obs[t]
        dst = MIX[:, t, 0:512]
        e = P.copy(dst, ob[1][:, :], ob[3], ph)
        P.banks.give(ob[0], e)
        head_norm(P, dst.rearrange("p (h d) -> p h d", h=4), 4, 128, sg, sc)

    run_lagged(units())

    mark(P, 'diff')
    ph = P.now()
    slot, buf, wt = P.wtake()
    wuq = buf[:, 0:1536].rearrange("p (k n) -> p k n", k=2)
    wukv = buf[:, 1536:2560]
    UQ = P.m(o, 3072).rearrange("p (t n) -> p t n", t=4)
    QT2o = o + 3072
    QT2 = P.m(QT2o, 2048, parts=96).rearrange("p (i n) -> p i n", i=4)
    UKV = P.m(w0, 4096).rearrange("p (t n) -> p t n", t=4)
    KT2 = P.m(P.HTo + 2048, 2048, parts=96).rearrange("p (i n) -> p i n", i=4)
    kf = P.m(o + 5120, 384)
    for t in range(4):
        for c, n, gn in ((0, 256, qg), (256, 128, kg)):
            r = head_norm(P, LC[:, t, c:c + n].unsqueeze(1), 1, n, gn, sc, ph)
        rr = rope(P, LC[:, t, 384:416].unsqueeze(1), 1, 16, r2[:, t, :], sc)
        b, bank, bf = P.banks.take()
        tk = P.tr([(bank[:, 128 * i:128 * i + 128], LC[:, t, 128 * i:128 * i + 128]) for i in range(3)], r, bf)
        LT = P.m(ro, 384)
        c = P.copy(LT, bank[:, 0:384], tk, P.T.last())
        P.banks.give(b, c)
        for c0, n in ((0, 512), (512, 256)):
            b, bank, bf = P.banks.take()
            tk = P.mm(bank[:, 0:n], [(LT[:, 128 * k:128 * k + 128], wuq[:, k, c0:c0 + n]) for k in range(2)],
                      c, bf, wt)
            P.banks.give(b, P.act(UQ[:, t, c0:c0 + n], bank[:, 0:n], ACT.Copy, tk, ph))
        for c0 in (0, 512):
            b, bank, bf = P.banks.take()
            tk = P.mm(bank[:, :], [(LT[:, 256:384], wukv[:, c0:c0 + 512])], c, bf)
            P.banks.give(b, P.act(UKV[:, t, c0:c0 + 512], bank[:, :], ACT.Copy, tk, ph))
        rope(P, UQ[:, t, :].rearrange("p (h d) -> p h d", h=8)[:, :, 64:96], 8, 16, r2[:, t, :], sc, P.C.last())
    P.wgive(slot, tk)
    scale = (96.0) ** -0.5
    mark(P, 'mla proj')
    for hg in range(2):
        mark(P, 'hg')
        R = Rings(P, ro, P.now())
        for t in range(4):
            ph = P.now()
            kv = kf.rearrange("p (h d) -> p h d", h=4)
            uk = UKV[:, t, 512 * hg:512 * hg + 512].rearrange("p (h d) -> p h d", h=4)
            P.copy(kv[:, :, 0:64], uk[:, :, 0:64], ph)
            r = P.copy(kv[:, :, 64:96], bc(LC[:, t, 384:416], 1, 4))
            for q in range(2):
                b, bank, bf = P.banks.take()
                src = (lambda i: UQ[:, t, 384 * hg + 96 * i:384 * hg + 96 * i + 96]) if q == 0 else \
                    (lambda i: kf[:, 96 * i:96 * i + 96])
                tk = P.tr([(bank[0:96, 128 * i:128 * i + 128], src(i)) for i in range(4)], r, bf)
                e = P.act((QT2, KT2)[q][:, :, 128 * t:128 * t + 128],
                          bank[0:96, :].rearrange("p (i n) -> p i n", i=4), ACT.Copy, tk, ph,
                          scale=(scale, 1.0)[q])
                P.banks.give(b, e)
        ready = P.now()
        mark(P, 'mla prep')
        ob2 = {}

        def att2(t, i):
            if i == 0:
                ob2[t] = P.banks.take()
            ob = ob2[t]
            k = 4 * (t % 2) + i
            ei, eb, x = softmax_rows(P, R, [(QT2[:, i, 128 * t:128 * t + 128], KT2[:, i, :])], 512, None,
                                     SUM[:, k:k + 1], SUM[:, 16 + k:17 + k], ready)
            yield
            c0 = 128 * (4 * hg + i) + 64
            for tk in turn_and_apply(P, R, ev, ei, eb, x, 512, lambda j: UKV[:, j, c0:c0 + 64],
                                     ob[1][:, 64 * i:64 * i + 64], ob[2], i == 0, 64):
                if tk is None:
                    yield
            ob2[t] = ob[0:3] + (tk,)

        def fin2(t):
            yield
            yield
            yield
            ob = ob2[t]
            r = SUM[:, 4 * (t % 2):4 * (t % 2) + 4]
            P.rec(r, r, ob[3], P.C.last())
            c0 = 512 + 256 * hg
            e = P.tt(MIX[:, t, c0:c0 + 256].rearrange("p (h d) -> p h d", h=4),
                     ob[1][:, 0:256].rearrange("p (h d) -> p h d", h=4), bc(r, 2, 64), MUL)
            P.banks.give(ob[0], e)

        def units2():
            for t in range(4):
                for i in range(4):
                    yield att2(t, i)
                yield fin2(t)
        run_lagged(units2())
    return MIX


def odd_mixer(P):
    A = P.A
    ev = Evac(P)
    o = P.L0
    ph = P.now()
    hd = transpose_x(P, lambda t: P.X[:, t, :], 0, deps=ph, lo=o + 12288, ready=ph)
    QKV = P.m(o, 12288).rearrange("p (t n) -> p t n", t=4)
    ro = o + 12288
    hik, lok = block(halves(P, P.HTo)), block(halves(P, o + 12288))
    run_dense(P, [Job("tok", 512, hik, lok,
                      (lambda t, ps, tk, c=c: ev(QKV[:, t, 512 * c:512 * c + 512], ps, tk, ph)), acc=[])
                  for c in range(6)], hd)
    ready = P.now()
    mark(P, 'proj')
    R = Rings(P, ro, ready)
    w0 = ro + Rings.SIZE
    TB = Ring([P.m(w0 + 896 * i, 896) for i in range(2)], ready)
    QK = Ring([P.m(P.HTo + 1024 * i, 1024) for i in range(3)], ready)
    SUM = P.m(P.HTo + 3072, 128)
    rel = A["rel"]
    rsem = [P.sem("rel") for _ in range(2)]
    qkt, tbt = {}, {}

    def load_bias(h):
        i, tb, f = TB.take()
        P.Y.dma(rsem[i], lambda e: e.dma_start(tb[0:64, :], rel[h, :, 1:15, :].rearrange("c j n -> c (j n)")), f, ready)
        tk = P.Y.dma(rsem[i], lambda e: e.dma_start(tb[64:128, :], rel[h, :, 0:14, :].rearrange("c j n -> c (j n)")), f)
        tbt[h] = (i, tb, tk)

    def prep(hp):
        qi, qb, qf = QK.take()
        toks = []
        for q in range(2):
            b, bank, bf = P.banks.take()
            tk = P.tr([(bank[:, 128 * t:128 * t + 128],
                        QKV[:, t, 1024 * q + 128 * hp:1024 * q + 128 * hp + 128]) for t in range(4)], ready, bf)
            e = P.act(qb[:, 512 * q:512 * q + 512], bank[:, :], ACT.Copy, tk, qf, scale=(0.125, 1.0)[q], chain=False)
            P.banks.give(b, e)
            toks.append(e)
        qkt[hp] = (qi, qb, toks)
        yield

    load_bias(0)

    def units():
        yield prep(0)
        for hp in range(8):
            if hp < 7:
                yield prep(hp + 1)
            for hh in range(2):
                if 2 * hp + hh + 1 < 16:
                    load_bias(2 * hp + hh + 1)
                st = {}
                for t in range(4):
                    yield att(hp, hh, t, st)
                yield fin(hp, hh, st)

    def att(hp, hh, t, st):
        h = 2 * hp + hh
        if t == 0:
            st["o"] = P.banks.take()
        ob = st["o"]
        qi, qb, qtok = qkt[hp]
        ti, tb, ttok = tbt[h]
        rows = slice(64 * hh, 64 * hh + 64)
        k = 4 * (h % 2) + t
        s0 = 64 * (6 - 2 * t)
        ei, eb, x = softmax_rows(P, R, [(qb[rows, 128 * t:128 * t + 128], qb[rows, 512:1024])], 512,
                                 (tb[:, s0:s0 + 512], ttok), SUM[:, k:k + 1], SUM[:, 16 + k:17 + k], qtok)
        if t == 3:
            TB.give(ti, x)
            if hh == 1:
                QK.give(qi, x)
        yield
        for tk in turn_and_apply(P, R, ev, ei, eb, x, 512, lambda j: QKV[:, j, 2048 + 64 * h:2048 + 64 * h + 64],
                                 ob[1][:, 64 * t:64 * t + 64], ob[2], t == 0, 64):
            if tk is None:
                yield
        st["tk"] = tk

    def fin(hp, hh, st):
        h = 2 * hp + hh
        yield
        yield
        yield
        r = SUM[:, 4 * (h % 2):4 * (h % 2) + 4]
        P.rec(r, r, st["tk"], P.C.last())
        ob = st["o"]
        e = P.tt(QKV[:, :, 64 * h:64 * h + 64], ob[1][:, 0:256].rearrange("p (t d) -> p t d", t=4),
                 bc(r, 2, 64), MUL)
        P.banks.give(ob[0], e)

    run_lagged(units())
    return QKV


def experts(P, l):
    A = P.A
    o = P.L0
    ph = P.now()
    hd = transpose_x(P, lambda t: P.X[:, t, :], 0, deps=ph, ready=ph)
    xs = P.sem("xd")
    for t in range(4):
        xd = P.Y.dma(xs, (lambda t: lambda e: e.dma_start(P.xd[128 * t:128 * t + 128, :], P.X[:, t, :]))(t), ph)
    ini = P.load([(P.tab[l][:, :], A["c_big"])])
    wr = P.m(o, 288).rearrange("p (k n) -> p k n", k=8)
    rb = P.m(o + 288, 36)
    ei = P.m(o + 324, 32)
    wl = P.load([(wr[:, :, 0:4], A["w_router_group_2"][l].rearrange("(k p) n -> p k n", p=128)),
                 (wr[:, :, 4:36], A["w_router_expert_2"][l].rearrange("(k p) n -> p k n", p=128)),
                 (rb[:, 0:4], A["b_router_group_2"][l].partition_broadcast(128)),
                 (rb[:, 4:36], A["b_router_expert_2"][l].partition_broadcast(128)),
                 (ei, A["c_eio"])], ph)
    b, bank, bf = P.banks.take()

    def fn(e):
        for t in range(4):
            for k in range(8):
                r = e.matmul(bank[:, 36 * t:36 * t + 36], P.HT[:, k, 128 * t:128 * t + 128], wr[:, k, :],
                             start=(k == 0), stop=(k == 7))
        return r
    tk = P.T(fn, hd, wl, bf)
    lg = P.m(o + 400, 144).rearrange("p (t n) -> p t n", t=4)
    e = P.tt(lg, bank[:, 0:144].rearrange("p (t n) -> p t n", t=4), bc(rb, 1, 4), ADD, tk, ph)
    P.banks.give(b, e)
    oh = P.m(o + 600, 128 * 2).rearrange("p (k t n) -> p k t n", k=2, t=4)
    gt = P.m(P.HTo + 3900, 8).rearrange("p (t k) -> p t k", t=4)
    idf = P.m(o + 924, 8)
    q0 = o + 1304 + 8192

    def four(at, n):
        return P.m(q0 + at, 4 * n).rearrange("p (t n) -> p t n", t=4)
    gp, m8, ml, goh, ge = four(0, 8), four(32, 8), four(64, 32), four(192, 4), four(208, 4)
    i8 = P.memu[:, 104:136].rearrange("p (t n) -> p t n", t=4)
    i8f = four(224, 8)
    a4 = four(256, 1)[:, :, 0]
    b4 = four(260, 1)[:, :, 0]
    c4 = four(264, 1)[:, :, 0]
    P.V(lambda e: e.memset(gp, -3e38), hd, ph)
    P.copy(gp[:, :, 0:4], lg[:, :, 0:4])

    def top8(src):
        for t in range(4):
            P.V(lambda e: e.max(m8[:, t, :], src[:, t, :]), chain=(t == 0))
        for t in range(4):
            P.V(lambda e: e.max_index(i8[:, t, :], m8[:, t, :], src[:, t, :]), chain=(t == 0))
        P.copy(i8f, i8)
    top8(gp)
    P.tt(goh, bc(ei[:, 0:4], 1, 4), bc(i8f[:, :, 0], 2, 4), ALU.is_equal)
    x = P.tt(ge, lg[:, :, 0:4], bc(m8[:, :, 0], 2, 4), SUB)
    x = P.act(ge, ge, ACT.Exp, x)
    mv = ml.rearrange("p t (g n) -> p t g n", g=4)
    for t in range(4):
        P.tt(mv[:, t], lg[:, t, 4:36].rearrange("p (g n) -> p g n", g=4), bc(goh[:, t], 2, 8), MUL, chain=(t == 0))
    P.ts(goh, goh, 1.0, 1e30, SUB, MUL)
    for t in range(4):
        P.tt(mv[:, t], mv[:, t], bc(goh[:, t], 2, 8), ADD, chain=(t == 0))
    P.red(a4, ge, ADD, x)
    top8(ml)
    for k in range(2):
        P.tt(oh[:, k], bc(ei, 1, 4), bc(i8f[:, :, k], 2, 32), ALU.is_equal, chain=(k == 0))
    y = P.tt(b4, m8[:, :, 1], m8[:, :, 0], SUB)
    y = P.act(b4, b4, ACT.Exp, y)
    P.ts(c4, b4, 1.0, None, ADD, None, y)
    P.tt(c4, c4, a4, MUL)
    P.rec(gt[:, :, 0], c4)
    P.tt(gt[:, :, 1], gt[:, :, 0], b4, MUL)
    ohs = P.m(o + 1000, 128).rearrange("p (t n) -> p t n", t=4)
    r = P.tt(ohs, oh[:, 0], oh[:, 1], ADD)
    b, bank, bf = P.banks.take()

    def fn(e):
        for t in range(4):
            for j in range(t + 1):
                r = e.matmul(bank[:, 32 * t:32 * t + 32], P.ustr if j == t else P.ones, ohs[:, j, :],
                             start=(j == 0), stop=(j == t))
        for j in range(4):
            r = e.matmul(bank[:, 128:160], P.ones, ohs[:, j, :], start=(j == 0), stop=(j == 3))
        return r
    tk = P.T(fn, r, bf)
    rk = P.m(o + 1130, 160)
    e = P.copy(rk, bank[:, 0:160], tk)
    P.banks.give(b, e)
    P.ts(rk[:, 0:128], rk[:, 0:128], 32.0, None, MUL)
    P.tt(rk[:, 0:128].rearrange("p (t n) -> p t n", t=4), rk[:, 0:128].rearrange("p (t n) -> p t n", t=4),
         bc(ei, 1, 4), ADD)
    du = P.memu[:, 136:144]
    tu = P.memu[:, 144:152]
    for k in range(2):
        P.tt(oh[:, k], oh[:, k], rk[:, 0:128].rearrange("p (t n) -> p t n", t=4), MUL)
        P.red(idf.rearrange("p (t k) -> p t k", t=4)[:, :, k], oh[:, k], ADD)
    P.copy(tu, P.tokid)
    d = P.copy(du, idf)
    cnt = P.memu[0:1, 152:153]
    mc = P.m(o + 1290, 1)
    P.red(mc, rk[:, 128:160], MAX)
    P.copy(P.memu[:, 64:96], rk[:, 128:160])
    P.cnt_ready = P.copy(P.memu[:, 152:153], mc)
    ss = P.sem("scat")
    for t in range(4):
        for k in range(2):
            i = 2 * t + k
            sct = P.G.dma(ss, (lambda i: lambda e: e.indirect_dma_start(
                P.tab[l].rearrange("r (e u) -> (r e) u", u=1), bass.IndirectOffsetOnAxis(du[:, i:i + 1], 0),
                tu[:, i:i + 1], None))(i), d, ini)
    IDX = P.memu[:, 0:64].rearrange("p (a e) -> p a e", a=2)
    il = P.load([(IDX[0:CAP, 0, :], P.tab[l][0:CAP, :])], sct, P.now())
    hx = P.V(lambda e: e.tensor_single_scalar(IDX[0:CAP, 1, :], IDX[0:CAP, 0, :], 1, ALU.logical_shift_right), il)

    mark(P, 'router')
    o1 = o + 1304
    assert CAP == 128 or CAP == 64
    XG = Ring([P.m(o1 + 1024 * i, 1024) for i in range(2)])
    XT = Ring([P.m(o1 + 2048 + 8 * CAP * i, 8 * CAP) for i in range(2)])
    HD = Ring([(P.r(o1 + 4096 + 1024 * i, 512), P.r(o1 + 4608 + 1024 * i, 512)) for i in range(2)])
    SG = Ring([P.m(o1 + 8192 + 512 * i, 512) for i in range(2)])
    WP = Ring([(P.r(o1 + 9216 + 2048 * i, 1024), P.r(o1 + 10240 + 2048 * i, 1024)) for i in range(2)])
    YY = Ring([P.m(o1 + 6144 + 1024 * i, 1024) for i in range(2)])
    WP.free = [ph] * 2
    HD.free = [ph] * 2
    xtra = [P.spare]
    P.wissue(P.spare, (ph,))
    e0 = o1 + 13312
    while e0 + 4096 <= P.total:
        xtra.append(e0)
        P.wissue(e0, (ph,))
        e0 += 4096
    gsem = [P.sem("gx") for _ in range(2)]
    ysem = [P.sem("ys") for _ in range(2)]
    z = [P.V((lambda b_: lambda e: e.memset(b_, 0.0))(b_), ph) for b_ in XG.bufs]
    ev = Evac(P)
    gath = {}
    ytok = []

    def gather(e_):
        gi, gb, gf = XG.take()
        tk = P.G.dma(gsem[gi], lambda e: e.indirect_dma_start(
            gb[0:CAP, :], None, P.xd[:, :], bass.IndirectOffsetOnAxis(IDX[0:CAP, 1, e_:e_ + 1], 0),
            bounds_check=S - 1, oob_is_err=False), gf, hx, xd, z)
        gath[e_] = (gi, gb, tk)

    def turn(e_):
        gi, gb, gtk = gath[e_]
        xi, xb, xf = XT.take()
        xv = xb.rearrange("p (k n) -> p k n", k=8)
        cs = []
        for half in range(2):
            b, bank, bf = P.banks.take()
            v = bank[:, 0:4 * CAP].rearrange("p (k n) -> p k n", k=4)
            tk = P.tr([(v[:, k, :], gb[0:CAP, 128 * (4 * half + k):128 * (4 * half + k) + 128]) for k in range(4)],
                      gtk, bf)
            c = ev(xv[:, 4 * half:4 * half + 4, :], v, tk, xf)
            P.banks.give(b, c)
            cs.append(c)
        XG.give(gi, tk)
        return xi, xv, cs

    gather(0)
    gather(1)
    nxt = turn(0)
    ngive = P.wnext + 0

    e_parts = {}

    def split_down(e_):
        slot, buf, wt = P.wtake()

        def make(k):
            pi, (wh, wl), pf = WP.take()
            w = buf[:, 1024 * k:1024 * k + 1024]
            h = P.act(wh, w, ACT.Copy, wt, pf, chain=False)
            e = P.tt(wl, w, wh.bitcast(F32), SUB, wt, pf, h, chain=False)
            if k == 3:
                give(slot, (h, e))
            return pi, wh, wl, (h, e)
        ready = [make(0), make(1)]

        def parts(k):
            if len(ready) > k:
                return ready[k]
            ready.append(make(k))
            return ready[k]
        e_parts[e_] = (slot, parts)

    def up(e_, cur):
        xi, xv, cs = cur
        outs = []
        for _ in range(2):
            slot, buf, wt = P.wtake()
            w = buf.rearrange("p (k n) -> p k n", k=8)
            b, bank, bf = P.banks.take()

            def fn(e, bank=bank, w=w):
                for c in range(4):
                    for k in range(8):
                        r = e.matmul(bank[:, CAP * c:CAP * c + CAP], w[:, k, 128 * c:128 * c + 128], xv[:, k, :],
                                     start=(k == 0), stop=(k == 7))
                return r
            tk = P.T(fn, wt, bf, cs)
            give(slot, tk)
            outs.append((b, bank, tk))
        XT.give(xi, tk)
        (b0, g_, t0), (b1, u_, t1) = outs
        split_down(e_)
        si, sb, sf = SG.take()
        n = 4 * CAP
        x = P.act(sb[:, 0:n], g_[:, 0:n], ACT.Exp, t0, sf, scale=-1.0, chain=False)
        P.ts(sb[:, 0:n], sb[:, 0:n], 1.0, None, ADD, None, x)
        P.rec(sb[:, 0:n], sb[:, 0:n])
        x = P.tt(sb[:, 0:n], sb[:, 0:n], g_[:, 0:n], MUL)
        P.banks.give(b0, x)
        hi, hb, hf = HD.take()
        x = P.tt(sb[:, 0:n], sb[:, 0:n], u_[:, 0:n], MUL, t1)
        P.banks.give(b1, x)
        h = P.act(hb[0][:, 0:n], sb[:, 0:n], ACT.Copy, x, hf, chain=False)
        x = P.tt(hb[1][:, 0:n], sb[:, 0:n], hb[0][:, 0:n].bitcast(F32), SUB, h, hf)
        SG.give(si, x)
        return hi, hb, (h, x)

    def down(e_, hi, hb, x):
        yi, yb, yf = YY.take()
        slot, parts = e_parts.pop(e_)
        es = []
        acc = [P.banks.take() for _ in range(2)]
        for k in range(4):
            pi, wh, wl, toks = parts(k)

            def fn(e):
                c = slice(CAP * k, CAP * k + CAP)
                for n in range(2):
                    m = slice(512 * n, 512 * n + 512)
                    for i, (a, b_) in enumerate(((hb[0], wh), (hb[0], wl), (hb[1], wh))):
                        r = e.matmul(acc[n][1][0:CAP, :], a[:, c], b_[:, m], start=(k == 0 and i == 0),
                                     stop=(k == 3 and i == 2))
                return r
            tk = P.T(fn, toks, [a[2] for a in acc], x)
            WP.give(pi, tk)
        for n in range(2):
            c = ev(yb[0:CAP, 512 * n:512 * n + 512], acc[n][1][0:CAP, :], tk, yf)
            P.banks.give(acc[n][0], c)
            es.append(c)
        HD.give(hi, tk)
        y = P.G.dma(ysem[yi], lambda e: e.indirect_dma_start(
            P.yd[:, :], bass.IndirectOffsetOnAxis(IDX[0:CAP, 0, e_:e_ + 1], 0), yb[0:CAP, :], None,
            bounds_check=2 * S - 1, oob_is_err=False), es)
        YY.give(yi, y)
        ytok.append(y)

    def give(slot, tk):
        P.wgive(slot, tk, keep=slot not in xtra or P.wnext < P.wuse_end)

    P.wuse_end = P.wuse + 3 * NE
    for e_ in range(NE):
        cur = nxt
        hdn = up(e_, cur)
        if e_ + 1 < NE:
            nxt = turn(e_ + 1)
        if e_ + 2 < NE:
            gather(e_ + 2)
        down(e_, *hdn)
    mark(P, 'experts')
    for q in (P.T, P.V, P.C, P.G, P.Y):
        q.wait(P.now(), ytok[-2:])
    overflow(P, l, IDX, xtra, XG.bufs[0], P.m(o1 + 2048, 1024), P.m(o1 + 13312 - 1024, 512),
             SG.bufs[0], YY.bufs[0])
    ph = P.now()
    P.pieces.free = [ph] * 4
    YB = P.m(o, 8192).rearrange("p (t k n) -> p t k n", t=4, k=2)
    P.idle_extra = None
    yl = P.load([(YB[:, t], P.yd[256 * t:256 * t + 256, :].rearrange("(p k) n -> p k n", k=2)) for t in range(4)],
                ytok, ph)
    gains = ln_load(P, l, ("ln2_g_2", "ln2_b_2"), o + 8192, ph)
    alpha = 4 ** 0.25
    xa = [P.act(P.X[:, t, :], P.X[:, t, :], ACT.Copy, ph, scale=alpha, chain=False) for t in range(4)]
    for k in range(2):
        for t in range(4):
            P.stt(P.X[:, t, :], YB[:, t, k, :], gt[:, t, k:k + 1], P.X[:, t, :], MUL, ADD, xa, yl, chain=(t == 0))
    return gains


def overflow(P, l, IDX, xtra, XGb, XTb, HDb, SGb, YYb):
    nc, A = P.nc, P.A
    nc.all_engine_barrier()
    for q in (P.T, P.V, P.C, P.G, P.Y):
        q.wait(P.cnt_ready)
    nc.all_engine_barrier()
    most = nc.values_load(P.memu[0:1, 152:153], min_val=0, max_val=512)
    with nc.If(most > CAP):
        with nc.Fori(0, NE) as e_:
            have = nc.values_load(P.memu[0:1, 64:64 + NE][:, bass.ds(e_, 1)], min_val=0, max_val=512)
            with nc.If(have > CAP):
                with nc.Fori(0, NBLK) as r_:
                    with nc.If(have > r_ * 128 + CAP):
                        overflow_block(P, l, e_, r_, xtra, XGb, XTb, HDb, SGb, YYb)
    nc.all_engine_barrier()


def overflow_block(P, l, e_, r_, slots, XGb, XTb, HDb, SGb, YYb):
    nc, A = P.nc, P.A
    T, V, C, G, Y = nc.tensor, nc.vector, nc.scalar, nc.gpsimd, nc.sync
    s = P.osem
    wg, wu, wd = (P.m(x, 4096) for x in slots[0:3])
    oi, ox = P.memu[:, 153:154], P.memu[:, 154:155]
    nc.all_engine_barrier()
    Y.dma_start(oi, P.tab[l][bass.ds(r_ * 128 + CAP, 128), bass.ds(e_, 1)],
                allow_slow_non_contiguous=True).then_inc(s["idx"], 16)
    for buf, name, k in ((wg, "w_gate_2", 8), (wu, "w_up_2", 8), (wd, "w_down_2", 4)):
        Y.dma_start(buf.rearrange("p (k n) -> p k n", k=k),
                    A[name][l][bass.ds(e_, 1)].rearrange("o (k p) n -> p (o k) n", p=128)).then_inc(s["w"], 16)
    V.wait_ge(s["idx"], 16)
    V.tensor_single_scalar(ox, oi, 1, ALU.logical_shift_right).then_inc(s["row"], 1)
    V.memset(XGb, 0.0).then_inc(s["row"], 1)
    G.wait_ge(s["row"], 2)
    G.indirect_dma_start(XGb, None, P.xd[:, :], bass.IndirectOffsetOnAxis(ox, 0),
                         bounds_check=S - 1, oob_is_err=False).then_inc(s["gath"], 16)
    T.wait_ge(s["gath"], 16)
    T.wait_ge(s["w"], 48)
    xv = XTb.rearrange("p (k n) -> p k n", k=8)
    bk = [b for b in P.banks.bufs[0:6]]
    for half in range(2):
        for k in range(4):
            t = T.transpose(bk[half][:, 128 * k:128 * k + 128],
                            XGb[:, 128 * (4 * half + k):128 * (4 * half + k) + 128], P.ident)
        t.then_inc(s["turn"], 1)
    for half in range(2):
        V.wait_ge(s["turn"], half + 1)
        V.tensor_copy(xv[:, 4 * half:4 * half + 4, :],
                      bk[half][:, :].rearrange("p (k n) -> p k n", k=4)).then_inc(s["xt"], 1)
    T.wait_ge(s["xt"], 2)
    for buf, bank in ((wg, bk[2]), (wu, bk[3])):
        w = buf.rearrange("p (k n) -> p k n", k=8)
        for c in range(4):
            for k in range(8):
                t = T.matmul(bank[:, 128 * c:128 * c + 128], w[:, k, 128 * c:128 * c + 128], xv[:, k, :],
                             start=(k == 0), stop=(k == 7))
        t.then_inc(s["up"], 1)
    C.wait_ge(s["up"], 1)
    C.activation(SGb, bk[2][:, :], ACT.Exp, scale=-1.0).then_inc(s["sig"], 1)
    V.wait_ge(s["sig"], 1)
    V.tensor_scalar(SGb, SGb, 1.0, None, ADD).then_inc(s["v"], 1)
    V.wait_ge(s["v"], 1)
    V.reciprocal(SGb, SGb).then_inc(s["v"], 1)
    V.wait_ge(s["v"], 2)
    V.tensor_tensor(SGb, SGb, bk[2][:, :], MUL).then_inc(s["v"], 1)
    V.wait_ge(s["v"], 3)
    V.wait_ge(s["up"], 2)
    V.tensor_tensor(HDb, SGb, bk[3][:, :], MUL).then_inc(s["v"], 1)
    T.wait_ge(s["v"], 4)
    w = wd.rearrange("p (k n) -> p k n", k=4)
    for n in range(2):
        for k in range(4):
            t = T.matmul(bk[4 + n][:, :], HDb[:, 128 * k:128 * k + 128], w[:, k, 512 * n:512 * n + 512],
                         start=(k == 0), stop=(k == 3))
        t.then_inc(s["down"], 1)
    for n in range(2):
        V.wait_ge(s["down"], n + 1)
        V.tensor_copy(YYb[:, 512 * n:512 * n + 512], bk[4 + n][:, :]).then_inc(s["y"], 1)
    G.wait_ge(s["y"], 2)
    G.indirect_dma_start(P.yd[:, :], bass.IndirectOffsetOnAxis(oi, 0), YYb, None,
                         bounds_check=2 * S - 1, oob_is_err=False).then_inc(s["out"], 16)
    G.wait_ge(s["out"], 16)
    nc.all_engine_barrier()
    ids = sorted(h.num for h in s.values())
    assert ids == list(range(ids[0], ids[0] + len(ids)))
    G.dma_reset(range(ids[0], ids[0] + len(ids)))
    G.sem_clear(range(ids[0], ids[0] + len(ids)))
    nc.all_engine_barrier()


def finish(P):
    s = P.sem("out")
    ph = P.now()
    for t in range(4):
        tk = P.Y.dma(s, (lambda t: lambda e: e.dma_start(P.out[0, 128 * t:128 * t + 128, :], P.X[:, t, :]))(t), ph)
    P.Y.wait(tk)


_INS = ['x', 'norm1_g', 'w_in', 'hgrn_lb_logits', 'hgrn_onorm_g', 'nsa_qn_g', 'nsa_kn_g', 'nsa_cmp_pos', 'nsa_cmp_w1',
        'nsa_cmp_w2', 'fox_qn_g', 'fox_kn_g', 'fox_fb', 'w_o', 'norm2_g', 'w_up', 'w_down', 'even_w_in_2',
        'even_lam_q1_2', 'even_lam_k1_2', 'even_lam_q2_2', 'even_lam_k2_2', 'even_subln_g_2', 'even_q_norm_g_2',
        'even_w_uq_2', 'even_kv_norm_g_2', 'even_w_ukv_2', 'even_w_o_2', 'odd_w_qkv_2',
        'odd_w_o_2', 'ln1_g_2', 'ln1_b_2', 'ln2_g_2', 'ln2_b_2', 'w_router_group_2', 'b_router_group_2',
        'w_router_expert_2', 'b_router_expert_2', 'w_gate_2', 'w_up_2', 'w_down_2']


def kernel(**inputs):
    import numpy as np
    import concourse.bacc as bacc
    from concourse.bass_utils import run_bass_kernel_spmd

    nc = bacc.Bacc("TRN2", target_bir_lowering=False, num_devices=1)
    data = {n: np.ascontiguousarray(inputs[n]) for n in _INS}
    data.update(constants())
    for n in ("norm1_g", "norm2_g"):
        data[n] = np.ascontiguousarray(data[n].reshape(2, 8, 128).transpose(0, 2, 1))
    data["hgrn_lb_logits"] = np.ascontiguousarray(data["hgrn_lb_logits"].reshape(2, 2, 128).transpose(2, 1, 0).reshape(128, 4))
    rb = np.asarray(inputs["odd_rel_bias_2"])[0]
    rel = np.full((16, 64, 15, 64), NEG, np.float32)
    for c in range(64):
        c0 = min(max(c - 8, 0), 48)
        rel[:, c, :, c0:c0 + 16] = rb[:, :, c0 - c + 15:c0 - c + 31]
    data["rel"] = rel
    arrays, A = {}, {}
    for n, a in data.items():
        arrays[f"in_{n}"] = a
        A[n] = nc.dram_tensor(f"in_{n}", a.shape, mybir.dt.from_np(a.dtype), kind="ExternalInput").ap()
    out = nc.dram_tensor("out_0", (1, S, D), F32, kind="ExternalOutput").ap()
    scr = {"xd": nc.dram_tensor("xd", (S, D), F32, kind="Internal").ap(),
           "yd": nc.dram_tensor("yd", (2 * S, D), F32, kind="Internal").ap(),
           "tab": [nc.dram_tensor(f"tab{i}", (ROWS, NE), U32, kind="Internal").ap() for i in range(2)]}
    Program.xd, Program.yd, Program.tab = scr["xd"], scr["yd"], scr["tab"]
    build(nc, A, out)
    r = run_bass_kernel_spmd(nc, [arrays], core_ids=[0])
    return r.results[0]["out_0"]
```
